# Optimizing a Trainium2 kernel written in Bass

```python
import jax, jax.numpy as jnp
from jax import lax
import numpy as np
import math

D_MODEL = 1024
BATCH = 1
SEQ = 256
DEPTH = 2

CTX_LEN = 256
GRID_W = 64
Q_BLOCK = 128
ROPE_THETA = 10000.0
EPS = 1e-6

F_GROUPS = 4
F_GROUP_DIM = 128
F_WIDTH = F_GROUPS * F_GROUP_DIM
MLA_HEADS = 8
MLA_Q_RANK = 256
MLA_KV_RANK = 256
MLA_NOPE_DIM = 64
MLA_ROPE_DIM = 32
MLA_QK_DIM = MLA_NOPE_DIM + MLA_ROPE_DIM
MLA_V_DIM = 64
MLA_WIDTH = MLA_HEADS * MLA_V_DIM
GQA_HEADS = 8
GQA_KV_HEADS = 2
GQA_GROUP = GQA_HEADS // GQA_KV_HEADS
GQA_HEAD_DIM = 64
GQA_WIDTH = GQA_HEADS * GQA_HEAD_DIM
GQA_KV_WIDTH = GQA_KV_HEADS * GQA_HEAD_DIM

N_BRANCHES = 3
D_FF = 4 * D_MODEL
N_MOD = 6

KV_COLS = MLA_KV_RANK + MLA_ROPE_DIM + 2 * GQA_KV_WIDTH
KV_SPLITS = (MLA_KV_RANK, MLA_KV_RANK + MLA_ROPE_DIM, MLA_KV_RANK + MLA_ROPE_DIM + GQA_KV_WIDTH)
REST_SPLITS = (F_WIDTH, F_WIDTH + MLA_Q_RANK, F_WIDTH + MLA_Q_RANK + GQA_WIDTH)
IN_COLS = KV_COLS + F_WIDTH + MLA_Q_RANK + GQA_WIDTH + N_BRANCHES * D_MODEL


def layer_norm(x, g=None, b=None):
    xf = x.astype(jnp.float32)
    mu = xf.mean(-1, keepdims=True)
    var = jnp.square(xf - mu).mean(-1, keepdims=True)
    y = (xf - mu) * lax.rsqrt(var + EPS)
    if g is not None:
        y = y * g.astype(jnp.float32) + b.astype(jnp.float32)
    return y.astype(x.dtype)

def rms_norm(x, g):
    xf = x.astype(jnp.float32)
    y = xf * lax.rsqrt(jnp.square(xf).mean(-1, keepdims=True) + EPS)
    return (y * g.astype(jnp.float32)).astype(x.dtype)

def modulate(x, shift, scale):
    return layer_norm(x) * (1 + scale) + shift

def rope_angles(rows, cols, d_rot):
    n = d_rot // 4
    freqs = ROPE_THETA ** (-jnp.arange(n, dtype=jnp.float32) / n)
    ang = jnp.concatenate([rows[:, None] * freqs, cols[:, None] * freqs], axis=-1)
    return jnp.cos(ang), jnp.sin(ang)

def apply_rope(x, cos, sin):
    x1, x2 = jnp.split(x, 2, axis=-1)
    cos = cos[:, None, :].astype(x.dtype)
    sin = sin[:, None, :].astype(x.dtype)
    return jnp.concatenate([x1 * cos - x2 * sin, x1 * sin + x2 * cos], axis=-1)

def attend(q, k, v):
    B, S, Hk, G, dk = q.shape
    nb = S // Q_BLOCK
    qb = jnp.moveaxis(q.reshape(B, nb, Q_BLOCK, Hk, G, dk), 1, 0)

    def block(qi):
        s = jnp.einsum("bqkgd,btkd->bkgqt", qi, k).astype(jnp.float32)
        w = jax.nn.softmax(s, axis=-1).astype(v.dtype)
        return jnp.einsum("bkgqt,btkd->bqkgd", w, v)

    o = lax.map(block, qb)
    return jnp.moveaxis(o, 0, 1).reshape(B, S, Hk * G * v.shape[-1])

def fourier_mix(u):
    B, S, _ = u.shape
    ug = u.reshape(B, S, F_GROUPS, F_GROUP_DIM).astype(jnp.float32)
    f = jnp.fft.fft2(ug, axes=(1, 3), norm="ortho").real
    return f.reshape(B, S, F_WIDTH).astype(u.dtype)

def kv_parts(p, lw, rope):
    B, T, _ = p.shape
    c_kv, k_r, k_g, v_g = jnp.split(p[..., :KV_COLS], KV_SPLITS, axis=-1)
    c_kv = rms_norm(c_kv, lw["mla_kv_g"])
    k_nope = (c_kv @ lw["w_uk"]).reshape(B, T, MLA_HEADS, MLA_NOPE_DIM)
    v_m = (c_kv @ lw["w_uv"]).reshape(B, T, MLA_HEADS, MLA_V_DIM)
    k_r = k_r[:, :, None, :]
    k_g = rms_norm(k_g.reshape(B, T, GQA_KV_HEADS, GQA_HEAD_DIM), lw["gqa_k_g"])
    v_g = v_g.reshape(B, T, GQA_KV_HEADS, GQA_HEAD_DIM)
    if rope is not None:
        k_r = apply_rope(k_r, *rope[0])
        k_g = apply_rope(k_g, *rope[1])
    k_m = jnp.concatenate([k_nope, jnp.broadcast_to(k_r, (B, T, MLA_HEADS, MLA_ROPE_DIM))], axis=-1)
    return (k_m, v_m, k_g, v_g)

def mixer(p, kv, lw, rope):
    B, S, _ = p.shape
    k_m, v_m, k_g, v_g = kv
    f_in, c_q, q_g, gate_logits = jnp.split(p[..., KV_COLS:], REST_SPLITS, axis=-1)
    y_f = fourier_mix(f_in) @ lw["w_fo"]
    q_m = (rms_norm(c_q, lw["mla_q_g"]) @ lw["w_uq"]).reshape(B, S, MLA_HEADS, MLA_QK_DIM)
    q_nope, q_rope = jnp.split(q_m, [MLA_NOPE_DIM], axis=-1)
    q_g = rms_norm(q_g.reshape(B, S, GQA_HEADS, GQA_HEAD_DIM), lw["gqa_q_g"])
    if rope is not None:
        q_rope = apply_rope(q_rope, *rope[0])
        q_g = apply_rope(q_g, *rope[1])
    q_m = jnp.concatenate([q_nope, q_rope], axis=-1)[:, :, :, None, :] * (MLA_QK_DIM ** -0.5)
    y_m = attend(q_m, k_m, v_m) @ lw["w_mo"]
    q_g = q_g.reshape(B, S, GQA_KV_HEADS, GQA_GROUP, GQA_HEAD_DIM) * (GQA_HEAD_DIM ** -0.5)
    y_g = attend(q_g, k_g, v_g) @ lw["w_go"]
    g_f, g_m, g_g = jnp.split(jax.nn.sigmoid(gate_logits + lw["b_gate"]), N_BRANCHES, axis=-1)
    return (g_f * y_f + g_m * y_m + g_g * y_g) @ lw["w_o"]

def sq_relu_mlp(h, lw):
    return jnp.square(jax.nn.relu(h @ lw["w1"])) @ lw["w2"]

def first_inputs(seed: int = 0) -> dict:
    key = jax.random.key(seed)
    ks = iter(jax.random.split(key, 32))

    def nrm(shape, scale):
        return jax.random.normal(next(ks), shape, jnp.float32) * scale

    def gain(shape):
        return 1.0 + nrm(shape, 0.02)

    L, D = DEPTH, D_MODEL
    beta = (8.0 * DEPTH) ** -0.25
    return {
        "x": nrm((BATCH, SEQ, D), 1.0),
        "c": nrm((BATCH, D), 1.0),
        "ctx": nrm((BATCH, CTX_LEN, D), 1.0),
        "c_ctx": nrm((D,), 1.0),
        "w_ada": nrm((L, D, N_MOD * D), 0.5 * D ** -0.5),
        "b_ada": nrm((L, N_MOD * D), 0.01),
        "w_in": nrm((L, D, IN_COLS), D ** -0.5),
        "b_gate": nrm((L, N_BRANCHES * D), 0.01),
        "mla_q_g": gain((L, MLA_Q_RANK)),
        "mla_kv_g": gain((L, MLA_KV_RANK)),
        "w_uq": nrm((L, MLA_Q_RANK, MLA_HEADS * MLA_QK_DIM), MLA_Q_RANK ** -0.5),
        "w_uk": nrm((L, MLA_KV_RANK, MLA_HEADS * MLA_NOPE_DIM), MLA_KV_RANK ** -0.5),
        "w_uv": nrm((L, MLA_KV_RANK, MLA_HEADS * MLA_V_DIM), MLA_KV_RANK ** -0.5),
        "gqa_q_g": gain((L, GQA_HEAD_DIM)),
        "gqa_k_g": gain((L, GQA_HEAD_DIM)),
        "w_fo": nrm((L, F_WIDTH, D), F_WIDTH ** -0.5),
        "w_mo": nrm((L, MLA_WIDTH, D), MLA_WIDTH ** -0.5),
        "w_go": nrm((L, GQA_WIDTH, D), GQA_WIDTH ** -0.5),
        "w_o": nrm((L, D, D), beta * D ** -0.5),
        "ln1_g": gain((L, D)),
        "ln1_b": nrm((L, D), 0.02),
        "w1": nrm((L, D, D_FF), D ** -0.5),
        "w2": nrm((L, D_FF, D), beta * D_FF ** -0.5),
        "ln2_g": gain((L, D)),
        "ln2_b": nrm((L, D), 0.02),
    }

def first_block(x, c, ctx, c_ctx, w_ada, b_ada, w_in, b_gate, mla_q_g, mla_kv_g, w_uq, w_uk, w_uv,
              gqa_q_g, gqa_k_g, w_fo, w_mo, w_go, w_o, ln1_g, ln1_b, w1, w2, ln2_g, ln2_b):
    B, S, D = x.shape
    ROWS = S // GRID_W
    rows = jnp.repeat(jnp.arange(ROWS), GRID_W).astype(jnp.float32)
    cols = jnp.tile(jnp.arange(GRID_W), ROWS).astype(jnp.float32)
    rope = (rope_angles(rows, cols, MLA_ROPE_DIM), rope_angles(rows, cols, GQA_HEAD_DIM))
    alpha = (2.0 * DEPTH) ** 0.25
    xc = ctx
    for l in range(DEPTH):
        last = l == DEPTH - 1
        lw = {
            "w_in": w_in[l], "b_gate": b_gate[l], "mla_q_g": mla_q_g[l], "mla_kv_g": mla_kv_g[l],
            "w_uq": w_uq[l], "w_uk": w_uk[l], "w_uv": w_uv[l], "gqa_q_g": gqa_q_g[l],
            "gqa_k_g": gqa_k_g[l], "w_fo": w_fo[l], "w_mo": w_mo[l], "w_go": w_go[l], "w_o": w_o[l],
            "w1": w1[l], "w2": w2[l],
        }
        mod_x = (jax.nn.silu(c) @ w_ada[l] + b_ada[l])[:, None, :]
        mod_c = (jax.nn.silu(c_ctx) @ w_ada[l] + b_ada[l])[None, None, :]
        sh1, sc1, g1, sh2, sc2, g2 = jnp.split(mod_x, N_MOD, axis=-1)
        csh1, csc1, cg1, csh2, csc2, cg2 = jnp.split(mod_c, N_MOD, axis=-1)

        h_x = modulate(x, sh1, sc1)
        h_c = modulate(xc, csh1, csc1)
        p_x = h_x @ lw["w_in"]
        p_c = h_c @ (lw["w_in"][:, :KV_COLS] if last else lw["w_in"])
        kv_c = kv_parts(p_c, lw, None)
        kv_x = kv_parts(p_x, lw, rope)
        kv_all = (
            jnp.concatenate([kv_c[0], kv_x[0]], axis=1),
            jnp.concatenate([kv_c[1], kv_x[1]], axis=1),
            jnp.concatenate([kv_c[2], kv_x[2]], axis=1),
            jnp.concatenate([kv_c[3], kv_x[3]], axis=1),
        )
        mix_x = mixer(p_x, kv_all, lw, rope)
        x = layer_norm(alpha * x + g1 * mix_x, ln1_g[l], ln1_b[l])
        x = layer_norm(alpha * x + g2 * sq_relu_mlp(modulate(x, sh2, sc2), lw), ln2_g[l], ln2_b[l])

        if not last:
            mix_c = mixer(p_c, kv_c, lw, None)
            xc = layer_norm(alpha * xc + cg1 * mix_c, ln1_g[l], ln1_b[l])
            xc = layer_norm(alpha * xc + cg2 * sq_relu_mlp(modulate(xc, csh2, csc2), lw), ln2_g[l], ln2_b[l])
    return x


D_FF_2 = 2816
NSA_HEADS = 8
NSA_GROUPS = 2
NSA_HPG = NSA_HEADS // NSA_GROUPS
NSA_DH = 64
CMP_BLOCK = 32
CMP_STRIDE = 16
CMP_HIDDEN = 256
SEL_BLOCK = 64
SEL_TOPN = 16
WINDOW = 512
Q_BLOCK_2 = 64
GLA_HEADS = 4
GLA_DK = 128
GLA_DV = 256
GLA_RANK = 16
GLA_TAU = 16.0
GLA_CHUNK = 64
REL_BUCKETS = 32
REL_MAX_DIST = 1024
NEG = -1e30

W_IN_SPLITS = (
    NSA_HEADS * NSA_DH,
    6 * NSA_GROUPS * NSA_DH,
    3 * NSA_HEADS,
    GLA_HEADS * GLA_DK,
    GLA_HEADS * GLA_DK,
    GLA_HEADS * GLA_DV,
    GLA_RANK,
    GLA_HEADS * GLA_DV,
    2 * D_MODEL,
)
D_IN = sum(W_IN_SPLITS)


def rmsnorm(x, g):
    xf = x.astype(jnp.float32)
    y = xf * lax.rsqrt(jnp.mean(xf * xf, axis=-1, keepdims=True) + EPS)
    return (y * g.astype(jnp.float32)).astype(x.dtype)

def swiglu(x, w_gate, w_up, w_down):
    return (jax.nn.silu(x @ w_gate) * (x @ w_up)) @ w_down

def rel_bucket(dist):
    n = jnp.maximum(dist, 0)
    exact = REL_BUCKETS // 2
    nf = jnp.maximum(n, 1).astype(jnp.float32)
    log_b = exact + (jnp.log(nf / exact) / math.log(REL_MAX_DIST / exact)
                     * (REL_BUCKETS - exact)).astype(jnp.int32)
    return jnp.where(n < exact, n, jnp.minimum(log_b, REL_BUCKETS - 1))

def masked_softmax(logits, mask):
    p = jax.nn.softmax(jnp.where(mask, logits, NEG), axis=-1)
    return jnp.where(mask, p, 0.0)

def nsa_compress(k, pos, w1, w2):
    B, S, G, dh = k.shape
    nc = (S - CMP_BLOCK) // CMP_STRIDE + 1
    idx = jnp.arange(nc)[:, None] * CMP_STRIDE + jnp.arange(CMP_BLOCK)[None, :]
    blocks = k[:, idx] + pos[None, None, :, None, :]
    blocks = blocks.transpose(0, 1, 3, 2, 4).reshape(B, nc, G, CMP_BLOCK * dh)
    return jax.nn.silu(blocks @ w1) @ w2

def nsa_attention(q, k_cmp, v_cmp, k_slc, v_slc, k_win, v_win, gates, rel_table):
    B, S, H, dh = q.shape
    G, HPG = NSA_GROUPS, NSA_HPG
    nqb = S // Q_BLOCK_2
    ns = S // SEL_BLOCK
    nc = k_cmp.shape[1]
    n_sel = min(SEL_TOPN, ns)
    kw_len = WINDOW + Q_BLOCK_2

    c_start = jnp.arange(nc) * CMP_STRIDE
    cmp_end = c_start + CMP_BLOCK - 1
    sb_start = jnp.arange(ns) * SEL_BLOCK
    overlap = ((c_start[:, None] < sb_start[None, :] + SEL_BLOCK)
               & (c_start[:, None] + CMP_BLOCK > sb_start[None, :])).astype(jnp.float32)
    js = jnp.arange(ns)
    table_g = rel_table.reshape(REL_BUCKETS, G, HPG).transpose(1, 0, 2)

    kb = k_slc.reshape(B, ns, SEL_BLOCK, G, dh).transpose(0, 3, 1, 2, 4)
    vb = v_slc.reshape(B, ns, SEL_BLOCK, G, dh).transpose(0, 3, 1, 2, 4)
    pad = ((0, 0), (WINDOW, 0), (0, 0), (0, 0))
    kw = jnp.pad(k_win, pad)
    vw = jnp.pad(v_win, pad)

    def to_blocks(a):
        return a.reshape(B, nqb, Q_BLOCK_2, *a.shape[2:]).swapaxes(0, 1)

    qs = to_blocks(q * (dh ** -0.5))
    gs = to_blocks(gates)
    bi = jnp.arange(B)[:, None, None, None]
    gi = jnp.arange(G)[None, :, None, None]

    def block_fn(args):
        c, qc, gc = args
        t = c * Q_BLOCK_2 + jnp.arange(Q_BLOCK_2)
        qg = qc.reshape(B, Q_BLOCK_2, G, HPG, dh)

        lc = jnp.einsum('bqghd,bcgd->bghqc', qg, k_cmp).astype(jnp.float32)
        bias_c = rel_table[rel_bucket(t[:, None] - cmp_end[None, :])]
        lc = lc + bias_c.reshape(Q_BLOCK_2, nc, G, HPG).transpose(2, 3, 0, 1)
        p_cmp = masked_softmax(lc, cmp_end[None, :] <= t[:, None])
        o_cmp = jnp.einsum('bghqc,bcgd->bqghd', p_cmp.astype(v_cmp.dtype), v_cmp)

        imp = jnp.einsum('bghqc,cs->bgqs', p_cmp, overlap)
        jcur = t // SEL_BLOCK
        forced = (js[None, :] == 0) | (js[None, :] == jcur[:, None]) | (js[None, :] == jcur[:, None] - 1)
        valid = js[None, :] <= jcur[:, None]
        score = jnp.where(forced, 1e6, jnp.where(valid, imp, -1e6))
        _, sel = lax.top_k(score, n_sel)
        ks = kb[bi, gi, sel]
        vs = vb[bi, gi, sel]
        s_pos = sel[..., None] * SEL_BLOCK + jnp.arange(SEL_BLOCK)
        ls = jnp.einsum('bqghd,bgqnrd->bghqnr', qg, ks).astype(jnp.float32)
        bias_s = table_g[gi[..., None], rel_bucket(t[:, None, None] - s_pos)]
        ls = ls + bias_s.transpose(0, 1, 5, 2, 3, 4)
        ksel = n_sel * SEL_BLOCK
        ls = ls.reshape(B, G, HPG, Q_BLOCK_2, ksel)
        ms = (s_pos <= t[:, None, None]).reshape(B, G, Q_BLOCK_2, ksel)[:, :, None]
        p_s = masked_softmax(ls, ms)
        o_slc = jnp.einsum('bghqk,bgqkd->bqghd', p_s.astype(vs.dtype),
                           vs.reshape(B, G, Q_BLOCK_2, ksel, dh))

        kwc = lax.dynamic_slice_in_dim(kw, c * Q_BLOCK_2, kw_len, axis=1)
        vwc = lax.dynamic_slice_in_dim(vw, c * Q_BLOCK_2, kw_len, axis=1)
        s_w = c * Q_BLOCK_2 - WINDOW + jnp.arange(kw_len)
        dist = t[:, None] - s_w[None, :]
        mw = (s_w[None, :] >= 0) & (dist >= 0) & (dist < WINDOW)
        lw = jnp.einsum('bqghd,bkgd->bghqk', qg, kwc).astype(jnp.float32)
        lw = lw + rel_table[rel_bucket(dist)].reshape(Q_BLOCK_2, kw_len, G, HPG).transpose(2, 3, 0, 1)
        p_w = masked_softmax(lw, mw)
        o_win = jnp.einsum('bghqk,bkgd->bqghd', p_w.astype(vwc.dtype), vwc)

        o = jnp.stack([o_cmp, o_slc, o_win], axis=-1)
        g = gc.reshape(B, Q_BLOCK_2, G, HPG, 3)[..., None, :]
        return jnp.sum(o * g, axis=-1).reshape(B, Q_BLOCK_2, H * dh).astype(q.dtype)

    out = lax.map(block_fn, (jnp.arange(nqb), qs, gs))
    return out.swapaxes(0, 1).reshape(B, S, H * dh)

def gla_attention(q, k, v, log_a):
    B, S, Hb, dk = q.shape
    dv = v.shape[-1]
    C = GLA_CHUNK
    n = S // C

    def chunks(a):
        return a.reshape(B, n, C, *a.shape[2:])

    qc, kc, vc, la = chunks(q * (dk ** -0.5)), chunks(k), chunks(v), chunks(log_a)
    b = jnp.cumsum(la.astype(jnp.float32), axis=2)
    b_last = b[:, :, -1:]
    q_dec = qc * jnp.exp(b)
    k_intra = kc * jnp.exp(-b)
    k_state = kc * jnp.exp(b_last - b)
    causal = jnp.tril(jnp.ones((C, C), dtype=bool))
    A = jnp.where(causal, jnp.einsum('bnihd,bnjhd->bnhij', q_dec, k_intra), 0.0)
    o_intra = jnp.einsum('bnhij,bnjhv->bnihv', A, vc.astype(jnp.float32))
    decay_chunk = jnp.exp(b_last[:, :, 0])

    def step(state, inp):
        qd, ksd, vcc, dch = inp
        o = jnp.einsum('bihd,bhdv->bihv', qd, state)
        state = dch[..., None] * state + jnp.einsum('bjhd,bjhv->bhdv', ksd, vcc.astype(jnp.float32))
        return state, o

    s0 = jnp.zeros((B, Hb, dk, dv), jnp.float32)
    _, o_inter = lax.scan(step, s0, (q_dec.swapaxes(0, 1), k_state.swapaxes(0, 1),
                                     vc.swapaxes(0, 1), decay_chunk.swapaxes(0, 1)))
    o = o_intra + o_inter.swapaxes(0, 1)
    return o.reshape(B, S, Hb, dv).astype(v.dtype)

def second_inputs(seed: int = 0) -> dict:
    key = jax.random.key(seed)
    ks = jax.random.split(key, 32)
    f32 = jnp.float32
    L, D = DEPTH, D_MODEL

    def w(k, shape, fan_in):
        return jax.random.normal(k, shape, f32) * fan_in ** -0.5

    def gain(k, shape):
        return 1.0 + 0.05 * jax.random.normal(k, shape, f32)

    return {
        "x": jax.random.normal(ks[0], (BATCH, SEQ, D), f32),
        "rel_table": 0.2 * jax.random.normal(ks[1], (REL_BUCKETS, NSA_HEADS), f32),
        "ffn1_norm": gain(ks[2], (L, D)),
        "ffn1_w_gate": w(ks[3], (L, D, D_FF_2), D),
        "ffn1_w_up": w(ks[4], (L, D, D_FF_2), D),
        "ffn1_w_down": w(ks[5], (L, D_FF_2, D), D_FF_2),
        "mix_norm": gain(ks[6], (L, D)),
        "w_in": w(ks[7], (L, D, D_IN), D),
        "cmp_pos_k": 0.5 * jax.random.normal(ks[8], (L, CMP_BLOCK, NSA_DH), f32),
        "cmp_pos_v": 0.5 * jax.random.normal(ks[9], (L, CMP_BLOCK, NSA_DH), f32),
        "cmp_k_w1": w(ks[10], (L, CMP_BLOCK * NSA_DH, CMP_HIDDEN), CMP_BLOCK * NSA_DH),
        "cmp_k_w2": w(ks[11], (L, CMP_HIDDEN, NSA_DH), CMP_HIDDEN),
        "cmp_v_w1": w(ks[12], (L, CMP_BLOCK * NSA_DH, CMP_HIDDEN), CMP_BLOCK * NSA_DH),
        "cmp_v_w2": w(ks[13], (L, CMP_HIDDEN, NSA_DH), CMP_HIDDEN),
        "gla_a_w2": w(ks[14], (L, GLA_RANK, GLA_HEADS * GLA_DK), GLA_RANK),
        "gla_a_b": 0.1 * jax.random.normal(ks[15], (L, GLA_HEADS * GLA_DK), f32),
        "gla_out_norm": gain(ks[16], (L, GLA_HEADS * GLA_DV)),
        "w_branch_nsa": w(ks[17], (L, NSA_HEADS * NSA_DH, D), NSA_HEADS * NSA_DH),
        "w_branch_gla": w(ks[18], (L, GLA_HEADS * GLA_DV, D), GLA_HEADS * GLA_DV),
        "w_out": w(ks[19], (L, D, D), D),
        "ffn2_norm": gain(ks[20], (L, D)),
        "ffn2_w_gate": w(ks[21], (L, D, D_FF_2), D),
        "ffn2_w_up": w(ks[22], (L, D, D_FF_2), D),
        "ffn2_w_down": w(ks[23], (L, D_FF_2, D), D_FF_2),
        "final_norm": gain(ks[24], (D,)),
    }

def second_block(x, rel_table, ffn1_norm, ffn1_w_gate, ffn1_w_up, ffn1_w_down, mix_norm, w_in,
              cmp_pos_k, cmp_pos_v, cmp_k_w1, cmp_k_w2, cmp_v_w1, cmp_v_w2, gla_a_w2, gla_a_b,
              gla_out_norm, w_branch_nsa, w_branch_gla, w_out, ffn2_norm, ffn2_w_gate, ffn2_w_up,
              ffn2_w_down, final_norm):
    B, S, D = x.shape
    offsets = np.cumsum(W_IN_SPLITS)[:-1].tolist()
    for l in range(DEPTH):
        x = x + 0.5 * swiglu(rmsnorm(x, ffn1_norm[l]), ffn1_w_gate[l], ffn1_w_up[l], ffn1_w_down[l])

        h = rmsnorm(x, mix_norm[l])
        proj = h @ w_in[l]
        q_a, kv_a, g_a, q_b, k_b, v_b, a_lr, r_b, g_merge = jnp.split(proj, offsets, axis=-1)

        q_a = q_a.reshape(B, S, NSA_HEADS, NSA_DH)
        kv_a = kv_a.reshape(B, S, 6, NSA_GROUPS, NSA_DH)
        k_cmp = nsa_compress(kv_a[:, :, 0], cmp_pos_k[l], cmp_k_w1[l], cmp_k_w2[l])
        v_cmp = nsa_compress(kv_a[:, :, 1], cmp_pos_v[l], cmp_v_w1[l], cmp_v_w2[l])
        gates_a = jax.nn.sigmoid(g_a).reshape(B, S, NSA_HEADS, 3)
        o_a = nsa_attention(q_a, k_cmp, v_cmp, kv_a[:, :, 2], kv_a[:, :, 3],
                            kv_a[:, :, 4], kv_a[:, :, 5], gates_a, rel_table)

        log_a = jax.nn.log_sigmoid((a_lr @ gla_a_w2[l] + gla_a_b[l]).astype(jnp.float32)) / GLA_TAU
        o_b = gla_attention(q_b.reshape(B, S, GLA_HEADS, GLA_DK),
                            k_b.reshape(B, S, GLA_HEADS, GLA_DK),
                            v_b.reshape(B, S, GLA_HEADS, GLA_DV),
                            log_a.reshape(B, S, GLA_HEADS, GLA_DK))
        o_b = rmsnorm(o_b, gla_out_norm[l].reshape(GLA_HEADS, GLA_DV))
        o_b = o_b.reshape(B, S, GLA_HEADS * GLA_DV) * jax.nn.silu(r_b)

        gm = jax.nn.sigmoid(g_merge).reshape(B, S, 2, D)
        y = gm[:, :, 0] * (o_a @ w_branch_nsa[l]) + gm[:, :, 1] * (o_b @ w_branch_gla[l])
        x = x + y @ w_out[l]

        x = x + 0.5 * swiglu(rmsnorm(x, ffn2_norm[l]), ffn2_w_gate[l], ffn2_w_up[l], ffn2_w_down[l])
    return rmsnorm(x, final_norm)


def setup_inputs(seed=0):
    out = dict(first_inputs(seed))
    for name, value in second_inputs(seed + 1).items():
        if name != "x":
            out[name + "_2"] = value
    return out


def reference(
    x, c, ctx, c_ctx, w_ada, b_ada, w_in, b_gate, mla_q_g, mla_kv_g, w_uq, w_uk, w_uv, gqa_q_g,
    gqa_k_g, w_fo, w_mo, w_go, w_o, ln1_g, ln1_b, w1, w2, ln2_g, ln2_b, rel_table_2,
    ffn1_norm_2, ffn1_w_gate_2, ffn1_w_up_2, ffn1_w_down_2, mix_norm_2, w_in_2, cmp_pos_k_2,
    cmp_pos_v_2, cmp_k_w1_2, cmp_k_w2_2, cmp_v_w1_2, cmp_v_w2_2, gla_a_w2_2, gla_a_b_2,
    gla_out_norm_2, w_branch_nsa_2, w_branch_gla_2, w_out_2, ffn2_norm_2, ffn2_w_gate_2,
    ffn2_w_up_2, ffn2_w_down_2, final_norm_2,
):
    x = first_block(
        x, c, ctx, c_ctx, w_ada, b_ada, w_in, b_gate, mla_q_g, mla_kv_g, w_uq, w_uk, w_uv,
        gqa_q_g, gqa_k_g, w_fo, w_mo, w_go, w_o, ln1_g, ln1_b, w1, w2, ln2_g, ln2_b,
    )
    return second_block(
        x, rel_table_2, ffn1_norm_2, ffn1_w_gate_2, ffn1_w_up_2, ffn1_w_down_2, mix_norm_2,
        w_in_2, cmp_pos_k_2, cmp_pos_v_2, cmp_k_w1_2, cmp_k_w2_2, cmp_v_w1_2, cmp_v_w2_2,
        gla_a_w2_2, gla_a_b_2, gla_out_norm_2, w_branch_nsa_2, w_branch_gla_2, w_out_2,
        ffn2_norm_2, ffn2_w_gate_2, ffn2_w_up_2, ffn2_w_down_2, final_norm_2,
    )


_drawn_inputs = setup_inputs


def setup_inputs(seed=0):
    import zlib

    import numpy as np

    out = dict(_drawn_inputs(seed))
    spreads = {}
    factors = {'ctx': 6.179,
     'b_ada': 4.541,
     'b_gate': 8.0,
     'mla_q_g': 8.0,
     'mla_kv_g': 8.0,
     'w_uq': 5.197,
     'w_uk': 5.846,
     'gqa_q_g': 8.0,
     'gqa_k_g': 8.0,
     'cmp_pos_k_2': 4.296,
     'gla_a_b_2': 2.969}
    for name, (base, spread) in spreads.items():
        noise = np.random.default_rng([zlib.crc32(name.encode()), seed]).standard_normal(out[name].shape)
        drawn = base * np.exp(spread * noise) if base else spread * noise
        out[name] = __import__('jax').numpy.asarray(drawn.astype(out[name].dtype))
    for name, factor in factors.items():
        out[name] = (out[name] * factor).astype(out[name].dtype)
    return out
```

```python
from contextlib import ExitStack, contextmanager

import concourse.bass as bass
from concourse import mybir

F32 = mybir.dt.float32
ALU = mybir.AluOpType
ACT = mybir.ActivationFunctionType
AX = mybir.AxisListType.X

P = 128
D = 1024
KD = D // P
CTX, SEQ = 256, 256
TOK = CTX + SEQ
LAYERS = 2
EPS = 1e-6
ALPHA = (2.0 * LAYERS) ** 0.25
NEG = -1e30

MODS = 6 * D // P
HEADS, NOPE, ROPE, HD = 8, 64, 32, 64
RANK = 256
GATE0 = 544 + 512 + 256 + 512
FF1 = 4 * D
MLA_SCALE = float(NOPE + ROPE) ** -0.5
GQA_SCALE = float(HD) ** -0.5

FF2 = 2816
FT = FF2 // P
NCMP, CMP_STRIDE, CMP_BLOCK = 15, 16, 32
JP = CMP_BLOCK // 2
GH, DV, CHUNK = 4, 256, 64
NCH = SEQ // CHUNK
TAU = 16.0
BUCKETS = 32

SLOTS = 4
SLOT = 4608
LAND = 192
BANKS = 8

VEC_TILES = [
    [("b_ada", 96), ("ln1_g", 16), ("ln1_b", 16)],
    [("b_gate", 48), ("ln2_g", 16), ("ln2_b", 16), ("mla_q_g", 4), ("mla_kv_g", 4), ("gqa_q_g", 2),
     ("gqa_k_g", 2), ("c", 8), ("c_ctx", 8), ("gla_out_norm_2", 16)],
    [("cmp_pos_k_2", 32), ("cmp_pos_v_2", 32), ("ffn1_norm_2", 16), ("mix_norm_2", 16), ("ffn2_norm_2", 16),
     ("final_norm_2", 8), ("gla_a_b_2", 8)],
]
VEC = {}
VEC_ROWS = []
for _t, _names in enumerate(VEC_TILES):
    _r = 0
    for _name, _n in _names:
        VEC[_name] = (_t, _r, _n)
        _r += _n
    VEC_ROWS.append(_r)

CONST = {}
_at = 0
for _name, _n in [("ident", 128), ("ones", 128), ("pair", 128), ("rot32", 128), ("rot64", 128), ("dft_d", 256),
                  ("cos_s", 512), ("nsin_s", 512), ("cos32", 256), ("sin32", 256), ("cos64", 256), ("sin64", 256),
                  ("causal", 128), ("has_cmp", 2), ("eps", 1), ("one", 1)]:
    CONST[_name] = (_at, _n)
    _at += _n
NCONST = _at


def shape_constants():
    import numpy as np

    c = {}
    i = np.arange(P)
    c["ident"] = np.eye(P)
    c["ones"] = np.ones((P, P))
    c["pair"] = (i[:, None] // HD == i[None, :] // HD).astype(np.float64)

    def rotation(n):
        r = np.zeros((P, P))
        for m in range(P):
            half = n // 2
            if m % n < half:
                r[m + half, m] = -1.0
            else:
                r[m - half, m] = 1.0
        return r

    c["rot32"], c["rot64"] = rotation(ROPE), rotation(HD)
    ang = 2 * np.pi * ((i[:, None] * i[None, :]) % P) / P
    norm = 1.0 / np.sqrt(P * SEQ)
    c["dft_d"] = np.concatenate([np.cos(ang), np.sin(ang)], axis=1) * norm
    s = np.arange(SEQ)
    angs = 2 * np.pi * ((s[:, None] * s[None, :]) % SEQ) / SEQ
    c["cos_s"] = np.concatenate([np.cos(angs)[:P], np.cos(angs)[P:]], axis=1)
    c["nsin_s"] = -np.concatenate([np.sin(angs)[:P], np.sin(angs)[P:]], axis=1)
    grid_w = 64
    rows = np.repeat(np.arange(SEQ // grid_w), grid_w).astype(np.float32)
    cols = np.tile(np.arange(grid_w), SEQ // grid_w).astype(np.float32)
    for d_rot in (ROPE, HD):
        n = d_rot // 4
        freqs = np.float32(10000.0) ** (-np.arange(n, dtype=np.float32) / np.float32(n))
        a = np.concatenate([rows[:, None] * freqs, cols[:, None] * freqs], axis=-1).astype(np.float32)
        a = a[:, i % (d_rot // 2)].T
        c[f"cos{d_rot}"], c[f"sin{d_rot}"] = np.cos(a), np.sin(a)
    c["causal"] = ((i[:, None] // CHUNK == i[None, :] // CHUNK) & (i[:, None] <= i[None, :])).astype(np.float64)
    c["has_cmp"] = np.stack([i >= CMP_BLOCK - 1, i >= 0], axis=1).astype(np.float64)
    c["eps"] = np.full((P, 1), EPS)
    c["one"] = np.ones((P, 1))
    consts = np.concatenate([c[n].reshape(P, -1) for n in CONST], axis=1).astype(np.float32)

    def bucket(dist):
        n = np.maximum(dist, 0)
        exact = BUCKETS // 2
        nf = np.maximum(n, 1).astype(np.float32)
        ratio = np.log(nf / np.float32(exact)) / np.float32(np.log(1024 / exact))
        log_b = exact + (ratio * np.float32(BUCKETS - exact)).astype(np.int32)
        return np.where(n < exact, n, np.minimum(log_b, BUCKETS - 1))

    def one_hot(dist):
        hot = np.zeros((BUCKETS + 1,) + dist.shape, np.float32)
        b = np.where(dist >= 0, bucket(dist), BUCKETS)
        for k in range(BUCKETS + 1):
            hot[k] = b == k
        return hot

    toeplitz = one_hot(255 - np.arange(512))
    blocks = one_hot(s[None, :] - (np.arange(NCMP)[:, None] * CMP_STRIDE + CMP_BLOCK - 1))
    return {"consts": consts, "bucket_of_distance": toeplitz,
            "bucket_of_block": np.ascontiguousarray(blocks.reshape(BUCKETS + 1, NCMP * SEQ))}


class Tally:

    def __init__(self):
        self.count = {}
        self.regs = []
        self.bank = 0

    def value(self, name, off=0, div=1):
        v = (self.count.get(name, 0) + off) // div
        for reg, per in self.regs:
            n = per.get(name, 0)
            assert n % div == 0, (name, n)
            if n:
                v = reg * (n // div) + v
        return v

    def next(self, name, n=1):
        self.count[name] = self.count.get(name, 0) + n
        return self.value(name)

    def take(self):
        b = self.bank
        self.bank = (b + 1) % BANKS
        return b, self.next(f"bank{b}")

    def last(self):
        b = (self.bank - 1) % BANKS
        return b, self.value(f"bank{b}")

    def panel(self):
        n = self.next("panel")
        slot = (self.count["panel"] - 1) % SLOTS
        return slot, self.value("panel", SLOTS - 1, SLOTS) * LAND, n

    @contextmanager
    def loop(self, reg, times, per):
        per = dict(per)
        tiles = per.pop("tiles", 0)
        for j in range(tiles):
            b = f"bank{(self.bank + j) % BANKS}"
            per[b] = per.get(b, 0) + 1
        before = dict(self.count)
        self.regs.append((reg, per))
        yield
        self.regs.pop()
        added = {n: v - before.get(n, 0) for n, v in self.count.items() if v != before.get(n, 0)}
        assert added == per, {n: (added.get(n, 0), per.get(n, 0)) for n in {*added, *per}
                              if added.get(n, 0) != per.get(n, 0)}
        for n, v in per.items():
            self.count[n] = before.get(n, 0) + v * times


class Chip:

    def __init__(self, nc, ctx):
        def sb(name, n, parts=P):
            return ctx.enter_context(nc.sbuf_tensor(name, [parts, n], F32))

        def sem(name):
            return ctx.enter_context(nc.semaphore(name))

        self.ring = [sb(f"ring{s}", SLOT) for s in range(SLOTS)]
        self.xT = sb("xT", KD * TOK)[:, :].rearrange("p (k t) -> p k t", k=KD)
        self.hbuf = sb("hT", KD * TOK)
        self.hT = self.hbuf[:, :].rearrange("p (k t) -> p k t", k=KD)
        self.h2 = self.hbuf[:, 0:KD * SEQ].rearrange("p (k t) -> p k t", k=KD)
        self.bias = self.hbuf[:, KD * SEQ:2 * KD * SEQ].rearrange("p (h u) -> p h u", h=HEADS)
        self.const = sb("const", NCONST)
        self.vecT = sb("vecT", len(VEC_TILES) * P)
        self.mods = sb("mods", 2 * MODS)[:, :].rearrange("p (m s) -> p m s", s=2)
        self.silu_c = sb("silu_c", 2 * KD)[:, :].rearrange("p (k s) -> p k s", s=2)
        self.arena = sb("arena", 20992)
        self.cmp_bias = sb("cmp_bias", 2 * HEADS * NCMP)[:, :].rearrange("p (q h n) -> p q h n", q=2, h=HEADS)
        self.hid_v = sb("hid_v", 2 * 2 * P)[:, :].rearrange("p (m g r n) -> p m g r n", m=2, g=2, r=4)
        self.p_cmp = sb("p_cmp", 2 * HEADS * 32)[:, :].rearrange("p (q h n) -> p q h n", q=2, h=HEADS)
        self.stat = sb("stat", 64)
        self.ps = ctx.enter_context(nc.psum_tensor("ps", [P, BANKS, 512], F32))

        self.panel_landed = [sem(f"panel_landed{s}") for s in range(SLOTS)]
        self.panel_begun = sem("panel_begun")
        self.bank_done = [sem(f"bank_done{b}") for b in range(BANKS)]
        self.bank_read = [sem(f"bank_read{b}") for b in range(BANKS)]
        self.sem = {name: sem(name) for name in (
            "act_step", "dve_step",
            "const_in", "vec_in", "tok_in", "table_in", "neg_row", "silu_c_ready", "row_out", "row_copied", "bias_in",
            "out_ready", "out_done",
            "x_ready", "y_ready", "centred", "squared", "h_ready",
            "squared_qk", "normed", "roped", "row_max", "prob_ready", "gated", "relu_ready",
            "minus_abs_z", "log1p_ready", "decay_ready", "edecay", "edecay_used", "gla_in", "gla_out", "gla_ready",
            "cmp_max", "cmp_exp", "cmp_prob", "nsa_max", "nsa_exp", "nsa_prob", "merged")}

    def area(self, at, *dims):
        n = 1
        for d in dims:
            n *= d
        v = self.arena[:, at:at + n]
        if len(dims) == 1:
            return v
        names = "abcd"[:len(dims)]
        return v.rearrange(f"p ({' '.join(names)}) -> p {' '.join(names)}", **dict(zip(names[1:], dims[1:])))

    def moved(self, result):
        return self.bank_read[result[0]], result[1]

    def col(self, name):
        at, n = CONST[name]
        return self.const[:, at:at + n]

    def vec(self, name, j):
        t, r, _ = VEC[name]
        return self.vecT[:, bass.ds(t * P + r + j, 1)]


CKV, CQ, KR, KG, VG, FIN, QG, QN, QR, KN, VM, OM, OG, PROBT = (
    0, 1024, 2048, 2560, 3072, 3584, 5632, 7680, 9728, 10752, 12800, 14848, 16896, 18944)
PROB = CKV
MIXED = QG
SQK, DFT1, ROT = OM, 19456, OM
GATE_F, TMP_M, TMP_G = PROB, PROBT + 1024, PROBT + 1536
SQ, MEAN, STD = 0, 4096, 4608
HID, RELU = 0, 4 * KD * TOK
A2, SILU2, SQ2, STD2 = 0, 5632, 6656, 8704
(QA, KSLC, KWIN, VSLC, VWIN, GA, DCH, KCMP, VCMP, HIDK, ALR, KBK, KBV, OA, PCT, PROB2, PROBT2, QB, KB, KIN, Z, T1, VB,
 RB, OB, CHAIN) = (0, 1024, 1280, 1536, 1792, 2048, 2096, 2112, 2128, 2256, 2320, 2576, 3056, 3536, 4560, 5072, 6608,
                   8144, 9168, 10192, 11216, 12240, 13264, 15312, 17360, 19408)
STATE, SQO, MIXED2, MGATE = PROB2, KB, VB, Z
XN, VN, TABLE, HOT, HOTC = 0, 4096, 4480, 4608, 5120
SH1, SC1, G1, SH2, SC2, G2 = (KD * j for j in range(6))
HALVES = [(0, CTX), (CTX, TOK)]
DOWN_TILES = [6, 6, 5, 5]


N_VEC = len(VEC) + 2
LAST_DOWN = 4
PER_BANK = {f"bank{b}": n for b, n in enumerate((30, 31, 32, 32, 32, 31, 30, 30))}
PER_LAYER = {
    "pe": {**PER_BANK, "panel": 60, "squared": 3, "h_ready": 3, "cmp_prob": 1, "nsa_prob": HEADS, "gla_in": 1,
           "gla_out": 1, "gla_ready": 1, "merged": KD},
    "act": {**PER_BANK, "act_step": 1, "minus_abs_z": 1, "decay_ready": 2, "edecay_used": 1, "cmp_max": 1, "nsa_max": HEADS},
    "dve": {**PER_BANK, "dve_step": 28, "log1p_ready": 1, "edecay": 3, "cmp_exp": 1, "nsa_exp": HEADS,
            "merged": KD},
}


def units(l):
    return [(half, kind, c, a) for half in ((0, 1) if l == 0 else (1,)) for kind in "mg"
            for c in range(HEADS // 2) for a in range(2)]


def build(nc, W, out, scratch, copies):
    with ExitStack() as ctx:
        k = Chip(nc, ctx)
        S, ps, area = k.sem, k.ps, k.area
        ident, ones, pair = k.col("ident"), k.col("ones"), k.col("pair")
        block = ctx.enter_context(nc.Block())

        ckv, cq = area(CKV, 2, TOK), area(CQ, 2, TOK)
        kr, kg = area(KR, TOK), area(KG, TOK)
        vg, fin = area(VG, 4, P), area(FIN, 4, TOK)
        qg, qn, qr = area(QG, 4, TOK), area(QN, 4, TOK), area(QR, 2, TOK)
        kn, vm = area(KN, 4, TOK), area(VM, 4, TOK)
        om, og = area(OM, 4, TOK), area(OG, 4, TOK)
        prob, probT = area(PROB, 2, 2, TOK), area(PROBT, 2, 4, SEQ)
        dft1 = area(DFT1, 2, 2, 2 * P)
        sqk = area(SQK, 9, TOK)
        dft_d = k.col("dft_d")
        cos_s = k.col("cos_s").rearrange("p (t s) -> p t s", t=2)
        nsin_s = k.col("nsin_s").rearrange("p (t s) -> p t s", t=2)
        y = k.xT[:, :, CTX:TOK]

        qa, kslc, kwin = area(QA, 4, SEQ), area(KSLC, SEQ), area(KWIN, SEQ)
        vslc, vwin = area(VSLC, 2, P), area(VWIN, 2, P)
        ga, dch = area(GA, 2, 3 * HEADS), area(DCH, GH, NCH)
        kcmp, vcmp, hidk = area(KCMP, NCMP), area(VCMP, 2, HD), area(HIDK, 2, 2 * NCMP)
        kbuf = [area(KBK, JP, 2, NCMP), area(KBV, JP, 2, NCMP)]
        oa, pcT = area(OA, 4, SEQ), area(PCT, 4, P)
        prob2, probT2 = area(PROB2, 2, 768), area(PROBT2, 2, 6, P)
        qb, kb, kin = area(QB, GH, SEQ), area(KB, GH, SEQ), area(KIN, GH, SEQ)
        z, t1 = area(Z, GH, SEQ), area(T1, GH, SEQ)
        vb, rb, ob = area(VB, 2, GH * DV), area(RB, KD, SEQ), area(OB, KD, SEQ)
        state = area(STATE, NCH - 1, GH, DV)
        kst, att = area(T1, 2, GH, P), area(Z, 2, GH, P)
        act2 = area(A2, FT, SEQ)
        relu = area(RELU, BANKS, TOK)
        rotated = ([("rot32", kr), ("rot64", kg)] + [("rot32", qr[:, j, :]) for j in range(2)]
                   + [("rot64", qg[:, c, :]) for c in range(4)])

        def gate(buf, g):
            j = 3 * buf + g
            return area(GATE_F + j * TOK if j < 4 else PROBT + (j - 4) * TOK, TOK)

        @block.sync
        def _(sp):
            T = Tally()

            def slot():
                s, _, n = T.panel()
                if not (isinstance(n, int) and n <= SLOTS):
                    sp.wait_ge(k.panel_begun, n - SLOTS + 1)
                return s

            def load(s, parts):
                for j, (dst, src) in enumerate(parts):
                    last = j == len(parts) - 1
                    sp.dma_start(dst, src).then_inc(
                        k.panel_landed[s], LAND - 16 * (len(parts) - 1) if last else 16)

            def at(s, off, rows, cols):
                return k.ring[s][:, off:off + rows * cols].rearrange("p (k n) -> p k n", k=rows)

            def rows(w, r0=0, n=None):
                v = w.rearrange("o (k p) n -> p (o k) n", p=P)
                return v if n is None else v[:, r0:r0 + n, :]

            vn = area(VN, 3, P)
            n_vec = 0
            for name, (t, r, n) in VEC.items():
                src = W[name]
                flat = src if len(src.shape) == 1 else src.rearrange(
                    f"{' '.join('abc'[:len(src.shape)])} -> ({' '.join('abc'[:len(src.shape)])})")
                if name in ("gqa_q_g", "gqa_k_g"):
                    for half in range(2):
                        sp.dma_start(vn[r:r + n, t, half * HD:(half + 1) * HD], src).then_inc(S["vec_in"], 16)
                    n_vec += 2
                else:
                    sp.dma_start(vn[r:r + n, t, :], flat.rearrange("(r p) -> r p", p=P)).then_inc(S["vec_in"], 16)
                    n_vec += 1
            assert n_vec == N_VEC
            sp.dma_start(k.const[:, :], W["consts"]).then_inc(S["const_in"], 16)
            xn = area(XN, 4, D)
            sp.dma_start(xn[:, 0:2, :], W["ctx"][0].rearrange("(t p) d -> p t d", p=P)).then_inc(S["tok_in"], 16)
            sp.dma_start(xn[:, 2:4, :], W["x"][0].rearrange("(t p) d -> p t d", p=P)).then_inc(S["tok_in"], 16)
            sp.dma_start(area(TABLE, HEADS)[0:BUCKETS, :], W["rel_table_2"]).then_inc(S["table_in"], 16)
            sp.dma_start(area(HOT, 512)[0:BUCKETS + 1, :], W["bucket_of_distance"]).then_inc(S["table_in"], 16)
            sp.dma_start(area(HOTC, NCMP * SEQ)[0:BUCKETS + 1, :], W["bucket_of_block"]).then_inc(S["table_in"], 16)

            def first_block(l):
                lay = slice(l, l + 1)
                w_ada, w_in = W["w_ada"][lay], W["w_in"][lay]
                first = 1 if l == 0 else 0
                for j in range(4 * first):
                    s = slot()
                    load(s, [(at(s, 0, KD, 512), rows(w_ada)[:, :, j * 512:j * 512 + 512])])
                with sp.Fori(0, 3 - first) as i, T.loop(i, 3 - first, {"panel": 4}):
                    for j in range(4):
                        s = slot()
                        n = i * 2048 + (first * 2048 + j * 512)
                        load(s, [(at(s, 0, KD, 512), rows(w_ada)[:, :, bass.ds(n, 512)])])
                s = slot()
                v = at(s, 0, KD, 512)
                load(s, [(v[:, :, 0:256], rows(w_in)[:, :, 0:256])]
                     + [(v[:, :, 256 + 32 * r:288 + 32 * r], rows(w_in)[:, :, 256:288]) for r in range(4)]
                     + [(v[:, :, 384:512], rows(w_in)[:, :, 288:416])])
                for c0, n in ((416, 384), (800, 512)):
                    s = slot()
                    load(s, [(at(s, 0, KD, n), rows(w_in)[:, :, c0:c0 + n])])
                s = slot()
                v = at(s, 0, KD, 512)
                load(s, [(v[:, :, c * P + a * HD:c * P + a * HD + HD],
                          rows(w_in)[:, :, 1312 + (4 * a + c) * HD:1312 + (4 * a + c + 1) * HD])
                         for c in range(4) for a in range(2)])
                s = slot()
                uq = W["w_uq"][lay].rearrange("o (k p) (h e) -> p (o k) h e", p=P, e=NOPE + ROPE)
                uqn = k.ring[s][:, 0:1024].rearrange("p (k h e) -> p k h e", k=2, h=HEADS)
                uqr = k.ring[s][:, 1024:1536].rearrange("p (k j a b e) -> p k j a b e", k=2, j=2, a=2, b=2)
                load(s, [(uqn[:, t], uq[:, t, :, 0:NOPE]) for t in range(2)]
                     + [(uqr[:, t, j, a], uq[:, t, 4 * j + a:4 * j + a + 3:2, NOPE:])
                        for t in range(2) for j in range(2) for a in range(2)]
                     + [(at(s, 1536, 2, 512), rows(W["w_uk"][lay])), (at(s, 2560, 2, 512), rows(W["w_uv"][lay]))])
                with sp.Fori(0, 2) as i, T.loop(i, 2, {"panel": 4}):
                    for j in range(4):
                        s = slot()
                        n = i * 512 + j * P
                        go = W["w_go"][lay].rearrange("o (a c d) n -> a d (o c) n", a=2, d=HD)
                        gov = at(s, 4096, 4, P)
                        load(s, [(at(s, 1024 * g, KD, P), rows(w_in)[:, :, bass.ds(n + GATE0 + g * D, P)])
                                 for g in range(3)]
                             + [(at(s, 3072 + 512 * g, 4, P), rows(W[w][lay])[:, :, bass.ds(n, P)])
                                for g, w in enumerate(("w_fo", "w_mo"))]
                             + [(gov[HD * a:HD * a + HD], go[a][:, :, bass.ds(n, P)]) for a in range(2)])
                for j in range(2):
                    s = slot()
                    load(s, [(at(s, 0, KD, 512), rows(W["w_o"][lay])[:, :, 512 * j:512 * j + 512])])
                with sp.Fori(0, 2) as i, T.loop(i, 2, {"panel": 4}):
                    for j in range(4):
                        s = slot()
                        load(s, [(at(s, 0, KD, 512), rows(W["w1"][lay])[:, :, bass.ds(i * 2048 + j * 512, 512)])])
                with sp.Fori(0, 2) as i, T.loop(i, 2, {"panel": 4}):
                    for j in range(4):
                        s = slot()
                        load(s, [(at(s, 0, KD, 512), rows(W["w2"][lay], KD * j, KD)[:, :, bass.ds(i * 512, 512)])])

            def ffn(l, f):
                lay = bass.ds(l, 1)
                gate, up, down = (W[f"{f}_w_{x}_2"][lay] for x in ("gate", "up", "down"))

                def pairs(c):
                    s = slot()
                    load(s, [(at(s, 0, KD, 256), rows(up)[:, :, c]), (at(s, 2048, KD, 256), rows(gate)[:, :, c])])

                with sp.Fori(0, 2) as i, T.loop(i, 2, {"panel": 4}):
                    for j in range(4):
                        pairs(bass.ds(i * 1024 + j * 256, 256))
                for j in range(8, 11):
                    pairs(slice(j * 256, j * 256 + 256))
                with sp.Fori(0, 2) as i, T.loop(i, 2, {"panel": 4}):
                    r0 = 0
                    for n in DOWN_TILES:
                        s = slot()
                        load(s, [(at(s, 0, n, 512), rows(down, r0, n)[:, :, bass.ds(i * 512, 512)])])
                        r0 += n

            def second_mixer(l):
                lay = bass.ds(l, 1)
                w_in = W["w_in_2"][lay]

                def cols(c0, n):
                    s = slot()
                    load(s, [(at(s, 0, KD, n), rows(w_in)[:, :, c0:c0 + n])])

                s = slot()
                v = at(s, 0, KD, 512)
                load(s, [(v[:, :, c * P + a * HD:c * P + a * HD + HD],
                          rows(w_in)[:, :, (4 * a + c) * HD:(4 * a + c + 1) * HD]) for c in range(4) for a in range(2)])
                s = slot()
                v = at(s, 0, KD, 512)
                load(s, [(v[:, :, g * P + r * HD:g * P + r * HD + HD],
                          rows(w_in)[:, :, 512 + g * HD:512 + g * HD + HD]) for g in range(4) for r in range(2)])
                cols(768, 512)
                s = slot()
                load(s, [(at(s, 0, KD, 24), rows(w_in)[:, :, 1280:1304]),
                         (at(s, 192, KD, 16), rows(w_in)[:, :, 3352:3368]),
                         (k.ring[s][0:16, 320:832], W["gla_a_w2_2"][lay].rearrange("o r n -> r (o n)"))])
                for x in "kv":
                    s = slot()
                    load(s, [(at(s, 0, JP, 256), rows(W[f"cmp_{x}_w1_2"][lay])),
                             (at(s, 4096, 2, HD), rows(W[f"cmp_{x}_w2_2"][lay]))])
                cols(1304, 512)
                cols(1816, 512)
                cols(2328, 512)
                cols(2840, 512)
                cols(3368, 512)
                cols(3880, 512)
                with sp.Fori(0, 2) as i, T.loop(i, 2, {"panel": 4}):
                    for j in range(4):
                        s = slot()
                        n = i * 512 + j * P
                        nsa = W["w_branch_nsa_2"][lay].rearrange("o (a c d) n -> a d (o c) n", a=2, d=HD)
                        nsav = at(s, 2048, 4, P)
                        load(s, [(at(s, 1024 * g, KD, P), rows(w_in)[:, :, bass.ds(n + 4392 + g * D, P)])
                                 for g in range(2)]
                             + [(nsav[HD * a:HD * a + HD], nsa[a][:, :, bass.ds(n, P)]) for a in range(2)]
                             + [(at(s, 2560, KD, P), rows(W["w_branch_gla_2"][lay])[:, :, bass.ds(n, P)])])
                for j in range(2):
                    s = slot()
                    load(s, [(at(s, 0, KD, 512), rows(W["w_out_2"][lay])[:, :, 512 * j:512 * j + 512])])

            for l in range(LAYERS):
                first_block(l)
                if l == 0:
                    sp.wait_ge(k.bank_read[0], 1)
                    row = k.p_cmp.rearrange("p q h n -> p (q h n)")[0:HEADS, :]
                    sp.dma_start(scratch, row).then_inc(S["row_out"], 16)
                    sp.wait_ge(S["row_out"], 16)
                    sp.dma_start(copies, scratch.unsqueeze(0).broadcast_to([P, HEADS, 512])) \
                        .then_inc(S["row_copied"], 16)
            sp.wait_ge(S["row_copied"], 16)
            sp.wait_ge(S["y_ready"], 1)
            sp.dma_start(k.bias, bass.AP(copies.tensor, P - 1, [[512 * HEADS - 1, P], [512, HEADS], [1, 2 * P]])) \
                .then_inc(S["bias_in"], 16)
            with sp.Fori(0, LAYERS) as l, T.loop(l, LAYERS, {"panel": 60}):
                ffn(l, "ffn1")
                second_mixer(l)
                ffn(l, "ffn2")
            sp.wait_ge(S["out_ready"], 4)
            sp.dma_start(out[0].rearrange("(t p) d -> p t d", p=P), area(0, 2, D)).then_inc(S["out_done"], 16)
            sp.wait_ge(S["out_done"], 16)

        @block.tensor
        def _(pe):
            T = Tally()

            def bank():
                b, n = T.take()
                if not (isinstance(n, int) and n == 1):
                    pe.wait_ge(k.bank_read[b], n - 1)
                return b

            fresh = [False]

            def panel():
                s, landed, _ = T.panel()
                pe.wait_ge(k.panel_landed[s], landed)
                fresh[0] = True
                return k.ring[s]

            def view(ring, off, rows, cols):
                return ring[:, off:off + rows * cols].rearrange("p (k n) -> p k n", k=rows)

            def products(o, pairs, start=True, stop=True):
                for j, (lhsT, rhs) in enumerate(pairs):
                    mm = pe.matmul(o, lhsT, rhs, start=start and j == 0, stop=stop and j == len(pairs) - 1,
                                   skip_group_check=True)
                    if fresh[0]:
                        mm.then_inc(k.panel_begun, 1)
                        fresh[0] = False
                return mm

            def result(n, pairs):
                b = bank()
                products(ps[:, b, 0:n], pairs).then_inc(k.bank_done[b], 1)
                return T.last()

            def flip(o, src):
                return pe.transpose(o, src, ident)

            pe.wait_ge(S["table_in"], 48)
            pe.wait_ge(S["neg_row"], T.next("neg_row"))
            table = area(TABLE, HEADS)[0:BUCKETS + 1, :]
            b = bank()
            pe.matmul(ps[0:HEADS, b, :], table, area(HOT, 512)[0:BUCKETS + 1, :], start=True, stop=True) \
                .then_inc(k.bank_done[b], 1)
            hotc = area(HOTC, NCMP, SEQ)
            b = bank()
            for q in range(2):
                for n in range(NCMP):
                    at = (q * NCMP + n) * HEADS
                    mm = pe.matmul(ps[:, b, at:at + HEADS], hotc[0:BUCKETS + 1, n, q * P:q * P + P], table,
                                   start=True, stop=True)
            mm.then_inc(k.bank_done[b], 1)
            pe.wait_ge(S["const_in"], T.next("const_in", 16))
            pe.wait_ge(S["vec_in"], T.next("vec_in", 16 * N_VEC))
            b = bank()
            for t, r in enumerate(VEC_ROWS):
                mm = pe.transpose(ps[:, b, t * P:t * P + r], area(VN, 3, P)[0:r, t, :], ident[0:r, 0:r])
            mm.then_inc(k.bank_done[b], 1)
            pe.wait_ge(S["tok_in"], T.next("tok_in", 32))
            for kt in range(KD):
                b = bank()
                for t in range(4):
                    mm = flip(ps[:, b, t * P:t * P + P], area(XN, 4, D)[:, t, kt * P:kt * P + P])
                mm.then_inc(k.bank_done[b], 1)

            def modulation():
                with pe.Fori(0, 3) as i, T.loop(i, 3, {"panel": 4, "tiles": 1}):
                    b = bank()
                    for j in range(4):
                        w = view(panel(), 0, KD, 512)
                        for m in range(4):
                            at = (4 * j + m) * 2
                            mm = products(ps[:, b, at:at + 2], [(w[:, kt, m * P:m * P + P], k.silu_c[:, kt, :])
                                                                for kt in range(KD)])
                    mm.then_inc(k.bank_done[b], 1)

            def norm(cols):
                n = cols.stop - cols.start
                result(n, [(ones, k.xT[:, kt, cols]) for kt in range(KD)])
                pe.wait_ge(S["squared"], T.next("squared"))
                sq = area(SQ, KD, TOK)
                result(n, [(ones, sq[:, kt, cols]) for kt in range(KD)])

            def project(cols):
                n = cols.stop - cols.start
                h = k.hT
                pe.wait_ge(S["h_ready"], T.next("h_ready"))
                w = view(panel(), 0, KD, 512)
                for m in range(4):
                    result(TOK, [(w[:, kt, m * P:m * P + P], h[:, kt, :]) for kt in range(KD)])
                w = view(panel(), 0, KD, 384)
                b = bank()
                for t in range(4):
                    mm = products(ps[:, b, t * P:t * P + P], [(h[:, kt, t * P:t * P + P], w[:, kt, 0:P])
                                                              for kt in range(KD)])
                mm.then_inc(k.bank_done[b], 1)
                for m in (1, 2):
                    result(n, [(w[:, kt, m * P:m * P + P], h[:, kt, cols]) for kt in range(KD)])
                for _ in range(2):
                    w = view(panel(), 0, KD, 512)
                    for m in range(4):
                        last = result(n, [(w[:, kt, m * P:m * P + P], h[:, kt, cols]) for kt in range(KD)])
                return last

            def fourier(l, qg_done):
                pe.wait_ge(*k.moved(qg_done))
                todo = [(half, g) for half in ((0, 1) if l == 0 else (1,)) for g in range(4)]
                first = []
                for u in range(len(todo) + 1):
                    if u < len(todo):
                        half, g = todo[u]
                        b = bank()
                        for t in range(2):
                            c0 = HALVES[half][0] + t * P
                            mm = products(ps[:, b, t * 2 * P:(t + 1) * 2 * P], [(fin[:, g, c0:c0 + P], dft_d)])
                        mm.then_inc(k.bank_done[b], 1)
                        first.append(T.last())
                    if u >= 1:
                        pe.wait_ge(*k.moved(first[u - 1]))
                        f = dft1[:, (u - 1) % 2]
                        result(SEQ, [(f[:, t, 0:P], cos_s[:, t, :]) for t in range(2)]
                               + [(f[:, t, P:2 * P], nsin_s[:, t, :]) for t in range(2)])

            def qk_norm(cols):
                n = cols.stop - cols.start
                pe.wait_ge(S["squared_qk"], T.next("squared_qk", 4))
                result(TOK, [(ones, sqk[:, j, :]) for j in (0, 1)])
                result(TOK, [(pair, sqk[:, 2, :])])
                result(n, [(ones, sqk[:, j, cols]) for j in (3, 4)])
                for c in range(4):
                    result(n, [(pair, sqk[:, 5 + c, cols])])

            def heads(cols):
                n = cols.stop - cols.start
                ring = panel()
                uqn, uqr, uk, uv = (view(ring, o, 2, c) for o, c in ((0, 512), (1024, 256), (1536, 512), (2560, 512)))
                pe.wait_ge(S["normed"], T.next("normed"))
                for c in range(4):
                    result(TOK, [(uk[:, t, c * P:c * P + P], ckv[:, t, :]) for t in range(2)])
                for t4 in range(4):
                    result(512, [(ckv[:, t, t4 * P:t4 * P + P], uv[:, t, :]) for t in range(2)])
                pe.wait_ge(S["normed"], T.next("normed", 2))
                for c in range(4):
                    result(n, [(uqn[:, t, c * P:c * P + P], cq[:, t, cols]) for t in range(2)])
                for j in range(2):
                    last = result(n, [(uqr[:, t, j * P:j * P + P], cq[:, t, cols]) for t in range(2)])
                return last

            def rope(qr_done):
                pe.wait_ge(S["normed"], T.next("normed"))
                pe.wait_ge(*k.moved(qr_done))
                for name, x in rotated:
                    result(SEQ, [(k.col(name), x[:, CTX:TOK])])

            def attention(l):
                todo = units(l)
                pe.wait_ge(S["roped"], T.next("roped"))
                pv = None
                turned = {}
                for u in range(len(todo) + 1):
                    if u < len(todo):
                        half, kind, c, a = todo[u]
                        keys = slice(0, HALVES[half][1])
                        for q in range(2):
                            c0 = HALVES[half][0] + q * P
                            qs = slice(c0, c0 + P)
                            at = slice(HD * a, HD * a + HD)
                            if kind == "m":
                                h = 2 * c + a
                                r0 = HD * a + ROPE * (c % 2)
                                rot = slice(r0, r0 + ROPE)
                                pairs = [(qn[at, c, qs], kn[at, c, keys]), (qr[rot, h // 4, qs], kr[rot, keys])]
                            else:
                                pairs = [(qg[at, c, qs], kg[at, keys])]
                            result(keys.stop, pairs)
                    if u >= 1:
                        half, kind, c, a = todo[u - 1]
                        tt = HALVES[half][1] // P
                        buf = (u - 1) % 2
                        pe.wait_ge(S["prob_ready"], T.next("prob_ready"))
                        for q in range(2):
                            b = bank()
                            for t in range(tt):
                                mm = flip(ps[:, b, t * P:t * P + P], prob[:, buf, q, t * P:t * P + P])
                            mm.then_inc(k.bank_done[b], 1)
                        in_turn = T.last()
                        if a == 0:
                            pv = bank()
                        pe.wait_ge(*k.moved(in_turn))
                        at = slice(HD * a, HD * a + HD)
                        h = 2 * c + a
                        mm = products(ps[at, pv, 0:SEQ],
                                      [(vm[:, t, h * HD:h * HD + HD] if kind == "m" else vg[:, t, at],
                                        probT[:, buf, t, :]) for t in range(tt)])
                        if a == 1:
                            mm.then_inc(k.bank_done[pv], 1)
                            turned = (pv, T.count[f"bank{pv}"])
                return turned

            def branches(cols, attended):
                n = cols.stop - cols.start
                pe.wait_ge(*k.moved(attended))
                with pe.Fori(0, 2) as i, T.loop(i, 2, {"panel": 4, "tiles": 24}):
                    for j in range(4):
                        ring = panel()
                        for g, x in enumerate((fin, om, og)):
                            w, wb = view(ring, 1024 * g, KD, P), view(ring, 3072 + 512 * g, 4, P)
                            result(n, [(w[:, kt, :], k.hT[:, kt, cols]) for kt in range(KD)])
                            result(n, [(wb[:, c, :], x[:, c, cols]) for c in range(4)])

            def mix_out(cols):
                n = cols.stop - cols.start
                pe.wait_ge(S["gated"], T.next("gated", KD))
                mixed = area(MIXED, KD, TOK)
                for j in range(2):
                    w = view(panel(), 0, KD, 512)
                    for m in range(4):
                        last = result(n, [(w[:, kt, m * P:m * P + P], mixed[:, kt, cols]) for kt in range(KD)])
                return last

            def mlp(cols):
                n = cols.stop - cols.start
                pe.wait_ge(S["h_ready"], T.next("h_ready"))
                with pe.Fori(0, 2) as i, T.loop(i, 2, {"panel": 4, "tiles": 16}):
                    for j in range(4):
                        w = view(panel(), 0, KD, 512)
                        for m in range(4):
                            result(n, [(w[:, kt, m * P:m * P + P], k.hT[:, kt, cols]) for kt in range(KD)])
                pe.wait_ge(*k.moved(T.last()))
                hid = area(HID, 4 * KD, n)
                with pe.Fori(0, 2) as i, T.loop(i, 2, {"panel": 4, "tiles": 4}):
                    bs = [bank() for _ in range(4)]
                    for j in range(4):
                        w = view(panel(), 0, KD, 512)
                        for m in range(4):
                            mm = products(ps[:, bs[m], 0:n], [(w[:, kt, m * P:m * P + P], hid[:, KD * j + kt, :])
                                                              for kt in range(KD)], start=j == 0, stop=j == 3)
                            if j == 3:
                                mm.then_inc(k.bank_done[bs[m]], 1)
                return T.last()

            pe.wait_ge(S["silu_c_ready"], T.next("silu_c_ready"))
            x_moved = T.last()
            for l in range(LAYERS):
                cols = slice(0 if l == 0 else CTX, TOK)
                modulation()
                if l == 0:
                    pe.wait_ge(*k.moved(x_moved))
                else:
                    pe.wait_ge(S["x_ready"], T.next("x_ready"))
                norm(slice(0, TOK))
                fourier(l, project(cols))
                qk_norm(cols)
                rope(heads(cols))
                branches(cols, attention(l))
                moved = mix_out(cols)
                pe.wait_ge(*k.moved(moved))
                norm(cols)
                pe.wait_ge(S["x_ready"], T.next("x_ready"))
                norm(cols)
                pe.wait_ge(*k.moved(mlp(cols)))
                norm(cols)

            h2 = k.h2

            def rms():
                pe.wait_ge(S["squared"], T.next("squared"))
                sq = area(SQ2, KD, SEQ)
                result(SEQ, [(ones, sq[:, kt, :]) for kt in range(KD)])

            def ffn():
                normed = T.next("h_ready")

                def pairs():
                    ring = panel()
                    for off in (0, 2048):
                        w = view(ring, off, KD, 256)
                        for m in range(2):
                            result(SEQ, [(w[:, kt, m * P:m * P + P], h2[:, kt, :]) for kt in range(KD)])

                with pe.Fori(0, 2) as i, T.loop(i, 2, {"panel": 4, "tiles": 16}):
                    pe.wait_ge(S["h_ready"], normed)
                    for j in range(4):
                        pairs()
                for j in range(8, 11):
                    pairs()
                b = (T.bank - 3) % BANKS
                multiplied = (b, T.value(f"bank{b}"))
                with pe.Fori(0, 2) as i, T.loop(i, 2, {"panel": 4, "tiles": 4}):
                    pe.wait_ge(*k.moved(multiplied))
                    bs = [bank() for _ in range(4)]
                    r0 = 0
                    for j, nk in enumerate(DOWN_TILES):
                        w = view(panel(), 0, nk, 512)
                        for m in range(4):
                            mm = products(ps[:, bs[m], 0:SEQ], [(w[:, kt, m * P:m * P + P], act2[:, r0 + kt, :])
                                                                for kt in range(nk)], start=j == 0, stop=j == 3)
                            if j == 3:
                                mm.then_inc(k.bank_done[bs[m]], 1)
                        r0 += nk

            def wide(n=4):
                w = view(panel(), 0, KD, 512)
                for m in range(n):
                    result(SEQ, [(w[:, kt, m * P:m * P + P], h2[:, kt, :]) for kt in range(KD)])
                return w

            def by_token(w, c0, n):
                b = bank()
                for t in range(2):
                    mm = products(ps[:, b, t * n:t * n + n], [(h2[:, kt, t * P:t * P + P], w[:, kt, c0:c0 + n])
                                                              for kt in range(KD)])
                mm.then_inc(k.bank_done[b], 1)
                return T.last()

            def in_projections():
                pe.wait_ge(S["h_ready"], T.next("h_ready"))
                wide()
                wide()
                b = (T.bank - 1) % BANKS
                compressed_in = T.last()
                w = view(panel(), 0, KD, 512)
                for c0, turned in ((0, False), (P, True), (2 * P, False), (3 * P, True)):
                    if turned:
                        by_token(w, c0, P)
                    else:
                        result(SEQ, [(w[:, kt, c0:c0 + P], h2[:, kt, :]) for kt in range(KD)])
                ring = panel()
                by_token(view(ring, 0, KD, 24), 0, 24)
                b = bank()
                wl = view(ring, 192, KD, 16)
                products(ps[0:16, b, 0:SEQ], [(wl[:, kt, :], h2[:, kt, :]) for kt in range(KD)]) \
                    .then_inc(k.bank_done[b], 1)
                pe.wait_ge(*k.moved(T.last()))
                for h in range(GH):
                    result(SEQ, [(ring[0:16, 320 + h * P:320 + h * P + P], area(ALR, SEQ)[0:16, :])])
                for x in range(2):
                    ring = panel()
                    w1, w2 = view(ring, 0, JP, 256), view(ring, 4096, 2, HD)
                    pe.wait_ge(*k.moved(compressed_in))
                    b = bank()
                    for m in range(2):
                        mm = products(ps[:, b, m * 2 * NCMP:(m + 1) * 2 * NCMP],
                                      [(w1[:, j, m * P:m * P + P], kbuf[x][:, j, :, :]) for j in range(JP)])
                    mm.then_inc(k.bank_done[b], 1)
                    pe.wait_ge(*k.moved(T.last()))
                    b = bank()
                    for g in range(2):
                        if x == 0:
                            mm = products(ps[HD * g:HD * g + HD, b, 0:NCMP],
                                          [(w2[:, m, :], hidk[:, m, g * NCMP:(g + 1) * NCMP]) for m in range(2)])
                        else:
                            mm = products(ps[:, b, g * HD:g * HD + HD],
                                          [(k.hid_v[:, m, g].rearrange("p r n -> p (r n)"), w2[:, m, :])
                                           for m in range(2)])
                    mm.then_inc(k.bank_done[b], 1)
                for _ in range(2):
                    wide()
                for _ in range(2):
                    w = view(panel(), 0, KD, 512)
                    for t in range(2):
                        result(512, [(h2[:, kt, t * P:t * P + P], w[:, kt, :]) for kt in range(KD)])
                for _ in range(2):
                    wide()

            def sparse_attention():
                pe.wait_ge(*k.moved(T.last()))
                for a in range(2):
                    b = bank()
                    at = slice(HD * a, HD * a + HD)
                    for q in range(2):
                        for c in range(4):
                            o = (q * 4 + c) * NCMP
                            mm = products(ps[:, b, o:o + NCMP], [(qa[at, c, q * P:q * P + P], kcmp[at, :])])
                    mm.then_inc(k.bank_done[b], 1)
                pv = turned = None
                for u in range(HEADS + 1):
                    if u < HEADS:
                        c, a = u // 2, u % 2
                        at = slice(HD * a, HD * a + HD)
                        for q in range(2):
                            n = (q + 1) * P
                            b = bank()
                            for j, key in enumerate((kslc, kwin)):
                                mm = products(ps[:, b, j * n:j * n + n],
                                              [(qa[at, c, q * P:q * P + P], key[at, 0:n])])
                            mm.then_inc(k.bank_done[b], 1)
                    if u == 0:
                        pe.wait_ge(S["cmp_prob"], T.next("cmp_prob"))
                        b = bank()
                        for q in range(2):
                            for g in range(2):
                                o = (q * 2 + g) * P
                                mm = flip(ps[:, b, o:o + P],
                                          k.p_cmp[:, q, 4 * g:4 * g + 4, :].rearrange("p h n -> p (h n)"))
                        mm.then_inc(k.bank_done[b], 1)
                    if u >= 1:
                        c, a = (u - 1) // 2, (u - 1) % 2
                        buf = (u - 1) % 2
                        at = slice(HD * a, HD * a + HD)
                        pe.wait_ge(S["nsa_prob"], T.next("nsa_prob"))
                        for blocks in (range(4), range(4, 6)):
                            b = bank()
                            for j, blk in enumerate(blocks):
                                mm = flip(ps[:, b, j * P:j * P + P], prob2[:, buf, blk * P:blk * P + P])
                            mm.then_inc(k.bank_done[b], 1)
                        in_turn = T.last()
                        if a == 0:
                            pv = bank()
                        pe.wait_ge(*k.moved(in_turn))
                        row = slice(32 * c, 32 * c + NCMP)
                        pt = probT2[:, buf]
                        products(ps[at, pv, 0:P], [(vslc[:, 0, at], pt[:, 0, :]), (vwin[:, 0, at], pt[:, 1, :]),
                                                   (vcmp[row, a, :], pcT[row, a, :])])
                        mm = products(ps[at, pv, P:2 * P],
                                      [(vslc[:, t, at], pt[:, 2 + t, :]) for t in range(2)]
                                      + [(vwin[:, t, at], pt[:, 4 + t, :]) for t in range(2)]
                                      + [(vcmp[row, a, :], pcT[row, 2 + a, :])])
                        if a == 1:
                            mm.then_inc(k.bank_done[pv], 1)
                            turned = (pv, T.value(f"bank{pv}"))
                return turned

            def linear_attention():
                pe.wait_ge(S["gla_in"], T.next("gla_in"))
                for t in range(2):
                    b = bank()
                    for h in range(GH):
                        mm = flip(ps[:, b, h * P:h * P + P], kb[:, h, t * P:t * P + P])
                    mm.then_inc(k.bank_done[b], 1)
                k_turned = T.last()
                for t in range(2):
                    b = bank()
                    for h in range(GH):
                        mm = products(ps[:, b, h * P:h * P + P], [(kin[:, h, t * P:t * P + P], qb[:, h, t * P:t * P + P])])
                    mm.then_inc(k.bank_done[b], 1)
                pe.wait_ge(*k.moved(k_turned))
                for n in range(NCH - 1):
                    rows = slice(CHUNK * (n % 2), CHUNK * (n % 2) + CHUNK)
                    for hp in range(2):
                        b = bank()
                        for j in range(2):
                            h = 2 * hp + j
                            mm = products(ps[:, b, j * DV:j * DV + DV],
                                          [(kst[rows, n // 2, h, :], vb[rows, n // 2, h * DV:h * DV + DV])])
                        mm.then_inc(k.bank_done[b], 1)
                pe.wait_ge(*k.moved(T.last()))
                for h in range(GH):
                    for v in range(2):
                        b = bank()
                        c0 = h * DV + v * P
                        for t in range(2):
                            products(ps[:, b, t * P:t * P + P], [(vb[:, t, c0:c0 + P], att[:, t, h, :])],
                                     start=t == 0, stop=False)
                        for n in range(1, NCH):
                            mm = products(ps[:, b, n * CHUNK:(n + 1) * CHUNK],
                                          [(state[:, n - 1, h, v * P:v * P + P], qb[:, h, n * CHUNK:(n + 1) * CHUNK])],
                                          start=False, stop=n == NCH - 1)
                        mm.then_inc(k.bank_done[b], 1)
                pe.wait_ge(S["gla_out"], T.next("gla_out"))
                sq = area(SQO, KD, SEQ)
                for hp in range(2):
                    b = bank()
                    for j in range(2):
                        h = 2 * hp + j
                        mm = products(ps[:, b, j * SEQ:j * SEQ + SEQ], [(ones, sq[:, 2 * h + v, :]) for v in range(2)])
                    mm.then_inc(k.bank_done[b], 1)

            def merge(nsa_done):
                gla_done = T.next("gla_ready")
                with pe.Fori(0, 2) as i, T.loop(i, 2, {"panel": 4, "tiles": 16}):
                    pe.wait_ge(*k.moved(nsa_done))
                    pe.wait_ge(S["gla_ready"], gla_done)
                    for j in range(4):
                        ring = panel()
                        wn, wg = view(ring, 2048, 4, P), view(ring, 2560, KD, P)
                        result(SEQ, [(wn[:, c, :], oa[:, c, :]) for c in range(4)])
                        result(SEQ, [(wg[:, kt, :], ob[:, kt, :]) for kt in range(KD)])
                        for g in range(2):
                            w = view(ring, 1024 * g, KD, P)
                            result(SEQ, [(w[:, kt, :], h2[:, kt, :]) for kt in range(KD)])
                pe.wait_ge(S["merged"], T.next("merged", KD))
                mixed = area(MIXED2, KD, SEQ)
                for j in range(2):
                    w = view(panel(), 0, KD, 512)
                    for m in range(4):
                        result(SEQ, [(w[:, kt, m * P:m * P + P], mixed[:, kt, :]) for kt in range(KD)])

            with pe.Fori(0, LAYERS) as l, T.loop(l, LAYERS, PER_LAYER["pe"]):
                rms()
                ffn()
                rms()
                in_projections()
                nsa_done = sparse_attention()
                linear_attention()
                merge(nsa_done)
                rms()
                ffn()
            rms()
            pe.wait_ge(S["h_ready"], T.next("h_ready"))
            for t in range(2):
                for g in range(2):
                    b = bank()
                    for j in range(4):
                        mm = flip(ps[:, b, j * P:j * P + P], h2[:, 4 * g + j, t * P:t * P + P])
                    mm.then_inc(k.bank_done[b], 1)

        @block.scalar
        def _(act):
            T = Tally()

            def skip(n):
                for _ in range(n):
                    T.take()
                return T.last()

            eps, one = k.col("eps"), k.col("one")

            skip(2)
            act.wait_ge(*k.moved(skip(1)))
            for s, name in enumerate(("c_ctx", "c")):
                t, r, n = VEC[name]
                ins = act.activation(k.silu_c[:, :, s], k.vecT[:, t * P + r:t * P + r + n], ACT.Silu)
            ins.then_inc(S["silu_c_ready"], 1)
            skip(KD)

            def norm(centred, cols):
                n = cols.stop - cols.start
                skip(1)
                act.wait_ge(S["centred"], T.next("centred"))
                act.activation(area(SQ, KD, TOK)[:, :, cols], centred[:, :, cols], ACT.Square) \
                    .then_inc(S["squared"], 1)
                b, v = T.take()
                act.wait_ge(k.bank_done[b], v)
                act.activation(area(STD, TOK)[:, cols], ps[:, b, 0:n],
                               ACT.Sqrt, scale=1.0 / D, bias=eps).then_inc(k.bank_read[b], 1)

            def project(cols):
                n = cols.stop - cols.start

                def square(o, src, result):
                    act.wait_ge(*k.moved(result))
                    act.activation(o, src, ACT.Square).then_inc(S["squared_qk"], 1)

                for m in range(2):
                    b, v = T.take()
                    act.wait_ge(k.bank_done[b], v)
                    act.activation(ckv[:, m, :], ps[:, b, 0:TOK], ACT.Copy).then_inc(k.bank_read[b], 1)
                    last = T.last()
                square(sqk[:, 0:2, :], ckv, last)
                b, v = T.take()
                act.wait_ge(k.bank_done[b], v)
                act.activation(kr, ps[:, b, 0:TOK], ACT.Copy).then_inc(k.bank_read[b], 1)
                b, v = T.take()
                act.wait_ge(k.bank_done[b], v)
                act.activation(kg, ps[:, b, 0:TOK], ACT.Copy).then_inc(k.bank_read[b], 1)
                square(sqk[:, 2, :], kg, T.last())
                b, v = T.take()
                act.wait_ge(k.bank_done[b], v)
                act.activation(vg, ps[:, b, :].rearrange("p (t c) -> p t c", t=4),
                               ACT.Copy).then_inc(k.bank_read[b], 1)
                for m in range(4):
                    b, v = T.take()
                    act.wait_ge(k.bank_done[b], v)
                    act.activation(fin[:, m, cols], ps[:, b, 0:n], ACT.Copy).then_inc(k.bank_read[b], 1)
                for m in range(2):
                    b, v = T.take()
                    act.wait_ge(k.bank_done[b], v)
                    act.activation(cq[:, m, cols], ps[:, b, 0:n], ACT.Copy).then_inc(k.bank_read[b], 1)
                    last = T.last()
                square(sqk[:, 3:5, cols], cq[:, :, cols], last)
                for m in range(4):
                    b, v = T.take()
                    act.wait_ge(k.bank_done[b], v)
                    act.activation(qg[:, m, cols], ps[:, b, 0:n], ACT.Copy).then_inc(k.bank_read[b], 1)
                    last = T.last()
                square(sqk[:, 5:9, cols], qg[:, :, cols], last)

            def fourier(l):
                todo = [(half, g) for half in ((0, 1) if l == 0 else (1,)) for g in range(4)]
                for u in range(len(todo) + 1):
                    if u < len(todo):
                        skip(1)
                    if u >= 1:
                        half, g = todo[u - 1]
                        b, v = T.take()
                        act.wait_ge(k.bank_done[b], v)
                        act.activation(fin[:, g, slice(*HALVES[half])], ps[:, b, 0:SEQ],
                                       ACT.Copy).then_inc(k.bank_read[b], 1)

            def qk_norm(cols):
                n = cols.stop - cols.start
                b, v = T.take()
                act.wait_ge(k.bank_done[b], v)
                act.activation(sqk[:, 0, :], ps[:, b, 0:TOK],
                               ACT.Sqrt, scale=1.0 / RANK, bias=eps).then_inc(k.bank_read[b], 1)
                b, v = T.take()
                act.wait_ge(k.bank_done[b], v)
                act.activation(sqk[:, 2, :], ps[:, b, 0:TOK],
                               ACT.Sqrt, scale=1.0 / HD, bias=eps).then_inc(k.bank_read[b], 1)
                b, v = T.take()
                act.wait_ge(k.bank_done[b], v)
                act.activation(sqk[:, 3, cols], ps[:, b, 0:n],
                               ACT.Sqrt, scale=1.0 / RANK, bias=eps).then_inc(k.bank_read[b], 1)
                for c in range(4):
                    b, v = T.take()
                    act.wait_ge(k.bank_done[b], v)
                    act.activation(sqk[:, 5 + c, cols], ps[:, b, 0:n],
                                   ACT.Sqrt, scale=1.0 / HD, bias=eps).then_inc(k.bank_read[b], 1)

            def heads(cols):
                n = cols.stop - cols.start
                for c in range(4):
                    b, v = T.take()
                    act.wait_ge(k.bank_done[b], v)
                    act.activation(kn[:, c, :], ps[:, b, 0:TOK], ACT.Copy).then_inc(k.bank_read[b], 1)
                for t in range(4):
                    b, v = T.take()
                    act.wait_ge(k.bank_done[b], v)
                    act.activation(vm[:, t, :], ps[:, b, 0:512], ACT.Copy).then_inc(k.bank_read[b], 1)
                for c in range(4):
                    b, v = T.take()
                    act.wait_ge(k.bank_done[b], v)
                    act.activation(qn[:, c, cols], ps[:, b, 0:n], ACT.Copy).then_inc(k.bank_read[b], 1)
                for j in range(2):
                    b, v = T.take()
                    act.wait_ge(k.bank_done[b], v)
                    act.activation(qr[:, j, cols], ps[:, b, 0:n], ACT.Copy).then_inc(k.bank_read[b], 1)
                skip(len(rotated))

            def attention(l):
                todo = units(l)
                score, turn = {}, {}
                for u in range(len(todo) + 1):
                    if u < len(todo):
                        half, kind, c, a = todo[u]
                        buf = u % 2
                        n = HALVES[half][1]
                        tiles = [T.take() for _ in range(2)]
                        act.wait_ge(S["row_max"], T.next("row_max"))
                        for q, (b, v) in enumerate(tiles):
                            act.wait_ge(k.bank_done[b], v)
                            act.activation(prob[:, buf, q, 0:n], ps[:, b, 0:n], ACT.Exp,
                                           bias=k.stat[:, 8 * buf + q:8 * buf + q + 1],
                                           scale=MLA_SCALE if kind == "m" else GQA_SCALE,
                                           accum_out=k.stat[:, 8 * buf + 2 + q:8 * buf + 3 + q]) \
                                .then_inc(k.bank_read[b], 1)
                    if u >= 1:
                        half, kind, c, a = todo[u - 1]
                        tt = HALVES[half][1] // P
                        for q in range(2):
                            b, v = T.take()
                            act.wait_ge(k.bank_done[b], v)
                            act.activation(probT[:, (u - 1) % 2, 0:tt, q * P:q * P + P], ps[:, b, 0:tt * P].rearrange("p (t c) -> p t c", t=tt),
                                           ACT.Copy).then_inc(k.bank_read[b], 1)
                        if a == 0:
                            skip(1)

            def branches(l, cols):
                n = cols.stop - cols.start
                t, r, _ = VEC["b_gate"]
                bias = k.stat[:, 48:60].rearrange("p (g m) -> p g m", g=3)
                every = k.vecT[:, t * P + r + l * 3 * KD:t * P + r + (l + 1) * 3 * KD].rearrange(
                    "p (g m) -> p g m", g=3)
                with act.Fori(0, 2) as i, T.loop(i, 2, {"tiles": 24, "act_step": 1}):
                    act.activation(bias, every[:, :, bass.ds(i * 4, 4)], ACT.Copy).then_inc(S["act_step"], 1)
                    act.wait_ge(S["act_step"], T.next("act_step"))
                    for j in range(4):
                        for g in range(3):
                            b, v = T.take()
                            act.wait_ge(k.bank_done[b], v)
                            act.activation(gate(j % 2, g)[:, cols], ps[:, b, 0:n],
                                           ACT.Sigmoid, bias=bias[:, g, j:j + 1]).then_inc(k.bank_read[b], 1)
                            last = T.last()
                            skip(1)
                    act.wait_ge(*k.moved(last))

            def mlp(cols):
                n = cols.stop - cols.start
                with act.Fori(0, 2) as i, T.loop(i, 2, {"tiles": 16}):
                    for j in range(4):
                        for m in range(4):
                            b, v = T.take()
                            act.wait_ge(k.bank_done[b], v)
                            act.activation(relu[:, 4 * (j % 2) + m, 0:n], ps[:, b, 0:n], ACT.Relu) \
                                .then_inc(S["relu_ready"], 1)
                with act.Fori(0, 2) as i, T.loop(i, 2, {"tiles": 4}):
                    skip(4)

            for l in range(LAYERS):
                cols = slice(0 if l == 0 else CTX, TOK)
                with act.Fori(0, 3) as i, T.loop(i, 3, {"tiles": 1}):
                    skip(1)
                norm(k.hT, slice(0, TOK))
                project(cols)
                fourier(l)
                qk_norm(cols)
                heads(cols)
                attention(l)
                branches(l, cols)
                skip(KD)
                norm(k.xT, cols)
                norm(k.hT, cols)
                mlp(cols)
                norm(k.xT, cols)

            def rms():
                act.activation(area(SQ2, KD, SEQ), y, ACT.Square).then_inc(S["squared"], 1)
                b, v = T.take()
                act.wait_ge(k.bank_done[b], v)
                act.activation(area(STD2, SEQ), ps[:, b, 0:SEQ],
                               ACT.Sqrt, scale=1.0 / D, bias=eps).then_inc(k.bank_read[b], 1)

            def ffn():
                def pairs(j):
                    skip(2)
                    for m in range(2):
                        b, v = T.take()
                        act.wait_ge(k.bank_done[b], v)
                        act.activation(area(SILU2, 2, 2, SEQ)[:, j % 2, m, :], ps[:, b, 0:SEQ],
                                       ACT.Silu).then_inc(k.bank_read[b], 1)

                with act.Fori(0, 2) as i, T.loop(i, 2, {"tiles": 16}):
                    for j in range(4):
                        pairs(j)
                for j in range(8, 11):
                    pairs(j)
                with act.Fori(0, 2) as i, T.loop(i, 2, {"tiles": 4}):
                    skip(4)

            def in_projections():
                for m in range(4):
                    b, v = T.take()
                    act.wait_ge(k.bank_done[b], v)
                    act.activation(qa[:, m, :], ps[:, b, 0:SEQ],
                                   ACT.Copy, scale=HD ** -0.5).then_inc(k.bank_read[b], 1)
                skip(4)
                two = lambda b: ps[:, b, 0:2 * P].rearrange("p (t c) -> p t c", t=2)
                b, v = T.take()
                act.wait_ge(k.bank_done[b], v)
                act.activation(kslc, ps[:, b, 0:SEQ], ACT.Copy).then_inc(k.bank_read[b], 1)
                b, v = T.take()
                act.wait_ge(k.bank_done[b], v)
                act.activation(vslc, two(b), ACT.Copy).then_inc(k.bank_read[b], 1)
                b, v = T.take()
                act.wait_ge(k.bank_done[b], v)
                act.activation(kwin, ps[:, b, 0:SEQ], ACT.Copy).then_inc(k.bank_read[b], 1)
                b, v = T.take()
                act.wait_ge(k.bank_done[b], v)
                act.activation(vwin, two(b), ACT.Copy).then_inc(k.bank_read[b], 1)
                b, v = T.take()
                act.wait_ge(k.bank_done[b], v)
                act.activation(ga, ps[:, b, 0:48].rearrange("p (t c) -> p t c", t=2),
                               ACT.Sigmoid).then_inc(k.bank_read[b], 1)
                b, v = T.take()
                act.wait_ge(k.bank_done[b], v)
                act.activation(area(ALR, SEQ)[0:16, :], ps[0:16, b, 0:SEQ], ACT.Copy).then_inc(k.bank_read[b], 1)
                skip(GH)
                b, v = T.take()
                act.wait_ge(k.bank_done[b], v)
                act.activation(hidk, ps[:, b, 0:4 * NCMP].rearrange("p (m n) -> p m n", m=2),
                               ACT.Silu).then_inc(k.bank_read[b], 1)
                b, v = T.take()
                act.wait_ge(k.bank_done[b], v)
                act.activation(kcmp, ps[:, b, 0:NCMP], ACT.Copy).then_inc(k.bank_read[b], 1)
                b, v = T.take()
                act.wait_ge(k.bank_done[b], v)
                for m in range(2):
                    src = ps[:, b, m * 2 * NCMP:(m + 1) * 2 * NCMP].rearrange("p (g n) -> p g n", g=2)
                    ins = act.activation(k.hid_v[:, m, :, :, 0:NCMP],
                                         src.unsqueeze(2).broadcast_to([P, 2, 4, NCMP]), ACT.Silu)
                ins.then_inc(k.bank_read[b], 1)
                b, v = T.take()
                act.wait_ge(k.bank_done[b], v)
                act.activation(vcmp, ps[:, b, 0:2 * HD].rearrange("p (g c) -> p g c", g=2),
                               ACT.Copy).then_inc(k.bank_read[b], 1)
                act.wait_ge(S["minus_abs_z"], T.next("minus_abs_z"))
                act.activation(t1, t1, ACT.Exp).then_inc(S["act_step"], 1)
                act.wait_ge(S["act_step"], T.next("act_step"))
                act.activation(t1, t1, ACT.Ln, bias=one).then_inc(S["log1p_ready"], 1)
                for m in range(4):
                    b, v = T.take()
                    act.wait_ge(k.bank_done[b], v)
                    act.activation(qb[:, m, :], ps[:, b, 0:SEQ],
                                   ACT.Copy, scale=P ** -0.5).then_inc(k.bank_read[b], 1)
                for m in range(4):
                    b, v = T.take()
                    act.wait_ge(k.bank_done[b], v)
                    act.activation(kb[:, m, :], ps[:, b, 0:SEQ], ACT.Copy).then_inc(k.bank_read[b], 1)
                act.wait_ge(S["decay_ready"], T.next("decay_ready"))
                act.activation(z, t1, ACT.Exp, scale=1.0 / TAU).then_inc(S["edecay"], 1)
                for half in range(2):
                    for t in range(2):
                        b, v = T.take()
                        act.wait_ge(k.bank_done[b], v)
                        act.activation(vb[:, t, half * 512:half * 512 + 512], ps[:, b, 0:512],
                                       ACT.Copy).then_inc(k.bank_read[b], 1)
                act.wait_ge(S["edecay_used"], T.next("edecay_used"))
                act.activation(z, t1, ACT.Exp, scale=-1.0 / TAU).then_inc(S["edecay"], 1)
                for m in range(4):
                    b, v = T.take()
                    act.wait_ge(k.bank_done[b], v)
                    act.activation(rb[:, m, :], ps[:, b, 0:SEQ], ACT.Silu).then_inc(k.bank_read[b], 1)
                act.wait_ge(S["decay_ready"], T.next("decay_ready"))
                act.activation(z, z, ACT.Exp, scale=1.0 / TAU).then_inc(S["edecay"], 1)
                for m in range(4, KD):
                    b, v = T.take()
                    act.wait_ge(k.bank_done[b], v)
                    act.activation(rb[:, m, :], ps[:, b, 0:SEQ], ACT.Silu).then_inc(k.bank_read[b], 1)

            def sparse_attention():
                skip(2)
                act.wait_ge(S["cmp_max"], T.next("cmp_max"))
                pc = k.p_cmp[:, :, :, 0:NCMP]
                act.activation(pc, pc, ACT.Exp).then_inc(S["cmp_exp"], 1)
                for u in range(HEADS + 1):
                    if u < HEADS:
                        skip(2)
                        buf = u % 2
                        act.wait_ge(S["nsa_max"], T.next("nsa_max"))
                        for j in range(4):
                            n = P if j < 2 else 2 * P
                            o = j * P if j < 2 else 2 * P + (j - 2) * 2 * P
                            p = prob2[:, buf, o:o + n]
                            ins = act.activation(p, p, ACT.Exp, bias=k.stat[:, 16 * buf + j:16 * buf + j + 1],
                                                 accum_out=k.stat[:, 16 * buf + 4 + j:16 * buf + 5 + j])
                        ins.then_inc(S["nsa_exp"], 1)
                    if u == 0:
                        b, v = T.take()
                        act.wait_ge(k.bank_done[b], v)
                        act.activation(pcT, ps[:, b, :].rearrange("p (t c) -> p t c", t=4),
                                       ACT.Copy).then_inc(k.bank_read[b], 1)
                    if u >= 1:
                        for b0, n in ((0, 4), (4, 2)):
                            b, v = T.take()
                            act.wait_ge(k.bank_done[b], v)
                            act.activation(probT2[:, (u - 1) % 2, b0:b0 + n, :], ps[:, b, 0:n * P].rearrange("p (t c) -> p t c", t=n),
                                           ACT.Copy).then_inc(k.bank_read[b], 1)
                        if u % 2 == 1:
                            skip(1)

            def linear_attention():
                for t in range(2):
                    b, v = T.take()
                    act.wait_ge(k.bank_done[b], v)
                    act.activation(kst[:, t], ps[:, b, :].rearrange("p (t c) -> p t c", t=4),
                                   ACT.Copy).then_inc(k.bank_read[b], 1)
                skip(2 + 2 * (NCH - 1))
                for j in range(KD):
                    b, v = T.take()
                    act.wait_ge(k.bank_done[b], v)
                    act.activation(ob[:, j, :], ps[:, b, 0:SEQ], ACT.Copy).then_inc(k.bank_read[b], 1)
                    last = T.last()
                act.wait_ge(*k.moved(last))
                act.activation(area(SQO, KD, SEQ), ob, ACT.Square).then_inc(S["gla_out"], 1)
                for hp in range(2):
                    b, v = T.take()
                    act.wait_ge(k.bank_done[b], v)
                    act.activation(t1[:, 2 * hp:2 * hp + 2, :], ps[:, b, :].rearrange("p (h c) -> p h c", h=2),
                                   ACT.Sqrt, scale=1.0 / DV, bias=eps).then_inc(k.bank_read[b], 1)

            def merge():
                with act.Fori(0, 2) as i, T.loop(i, 2, {"tiles": 16}):
                    for j in range(4):
                        skip(2)
                        for g in range(2):
                            b, v = T.take()
                            act.wait_ge(k.bank_done[b], v)
                            act.activation(area(MGATE, 2, 2, SEQ)[:, j % 2, g, :], ps[:, b, 0:SEQ],
                                           ACT.Sigmoid).then_inc(k.bank_read[b], 1)
                skip(KD)

            act.wait_ge(S["y_ready"], T.next("y_ready"))
            with act.Fori(0, LAYERS) as l, T.loop(l, LAYERS, PER_LAYER["act"]):
                act.wait_ge(k.bank_read[LAST_DOWN], T.value(f"bank{LAST_DOWN}"))
                rms()
                ffn()
                act.wait_ge(*k.moved(T.last()))
                rms()
                in_projections()
                sparse_attention()
                linear_attention()
                merge()
                act.wait_ge(*k.moved(T.last()))
                rms()
                ffn()
                assert T.last()[0] == LAST_DOWN, T.last()
            act.wait_ge(*k.moved(T.last()))
            rms()
            outT = area(0, 2, D)
            for t in range(2):
                for g in range(2):
                    b, v = T.take()
                    act.wait_ge(k.bank_done[b], v)
                    act.activation(outT[:, t, g * 512:g * 512 + 512], ps[:, b, :], ACT.Copy) \
                        .then_inc(S["out_ready"], 1)

        @block.vector
        def _(dve):
            T = Tally()

            def skip(n):
                for _ in range(n):
                    T.take()
                return T.last()

            def over(v, dims):
                return v.broadcast_to(dims)

            dve.memset(area(TABLE, HEADS)[BUCKETS:BUCKETS + 1, :], NEG).then_inc(S["neg_row"], 1)
            b, v = T.take()
            dve.wait_ge(k.bank_done[b], v)
            row = k.p_cmp.rearrange("p q h n -> p (q h n)")[0:HEADS, :]
            dve.tensor_copy(row, ps[0:HEADS, b, :]).then_inc(k.bank_read[b], 1)
            b, v = T.take()
            dve.wait_ge(k.bank_done[b], v)
            dve.tensor_copy(k.cmp_bias, ps[:, b, 0:2 * NCMP * HEADS].rearrange(
           "p (q n h) -> p q h n", q=2, n=NCMP)) \
                .then_inc(k.bank_read[b], 1)
            b, v = T.take()
            dve.wait_ge(k.bank_done[b], v)
            for t, r in enumerate(VEC_ROWS):
                ins = dve.tensor_copy(k.vecT[:, t * P:t * P + r], ps[:, b, t * P:t * P + r])
            ins.then_inc(k.bank_read[b], 1)
            for kt in range(KD):
                b, v = T.take()
                dve.wait_ge(k.bank_done[b], v)
                dve.tensor_copy(k.xT[:, kt, :], ps[:, b, :]).then_inc(k.bank_read[b], 1)
            dve.wait_ge(*k.moved(T.last()))

            def modulation(l):
                t, r, _ = VEC["b_ada"]
                with dve.Fori(0, 3) as i, T.loop(i, 3, {"tiles": 1}):
                    b, v = T.take()
                    dve.wait_ge(k.bank_done[b], v)
                    bias = k.vecT[:, bass.ds(i * 16 + (t * P + r + l * MODS), 16)]
                    dve.tensor_tensor(k.mods[:, bass.ds(i * 16, 16), :],
                                      ps[:, b, 0:32].rearrange("p (m s) -> p m s", s=2),
                                      over(bias.unsqueeze(2), [P, 16, 2]), ALU.add) \
                        .then_inc(k.bank_read[b], 1)
                dve.wait_ge(*k.moved(T.last()))
                for sc in (SC1, SC2):
                    ins = dve.tensor_scalar(k.mods[:, sc:sc + KD, :], k.mods[:, sc:sc + KD, :], 1.0, None, ALU.add)
                ins.then_inc(S["dve_step"], 1)
                dve.wait_ge(S["dve_step"], T.next("dve_step"))

            def norm(dst, cols, affine, ready):
                n = cols.stop - cols.start
                mean, std = area(MEAN, TOK)[:, cols], area(STD, TOK)[:, cols]
                wide = [P, KD, n]
                b, v = T.take()
                dve.wait_ge(k.bank_done[b], v)
                dve.tensor_scalar(mean, ps[:, b, 0:n], 1.0 / D, None, ALU.mult).then_inc(k.bank_read[b], 1)
                dve.wait_ge(*k.moved(T.last()))
                d = dst[:, :, cols]
                dve.tensor_tensor(d, k.xT[:, :, cols], over(mean.unsqueeze(1), wide), ALU.subtract) \
                    .then_inc(S["centred"], 1)
                dve.wait_ge(*k.moved(skip(1)))
                dve.reciprocal(std, std).then_inc(S["dve_step"], 1)
                dve.wait_ge(S["dve_step"], T.next("dve_step"))
                dve.tensor_tensor(d, d, over(std.unsqueeze(1), wide), ALU.mult).then_inc(S["dve_step"], 1)
                dve.wait_ge(S["dve_step"], T.next("dve_step"))
                for kt in range(KD):
                    for part, scale, shift in affine(kt):
                        o = dst[:, kt, part]
                        ins = dve.tensor_scalar(o, o, scale, shift, ALU.mult, ALU.add)
                ins.then_inc(S[ready], 1)
                if ready != "h_ready":
                    dve.wait_ge(S[ready], T.next(ready))

            def modulated(sc, sh, halves):
                return lambda kt: [(slice(*HALVES[s]), k.mods[:, sc + kt, s:s + 1], k.mods[:, sh + kt, s:s + 1])
                                   for s in halves]

            def gained(name, l, cols):
                return lambda kt: [(cols, k.vec(f"{name}_g", l * KD + kt), k.vec(f"{name}_b", l * KD + kt))]

            def fourier(l):
                todo = 8 if l == 0 else 4
                for u in range(todo + 1):
                    if u < todo:
                        b, v = T.take()
                        dve.wait_ge(k.bank_done[b], v)
                        dve.tensor_copy(dft1[:, u % 2], ps[:, b, :].rearrange("p (t c) -> p t c", t=2)) \
                            .then_inc(k.bank_read[b], 1)
                    if u >= 1:
                        skip(1)

            def qk_norm(l, cols):
                for x, std, name, col, tiles, cs in (
                        (ckv, 0, "mla_kv_g", 2 * l, 2, slice(0, TOK)), (kg.unsqueeze(1), 2, "gqa_k_g", l, 1, slice(0, TOK)),
                        (cq, 3, "mla_q_g", 2 * l, 2, cols)):
                    dve.wait_ge(*k.moved(skip(1)))
                    r = sqk[:, std, cs]
                    dve.reciprocal(r, r).then_inc(S["dve_step"], 1)
                    dve.wait_ge(S["dve_step"], T.next("dve_step"))
                    for j in range(tiles):
                        ins = dve.scalar_tensor_tensor(x[:, j, cs], x[:, j, cs], k.vec(name, col + j), r,
                                                       ALU.mult, ALU.mult)
                    ins.then_inc(S["normed"], 1)
                dve.wait_ge(*k.moved(skip(4)))
                r = sqk[:, 5:9, cols]
                dve.reciprocal(r, r).then_inc(S["dve_step"], 1)
                dve.wait_ge(S["dve_step"], T.next("dve_step"))
                x = qg[:, :, cols]
                ins = dve.scalar_tensor_tensor(x, x, k.vec("gqa_q_g", l), r, ALU.mult, ALU.mult)
                ins.then_inc(S["normed"], 1)
                dve.wait_ge(S["normed"], T.next("normed", 4))

            def rope():
                skip(4 + 4 + 4 + 2)
                todo = rotated
                for j, (name, x) in enumerate(todo):
                    b, v = T.take()
                    dve.wait_ge(k.bank_done[b], v)
                    sin, cos = k.col(name.replace("rot", "sin")), k.col(name.replace("rot", "cos"))
                    dve.tensor_tensor(area(ROT + j * SEQ, SEQ), ps[:, b, 0:SEQ], sin, ALU.mult) \
                        .then_inc(k.bank_read[b], 1)
                    ins = dve.tensor_tensor(x[:, CTX:TOK], x[:, CTX:TOK], cos, ALU.mult)
                ins.then_inc(S["dve_step"], 1)
                dve.wait_ge(S["dve_step"], T.next("dve_step"))
                for j, (name, x) in enumerate(todo):
                    ins = dve.tensor_tensor(x[:, CTX:TOK], x[:, CTX:TOK], area(ROT + j * SEQ, SEQ), ALU.add)
                ins.then_inc(S["roped"], 1)

            def attention(l):
                todo = units(l)
                score, out_of = {}, {}

                def moved(u):
                    half, kind, c, a = todo[u]
                    b, n = out_of[u // 2]
                    dve.wait_ge(k.bank_done[b], n)
                    o = om if kind == "m" else og
                    dve.tensor_copy(o[:, c, slice(*HALVES[half])], ps[:, b, 0:SEQ]).then_inc(k.bank_read[b], 1)

                for u in range(len(todo) + 1):
                    if u < len(todo):
                        half, kind, c, a = todo[u]
                        buf, n = u % 2, HALVES[half][1]
                        tiles = [T.take() for _ in range(2)]
                        score[u] = tiles
                        nmax = k.stat[:, 8 * buf:8 * buf + 2]
                        for q, (b, v) in enumerate(tiles):
                            dve.wait_ge(k.bank_done[b], v)
                            ins = dve.tensor_reduce(nmax[:, q:q + 1], ps[:, b, 0:n], AX, ALU.max, negate=True)
                        ins.then_inc(S["dve_step"], 1)
                        dve.wait_ge(S["dve_step"], T.next("dve_step"))
                        scale = MLA_SCALE if kind == "m" else GQA_SCALE
                        dve.tensor_scalar(nmax, nmax, scale, None, ALU.mult).then_inc(S["row_max"], 1)
                    if u >= 3 and u % 2 == 1:
                        moved(u - 2)
                    if u >= 1:
                        half, kind, c, a = todo[u - 1]
                        buf, n = (u - 1) % 2, HALVES[half][1]
                        dve.wait_ge(*k.moved(score[u - 1][1]))
                        rsum = k.stat[:, 8 * buf + 2:8 * buf + 4]
                        dve.reciprocal(rsum, rsum).then_inc(S["dve_step"], 1)
                        dve.wait_ge(S["dve_step"], T.next("dve_step"))
                        for q in range(2):
                            p = prob[:, buf, q, 0:n]
                            ins = dve.tensor_scalar(p, p, rsum[:, q:q + 1], None, ALU.mult)
                        ins.then_inc(S["prob_ready"], 1)
                        skip(2)
                        if a == 0:
                            out_of[(u - 1) // 2] = T.take()
                moved(len(todo) - 1)

            def branches(l, cols):
                n = cols.stop - cols.start
                mixed = area(MIXED, KD, TOK)
                x = k.xT[:, :, cols]
                dve.tensor_scalar(x, x, ALPHA, None, ALU.mult)
                tm, tg = area(TMP_M, TOK)[:, cols], area(TMP_G, TOK)[:, cols]
                with dve.Fori(0, 2) as i, T.loop(i, 2, {"tiles": 24, "dve_step": 4, "gated": 4}):
                    for j in range(4):
                        m = mixed[:, bass.ds(i * 4 + j, 1), cols].rearrange("p o n -> p (o n)")
                        for g, o in enumerate((m, tm, tg)):
                            dve.wait_ge(*k.moved(skip(1)))
                            b, v = T.take()
                            dve.wait_ge(k.bank_done[b], v)
                            dve.tensor_tensor(o, gate(j % 2, g)[:, cols], ps[:, b, 0:n], ALU.mult) \
                                .then_inc(k.bank_read[b], 1)
                        dve.wait_ge(*k.moved(T.last()))
                        dve.tensor_tensor(m, m, tm, ALU.add).then_inc(S["dve_step"], 1)
                        dve.wait_ge(S["dve_step"], T.next("dve_step"))
                        dve.tensor_tensor(m, m, tg, ALU.add).then_inc(S["gated"], 1)
                        dve.wait_ge(S["gated"], T.next("gated"))

            def residual(tile, b, cols, halves, g):
                for s in halves:
                    c0, c1 = HALVES[s]
                    x = k.xT[:, tile, c0:c1]
                    if not isinstance(tile, int):
                        x = x.rearrange("p o n -> p (o n)")
                        gate_col = k.mods[:, bass.ds(tile.start + g, 1), s]
                    else:
                        gate_col = k.mods[:, g + tile, s:s + 1]
                    src = ps[:, b, c0 - cols.start:c1 - cols.start]
                    ins = dve.scalar_tensor_tensor(x, src, gate_col, x, ALU.mult, ALU.add)
                return ins

            for l in range(LAYERS):
                cols = slice(0 if l == 0 else CTX, TOK)
                halves = (0, 1) if l == 0 else (1,)
                modulation(l)
                norm(k.hT, slice(0, TOK), modulated(SC1, SH1, (0, 1)), "h_ready")
                skip(4 + 1 + 2 + 4 + 4)
                fourier(l)
                qk_norm(l, cols)
                rope()
                attention(l)
                branches(l, cols)
                for m in range(KD):
                    b, v = T.take()
                    dve.wait_ge(k.bank_done[b], v)
                    residual(m, b, cols, halves, G1).then_inc(k.bank_read[b], 1)
                dve.wait_ge(*k.moved(T.last()))
                norm(k.xT, cols, gained("ln1", l, cols), "x_ready")
                norm(k.hT, cols, modulated(SC2, SH2, halves), "h_ready")
                x = k.xT[:, :, cols]
                dve.tensor_scalar(x, x, ALPHA, None, ALU.mult).then_inc(S["dve_step"], 1)
                dve.wait_ge(S["dve_step"], T.next("dve_step"))
                hid = area(HID, 4 * KD, cols.stop - cols.start)
                with dve.Fori(0, 2) as i, T.loop(i, 2, {"tiles": 16, "relu_ready": 16}):
                    for j in range(16):
                        b, _ = T.take()
                        dve.wait_ge(S["relu_ready"], T.next("relu_ready"))
                        dve.tensor_tensor(hid[:, bass.ds(i * 16 + j, 1), :].rearrange("p o n -> p (o n)"),
                                          relu[:, j % 8, 0:cols.stop - cols.start],
                                          ps[:, b, 0:cols.stop - cols.start], ALU.mult) \
                            .then_inc(k.bank_read[b], 1)
                with dve.Fori(0, 2) as i, T.loop(i, 2, {"tiles": 4}):
                    for m in range(4):
                        b, v = T.take()
                        dve.wait_ge(k.bank_done[b], v)
                        residual(bass.ds(i * 4 + m, 1), b, cols, halves, G2).then_inc(k.bank_read[b], 1)
                dve.wait_ge(*k.moved(T.last()))
                norm(k.xT, cols, gained("ln2", l, cols), "x_ready" if l == 0 else "y_ready")

            h2 = k.h2
            dve.memset(area(CHAIN, GH * SEQ), 1.0)
            dve.wait_ge(S["row_out"], 16)
            dve.memset(k.p_cmp, 0.0)
            dve.memset(k.hid_v, 0.0).then_inc(S["dve_step"], 1)
            dve.wait_ge(S["dve_step"], T.next("dve_step"))
            chain = area(CHAIN, GH * NCH, CHUNK)
            dve.memset(chain[:, :, 0:1], 0.0).then_inc(S["dve_step"], 1)
            dve.wait_ge(S["dve_step"], T.next("dve_step"))
            dve.wait_ge(S["bias_in"], 16)

            def rms(name, l):
                std = area(STD2, SEQ)
                dve.wait_ge(*k.moved(skip(1)))
                dve.reciprocal(std, std).then_inc(S["dve_step"], 1)
                dve.wait_ge(S["dve_step"], T.next("dve_step"))
                for kt in range(KD):
                    j = kt if l is None else l * KD + kt
                    ins = dve.scalar_tensor_tensor(h2[:, kt, :], y[:, kt, :], k.vec(name, j), std, ALU.mult, ALU.mult)
                ins.then_inc(S["h_ready"], 1)

            def ffn():
                def pairs(j, i):
                    up = [T.take() for _ in range(2)]
                    for m, (b, v) in enumerate(up):
                        dve.wait_ge(k.bank_done[b], v)
                        dve.wait_ge(*k.moved(skip(1)))
                        o = act2[:, bass.ds(i * 8 + 2 * j + m, 1), :].rearrange("p o n -> p (o n)") if i is not None \
                            else act2[:, 2 * j + m, :]
                        dve.tensor_tensor(o, area(SILU2, 2, 2, SEQ)[:, j % 2, m, :], ps[:, b, 0:SEQ], ALU.mult) \
                            .then_inc(k.bank_read[b], 1)

                with dve.Fori(0, 2) as i, T.loop(i, 2, {"tiles": 16}):
                    for j in range(4):
                        pairs(j, i)
                for j in range(8, 11):
                    pairs(j, None)
                with dve.Fori(0, 2) as i, T.loop(i, 2, {"tiles": 4}):
                    for m in range(4):
                        b, v = T.take()
                        dve.wait_ge(k.bank_done[b], v)
                        x = y[:, bass.ds(i * 4 + m, 1), :].rearrange("p o n -> p (o n)")
                        dve.scalar_tensor_tensor(x, ps[:, b, 0:SEQ], 0.5, x, ALU.mult, ALU.add) \
                            .then_inc(k.bank_read[b], 1)
                dve.wait_ge(*k.moved(T.last()))

            def in_projections(l):
                skip(4)
                for x, name in enumerate(("cmp_pos_k_2", "cmp_pos_v_2")):
                    t, r, _ = VEC[name]
                    for g in range(2):
                        b, v = T.take()
                        dve.wait_ge(k.bank_done[b], v)
                        for half in range(2):
                            at = slice(HD * half, HD * half + HD)
                            src = ps[at, b, 0:SEQ].rearrange("p (n j e) -> p e j n", j=JP // 2, e=2)
                            for s in range(2):
                                pos = k.vecT[at, bass.ds(l * JP + (t * P + r + s * JP // 2), JP // 2)]
                                ins = dve.tensor_tensor(
                                    kbuf[x][at, s * JP // 2:(s + 1) * JP // 2, g, :], src[:, half, :, s:s + NCMP],
                                    over(pos.unsqueeze(2), [HD, JP // 2, NCMP]), ALU.add)
                        ins.then_inc(k.bank_read[b], 1)
                skip(6)
                for h in range(GH):
                    b, v = T.take()
                    dve.wait_ge(k.bank_done[b], v)
                    dve.tensor_scalar(z[:, h, :], ps[:, b, 0:SEQ], k.vec("gla_a_b_2", l * GH + h), None,
                                      ALU.add) \
                        .then_inc(k.bank_read[b], 1)
                dve.wait_ge(*k.moved(T.last()))
                dve.scalar_tensor_tensor(t1, z, -1.0, z, ALU.mult, ALU.min).then_inc(S["minus_abs_z"], 1)
                dve.wait_ge(S["log1p_ready"], T.next("log1p_ready"))
                dve.scalar_tensor_tensor(z, z, 0.0, t1, ALU.min, ALU.subtract).then_inc(S["dve_step"], 1)
                dve.wait_ge(S["dve_step"], T.next("dve_step"))
                flat = lambda v: v.rearrange("p h t -> p (h t)")
                dve.tensor_tensor_scan(flat(t1), area(CHAIN, GH * SEQ), flat(z), 0.0, ALU.mult, ALU.add) \
                    .then_inc(S["decay_ready"], 1)
                dve.wait_ge(S["edecay"], T.next("edecay"))
                ends = z.rearrange("p h (n i) -> p h n i", n=NCH)[:, :, :, CHUNK - 1]
                dve.tensor_copy(dch, ends)
                dve.tensor_tensor(qb, qb, z, ALU.mult).then_inc(S["edecay_used"], 1)
                dve.wait_ge(S["edecay"], T.next("edecay"))
                dve.tensor_tensor(kin, kb, z, ALU.mult).then_inc(S["dve_step"], 1)
                dve.wait_ge(S["dve_step"], T.next("dve_step"))
                chunks = lambda v: flat(v).rearrange("p (n i) -> p n i", i=CHUNK)
                dve.tensor_tensor(chunks(z), over(chunks(t1)[:, :, CHUNK - 1:CHUNK], [P, GH * NCH, CHUNK]),
                                  chunks(t1), ALU.subtract).then_inc(S["decay_ready"], 1)
                dve.wait_ge(S["edecay"], T.next("edecay"))
                dve.tensor_tensor(kb, kb, z, ALU.mult).then_inc(S["gla_in"], 1)
                skip(4 + 4 + 4 + 4 + 8)

            def sparse_attention():
                pc = k.p_cmp[:, :, :, 0:NCMP]
                for a in range(2):
                    b, v = T.take()
                    dve.wait_ge(k.bank_done[b], v)
                    dve.tensor_tensor(pc[:, :, 4 * a:4 * a + 4, :],
                                      ps[:, b, 0:8 * NCMP].rearrange("p (q c n) -> p q c n", q=2, c=4),
                                      k.cmp_bias[:, :, 4 * a:4 * a + 4, :], ALU.add) \
                        .then_inc(k.bank_read[b], 1)
                dve.wait_ge(*k.moved(T.last()))
                st = k.stat[:, 32:48].rearrange("p (q h) -> p q h", q=2)
                wide = [P, 2, HEADS, NCMP]
                dve.tensor_reduce(st, pc, AX, ALU.max).then_inc(S["dve_step"], 1)
                dve.wait_ge(S["dve_step"], T.next("dve_step"))
                dve.tensor_tensor(pc, pc, over(st.unsqueeze(3), wide), ALU.subtract).then_inc(S["cmp_max"], 1)
                heads3 = ga.rearrange("p q (h b) -> p q h b", b=3)
                dve.wait_ge(S["cmp_exp"], T.next("cmp_exp"))
                dve.tensor_reduce(st, pc, AX, ALU.add).then_inc(S["dve_step"], 1)
                dve.wait_ge(S["dve_step"], T.next("dve_step"))
                dve.reciprocal(st, st).then_inc(S["dve_step"], 1)
                dve.wait_ge(S["dve_step"], T.next("dve_step"))
                dve.tensor_tensor(st, st, heads3[:, :, :, 0], ALU.mult).then_inc(S["dve_step"], 1)
                dve.wait_ge(S["dve_step"], T.next("dve_step"))
                dve.tensor_tensor(st, st, over(k.col("has_cmp").unsqueeze(2), [P, 2, HEADS]), ALU.mult) \
                    .then_inc(S["dve_step"], 1)
                dve.wait_ge(S["dve_step"], T.next("dve_step"))
                dve.tensor_tensor(pc, pc, over(st.unsqueeze(3), wide), ALU.mult).then_inc(S["cmp_prob"], 1)

                out_of = {}

                def moved(u):
                    b, n = out_of[u // 2]
                    dve.wait_ge(k.bank_done[b], n)
                    dve.tensor_copy(oa[:, u // 2, :], ps[:, b, 0:SEQ]).then_inc(k.bank_read[b], 1)

                for u in range(HEADS + 1):
                    if u < HEADS:
                        c, a = u // 2, u % 2
                        h, buf = c + 4 * a, u % 2
                        nmax = k.stat[:, 16 * buf:16 * buf + 4]
                        parts = []
                        for q in range(2):
                            n = (q + 1) * P
                            b, v = T.take()
                            dve.wait_ge(k.bank_done[b], v)
                            p = prob2[:, buf, q * 2 * P:q * 2 * P + 2 * n].rearrange("p (j t) -> p j t", j=2)
                            dve.tensor_tensor(p, ps[:, b, 0:2 * n].rearrange("p (j t) -> p j t", j=2),
                                              over(k.bias[:, h, 2 * P - n:2 * P].unsqueeze(1), [P, 2, n]),
                                              ALU.add) \
                                .then_inc(k.bank_read[b], 1)
                            parts.append(p)
                        dve.wait_ge(*k.moved(T.last()))
                        for q in range(2):
                            ins = dve.tensor_reduce(nmax[:, 2 * q:2 * q + 2], parts[q], AX, ALU.max, negate=True)
                        ins.then_inc(S["nsa_max"], 1)
                    if u == 0:
                        skip(1)
                    if u >= 3 and u % 2 == 1:
                        moved(u - 2)
                    if u >= 1:
                        c, a = (u - 1) // 2, (u - 1) % 2
                        h, buf = c + 4 * a, (u - 1) % 2
                        dve.wait_ge(S["nsa_exp"], T.next("nsa_exp"))
                        sums = k.stat[:, 16 * buf + 4:16 * buf + 8]
                        dve.reciprocal(sums, sums).then_inc(S["dve_step"], 1)
                        dve.wait_ge(S["dve_step"], T.next("dve_step"))
                        two = sums.rearrange("p (q j) -> p q j", q=2)
                        dve.tensor_tensor(two, two, heads3[:, :, h, 1:3], ALU.mult).then_inc(S["dve_step"], 1)
                        dve.wait_ge(S["dve_step"], T.next("dve_step"))
                        for j in range(4):
                            n = P if j < 2 else 2 * P
                            o = j * P if j < 2 else 2 * P + (j - 2) * 2 * P
                            p = prob2[:, buf, o:o + n]
                            ins = dve.tensor_scalar(p, p, sums[:, j:j + 1], None, ALU.mult)
                        ins.then_inc(S["nsa_prob"], 1)
                        skip(2)
                        if a == 0:
                            out_of[(u - 1) // 2] = T.take()
                moved(HEADS - 1)

            def linear_attention(l):
                skip(2)
                for t in range(2):
                    b, v = T.take()
                    dve.wait_ge(k.bank_done[b], v)
                    dve.tensor_tensor(att[:, t], ps[:, b, :].rearrange("p (h c) -> p h c", h=GH),
                                      over(k.col("causal").unsqueeze(1), [P, GH, P]), ALU.mult) \
                        .then_inc(k.bank_read[b], 1)
                for n in range(NCH - 1):
                    for hp in range(2):
                        b, v = T.take()
                        dve.wait_ge(k.bank_done[b], v)
                        two = state[:, n, 2 * hp:2 * hp + 2, :]
                        kv = ps[:, b, :].rearrange("p (h c) -> p h c", h=2)
                        if n == 0:
                            ins = dve.tensor_copy(two, kv)
                        else:
                            for j in range(2):
                                h = 2 * hp + j
                                ins = dve.scalar_tensor_tensor(two[:, j, :], state[:, n - 1, h, :], dch[:, h, n:n + 1],
                                                               kv[:, j, :], ALU.mult, ALU.add)
                        ins.then_inc(k.bank_read[b], 1)
                    dve.wait_ge(*k.moved(T.last()))
                skip(KD)
                dve.wait_ge(*k.moved(skip(2)))
                dve.reciprocal(t1, t1).then_inc(S["dve_step"], 1)
                dve.wait_ge(S["dve_step"], T.next("dve_step"))
                heads = ob.rearrange("p (h v) t -> p h v t", v=2)
                dve.tensor_tensor(heads, heads, over(t1.unsqueeze(2), [P, GH, 2, SEQ]), ALU.mult) \
                    .then_inc(S["dve_step"], 1)
                dve.wait_ge(S["dve_step"], T.next("dve_step"))
                for j in range(KD):
                    ins = dve.scalar_tensor_tensor(ob[:, j, :], ob[:, j, :], k.vec("gla_out_norm_2", l * KD + j),
                                                   rb[:, j, :], ALU.mult, ALU.mult)
                ins.then_inc(S["gla_ready"], 1)

            def merge():
                mixed = area(MIXED2, KD, SEQ)
                tmp = area(MGATE + 1024, SEQ)
                with dve.Fori(0, 2) as i, T.loop(i, 2, {"tiles": 16, "merged": 4}):
                    for j in range(4):
                        branch = [T.take() for _ in range(2)]
                        m = mixed[:, bass.ds(i * 4 + j, 1), :].rearrange("p o n -> p (o n)")
                        gates = area(MGATE, 2, 2, SEQ)[:, j % 2]
                        last = skip(2)
                        dve.wait_ge(*k.moved(last))
                        for (b, v), o, gt in zip(branch, (m, tmp), range(2)):
                            dve.wait_ge(k.bank_done[b], v)
                            dve.tensor_tensor(o, gates[:, gt, :], ps[:, b, 0:SEQ], ALU.mult) \
                                .then_inc(k.bank_read[b], 1)
                        dve.wait_ge(*k.moved(branch[1]))
                        dve.tensor_tensor(m, m, tmp, ALU.add).then_inc(S["merged"], 1)
                        dve.wait_ge(S["merged"], T.next("merged"))
                for j in range(KD):
                    b, v = T.take()
                    dve.wait_ge(k.bank_done[b], v)
                    dve.tensor_tensor(y[:, j, :], y[:, j, :], ps[:, b, 0:SEQ], ALU.add).then_inc(k.bank_read[b], 1)
                dve.wait_ge(*k.moved(T.last()))

            with dve.Fori(0, LAYERS) as l, T.loop(l, LAYERS, PER_LAYER["dve"]):
                rms("ffn1_norm_2", l)
                ffn()
                rms("mix_norm_2", l)
                in_projections(l)
                sparse_attention()
                linear_attention(l)
                merge()
                rms("ffn2_norm_2", l)
                ffn()
            rms("final_norm_2", None)


_INS = ["x", "c", "ctx", "c_ctx", "w_ada", "b_ada", "w_in", "b_gate", "mla_q_g", "mla_kv_g", "w_uq", "w_uk", "w_uv",
        "gqa_q_g", "gqa_k_g", "w_fo", "w_mo", "w_go", "w_o", "ln1_g", "ln1_b", "w1", "w2", "ln2_g", "ln2_b",
        "rel_table_2", "ffn1_norm_2", "ffn1_w_gate_2", "ffn1_w_up_2", "ffn1_w_down_2", "mix_norm_2", "w_in_2",
        "cmp_pos_k_2", "cmp_pos_v_2", "cmp_k_w1_2", "cmp_k_w2_2", "cmp_v_w1_2", "cmp_v_w2_2", "gla_a_w2_2",
        "gla_a_b_2", "gla_out_norm_2", "w_branch_nsa_2", "w_branch_gla_2", "w_out_2", "ffn2_norm_2",
        "ffn2_w_gate_2", "ffn2_w_up_2", "ffn2_w_down_2", "final_norm_2"]


def kernel(**inputs):
    import numpy as np
    import concourse.bacc as bacc
    from concourse.bass_utils import run_bass_kernel_spmd

    nc = bacc.Bacc("TRN2", target_bir_lowering=False, num_devices=1)
    arrays = {name: np.ascontiguousarray(inputs[name]) for name in _INS}
    arrays.update(shape_constants())
    feed, W = {}, {}
    for name, a in arrays.items():
        feed[f"in_{name}"] = a
        W[name] = nc.dram_tensor(f"in_{name}", a.shape, mybir.dt.from_np(a.dtype), kind="ExternalInput").ap()
    out = nc.dram_tensor("out", (1, SEQ, D), F32, kind="ExternalOutput").ap()
    scratch = nc.dram_tensor("bias_by_distance", (HEADS, 512), F32, kind="Internal").ap()
    copies = nc.dram_tensor("bias_copies", (P, HEADS, 512), F32, kind="Internal").ap()
    build(nc, W, out, scratch, copies)
    r = run_bass_kernel_spmd(nc, [feed], core_ids=[0])
    return r.results[0]["out"]
```

```python
from contextlib import ExitStack, contextmanager

import concourse.bass as bass
from concourse import mybir

F32 = mybir.dt.float32
F32R = mybir.dt.float32r
ALU = mybir.AluOpType
ACT = mybir.ActivationFunctionType
AX = mybir.AxisListType.X

P = 128
D = 1024
KD = D // P
CTX, SEQ = 256, 256
TOK = CTX + SEQ
LAYERS = 2
EPS = 1e-6
ALPHA = (2.0 * LAYERS) ** 0.25
NEG = -1e30

MODS = 6 * D // P
HEADS, NOPE, ROPE, HD = 8, 64, 32, 64
RANK = 256
GATE0 = 544 + 512 + 256 + 512
FF1 = 4 * D
MLA_SCALE = float(NOPE + ROPE) ** -0.5
GQA_SCALE = float(HD) ** -0.5

FF2 = 2816
FT = FF2 // P
NCMP, CMP_STRIDE, CMP_BLOCK = 15, 16, 32
JP = CMP_BLOCK // 2
GH, DV, CHUNK = 4, 256, 64
NCH = SEQ // CHUNK
TAU = 16.0
BUCKETS = 32

SLOTS = 4
SLOT = 2048
LAND = 192
BANKS = 8

VEC_TILES = [
    [("b_ada", 96), ("ln1_g", 16), ("ln1_b", 16)],
    [("b_gate", 48), ("ln2_g", 16), ("ln2_b", 16), ("mla_q_g", 4), ("mla_kv_g", 4), ("gqa_q_g", 2),
     ("gqa_k_g", 2), ("c", 8), ("c_ctx", 8), ("gla_out_norm_2", 16)],
    [("cmp_pos_k_2", 32), ("cmp_pos_v_2", 32), ("ffn1_norm_2", 16), ("mix_norm_2", 16), ("ffn2_norm_2", 16),
     ("final_norm_2", 8), ("gla_a_b_2", 8)],
]
VEC = {}
VEC_ROWS = []
for _t, _names in enumerate(VEC_TILES):
    _r = 0
    for _name, _n in _names:
        VEC[_name] = (_t, _r, _n)
        _r += _n
    VEC_ROWS.append(_r)

CONST = {}
_at = 0
for _name, _n in [("ident", 128), ("ones", 128), ("pair", 128), ("rot32", 128), ("rot64", 128), ("dft_d", 256),
                  ("cos_s", 512), ("nsin_s", 512), ("cos32", 256), ("sin32", 256), ("cos64", 256), ("sin64", 256),
                  ("causal", 128), ("has_cmp", 2), ("eps", 1), ("one", 1)]:
    CONST[_name] = (_at, _n)
    _at += _n
NCONST = _at


def shape_constants():
    import numpy as np

    c = {}
    i = np.arange(P)
    c["ident"] = np.eye(P)
    c["ones"] = np.ones((P, P))
    c["pair"] = (i[:, None] // HD == i[None, :] // HD).astype(np.float64)

    def rotation(n):
        r = np.zeros((P, P))
        for m in range(P):
            half = n // 2
            if m % n < half:
                r[m + half, m] = -1.0
            else:
                r[m - half, m] = 1.0
        return r

    c["rot32"], c["rot64"] = rotation(ROPE), rotation(HD)
    ang = 2 * np.pi * ((i[:, None] * i[None, :]) % P) / P
    norm = 1.0 / np.sqrt(P * SEQ)
    c["dft_d"] = np.concatenate([np.cos(ang), np.sin(ang)], axis=1) * norm
    s = np.arange(SEQ)
    angs = 2 * np.pi * ((s[:, None] * s[None, :]) % SEQ) / SEQ
    c["cos_s"] = np.concatenate([np.cos(angs)[:P], np.cos(angs)[P:]], axis=1)
    c["nsin_s"] = -np.concatenate([np.sin(angs)[:P], np.sin(angs)[P:]], axis=1)
    grid_w = 64
    rows = np.repeat(np.arange(SEQ // grid_w), grid_w).astype(np.float32)
    cols = np.tile(np.arange(grid_w), SEQ // grid_w).astype(np.float32)
    for d_rot in (ROPE, HD):
        n = d_rot // 4
        freqs = np.float32(10000.0) ** (-np.arange(n, dtype=np.float32) / np.float32(n))
        a = np.concatenate([rows[:, None] * freqs, cols[:, None] * freqs], axis=-1).astype(np.float32)
        a = a[:, i % (d_rot // 2)].T
        c[f"cos{d_rot}"], c[f"sin{d_rot}"] = np.cos(a), np.sin(a)
    c["causal"] = ((i[:, None] // CHUNK == i[None, :] // CHUNK) & (i[:, None] <= i[None, :])).astype(np.float64)
    c["has_cmp"] = np.stack([i >= CMP_BLOCK - 1, i >= 0], axis=1).astype(np.float64)
    c["eps"] = np.full((P, 1), EPS)
    c["one"] = np.ones((P, 1))
    consts = np.concatenate([c[n].reshape(P, -1) for n in CONST], axis=1).astype(np.float32)

    def bucket(dist):
        n = np.maximum(dist, 0)
        exact = BUCKETS // 2
        nf = np.maximum(n, 1).astype(np.float32)
        ratio = np.log(nf / np.float32(exact)) / np.float32(np.log(1024 / exact))
        log_b = exact + (ratio * np.float32(BUCKETS - exact)).astype(np.int32)
        return np.where(n < exact, n, np.minimum(log_b, BUCKETS - 1))

    def one_hot(dist):
        hot = np.zeros((BUCKETS + 1,) + dist.shape, np.float32)
        b = np.where(dist >= 0, bucket(dist), BUCKETS)
        for k in range(BUCKETS + 1):
            hot[k] = b == k
        return hot

    toeplitz = one_hot(255 - np.arange(512))
    blocks = one_hot(s[None, :] - (np.arange(NCMP)[:, None] * CMP_STRIDE + CMP_BLOCK - 1))
    return {"consts": consts, "bucket_of_distance": toeplitz,
            "bucket_of_block": np.ascontiguousarray(blocks.reshape(BUCKETS + 1, NCMP * SEQ))}


class Tally:

    def __init__(self):
        self.count = {}
        self.regs = []
        self.bank = 0

    def value(self, name, off=0, div=1):
        v = (self.count.get(name, 0) + off) // div
        for reg, per in self.regs:
            n = per.get(name, 0)
            assert n % div == 0, (name, n)
            if n:
                v = reg * (n // div) + v
        return v

    def next(self, name, n=1):
        self.count[name] = self.count.get(name, 0) + n
        return self.value(name)

    def take(self):
        b = self.bank
        self.bank = (b + 1) % BANKS
        return b, self.next(f"bank{b}")

    def last(self):
        b = (self.bank - 1) % BANKS
        return b, self.value(f"bank{b}")

    def panel(self):
        n = self.next("panel")
        slot = (self.count["panel"] - 1) % SLOTS
        return slot, self.value("panel", SLOTS - 1, SLOTS), n

    @contextmanager
    def loop(self, reg, times, per):
        per = dict(per)
        tiles = per.pop("tiles", 0)
        for j in range(tiles):
            b = f"bank{(self.bank + j) % BANKS}"
            per[b] = per.get(b, 0) + 1
        before = dict(self.count)
        self.regs.append((reg, per))
        yield
        self.regs.pop()
        added = {n: v - before.get(n, 0) for n, v in self.count.items() if v != before.get(n, 0)}
        assert added == per, {n: (added.get(n, 0), per.get(n, 0)) for n in {*added, *per}
                              if added.get(n, 0) != per.get(n, 0)}
        for n, v in per.items():
            self.count[n] = before.get(n, 0) + v * times


class Chip:

    def __init__(self, nc, ctx):
        def sb(name, n, dtype=F32):
            return ctx.enter_context(nc.sbuf_tensor(name, [P, n], dtype))

        def both(name, n):
            with nc.sbuf_tensor(name, [P, n], F32) as plain:
                pass
            return plain, sb(f"{name}_r", n, F32R)

        def sem(name):
            return ctx.enter_context(nc.semaphore(name))

        self.ring, self.ring_lo = zip(*(both(f"ring{s}", SLOT) for s in range(SLOTS)))
        self.ring_hi = [sb(f"ring{s}_hi", SLOT, F32R) for s in range(SLOTS)]
        self.xT = sb("xT", KD * TOK)[:, :].rearrange("p (k t) -> p k t", k=KD)
        hbuf, hbuf_r = both("hT", 2 * KD * TOK)

        def halves(n):
            return tuple(hbuf_r[:, j * KD * n:(j + 1) * KD * n].rearrange("p (k t) -> p k t", k=KD) for j in range(2))

        self.h, self.h2 = halves(TOK), halves(SEQ)
        at = 2 * KD * SEQ
        self.bias = hbuf[:, at:at + 2 * P * HEADS].rearrange("p (h u) -> p h u", h=HEADS)
        at += 2 * P * HEADS
        blocks = JP * 2 * NCMP

        def kv_blocks(t, j):
            return t[:, at + j * blocks:at + (j + 1) * blocks].rearrange("p (j n) -> p j n", j=JP)

        self.kbuf = [kv_blocks(hbuf, x) for x in range(2)]
        self.kbuf_split = [(kv_blocks(hbuf_r, 2 + x), kv_blocks(hbuf_r, x)) for x in range(2)]
        self.const = sb("const", NCONST)
        self.vecT = sb("vecT", len(VEC_TILES) * P)
        self.mods = sb("mods", LAYERS * 2 * MODS)[:, :].rearrange("p (m s) -> p m s", s=2)
        silu, silu_r = both("silu_c", 2 * KD)
        silu_hi = sb("silu_c_hi", 2 * KD, F32R)
        self.silu_c, *self.silu_split = (v[:, :].rearrange("p (k s) -> p k s", s=2) for v in (silu, silu_hi, silu_r))
        self.arena, self.arena_r = both("arena", ARENA)
        self.cmp_bias = sb("cmp_bias", 2 * HEADS * NCMP)[:, :].rearrange("p (q h n) -> p q h n", q=2, h=HEADS)
        hid_v, p_cmp = sb("hid_v", 2 * 2 * P), sb("p_cmp", 2 * HEADS * 32)
        self.hid_v = hid_v[:, :].rearrange("p (m g r n) -> p m g r n", m=2, g=2, r=4)
        self.p_cmp = p_cmp[:, :].rearrange("p (q h n) -> p q h n", q=2, h=HEADS)
        self.bias_row = p_cmp[0:HEADS, :]
        self.mod_rows = [hid_v[0:2, :], p_cmp[0:2, :]]
        self.stat = sb("stat", 64)
        self.ps = ctx.enter_context(nc.psum_tensor("ps", [P, BANKS, 512], F32))

        self.panel_landed = [sem(f"panel_landed{s}") for s in range(SLOTS)]
        self.hi_ready = [sem(f"hi_ready{s}") for s in range(SLOTS)]
        self.lo_ready = [sem(f"lo_ready{s}") for s in range(SLOTS)]
        self.panel_begun = sem("panel_begun")
        self.bank_done = [sem(f"bank_done{b}") for b in range(BANKS)]
        self.bank_read = [sem(f"bank_read{b}") for b in range(BANKS)]
        self.sem = {name: sem(name) for name in (
            "act_step", "dve_step",
            "const_in", "vec_in", "tok_in", "table_in", "neg_row", "silu_plain", "silu_rounded", "silu_split", "row_out",
            "row_copied", "bias_in", "final_ready", "out_ready", "out_done",
            "x_ready", "y_ready", "centred", "squared", "scaled", "h_plain", "h_rounded", "h_ready",
            "mods_ready", "squared_qk", "normed", "latent_rounded", "latent_split", "roped", "row_max", "prob_ready",
            "branch_rounded", "branch_split", "gated", "mixed_rounded", "mixed_split", "relu_ready", "hid_rounded", "hid_split",
            "hid_used",
            "act2_split", "blocks_split", "small_in", "minus_abs_z", "log1p_ready", "decay_ready", "edecay", "edecay_used", "gla_in",
            "gla_out", "cmp_max", "cmp_exp", "cmp_prob", "nsa_max", "nsa_exp", "nsa_prob", "merge_in",
            "merged")}

    def area(self, at, *dims, rounded=False):
        n = 1
        for d in dims:
            n *= d
        v = (self.arena_r if rounded else self.arena)[:, at:at + n]
        if len(dims) == 1:
            return v
        names = "abcd"[:len(dims)]
        return v.rearrange(f"p ({' '.join(names)}) -> p {' '.join(names)}", **dict(zip(names[1:], dims[1:])))

    def split(self, hi, lo, *dims):
        return self.area(hi, *dims, rounded=True), self.area(lo, *dims, rounded=True)

    def moved(self, result):
        return self.bank_read[result[0]], result[1]

    def col(self, name):
        at, n = CONST[name]
        return self.const[:, at:at + n]

    def vec(self, name, j):
        t, r, _ = VEC[name]
        return self.vecT[:, bass.ds(t * P + r + j, 1)]


def cut(v, *at):
    return v[0][at], v[1][at]


ALL = slice(None)

ARENA = 18944
CKV, CQ, KR, KG, VG, QR, QG, QN, KN, FIN, PROBT, OM, VM = (
    0, 1024, 2048, 2560, 3072, 3584, 4608, 6656, 8704, 10752, 12800, 14848, 16896)
PROB = CKV
OG = VM
SQK, DFT1, ROT = PROBT, QN, OM
SQ_KG, SQ_CQ, SQ_QG, SQ_CKV = 0, 1, 3, 7
STD_CKV = 8
FIN_HI, OM_HI, OG_HI, MIXED, TMP_M, GATES = 0, 2048, 4096, 6144, 10240, PROBT
MIXED_HI = 0
SQ, MEAN, STD, PLAIN = 0, 4096, 4608, 5120
HID, HID_HI, HID_SLOTS = 0, 4 * KD * TOK, 4
A2, A2_HI, SILU2, PLAIN2, SQ2, STD2 = 0, 5632, 11264, 12288, 16400, 18448
(QA, KSLC, KWIN, VSLC, VWIN, GA, DCH, KCMP, VCMP, HIDK, ALR, OA, PCT, PROB2, PROBT2, QB, KB, KIN, Z, T1, VB,
 RB, OB) = (0, 1024, 1280, 1536, 1792, 2048, 2096, 2112, 2128, 2256, 2320, 2576, 3600, 4112, 5648,
            7184, 8208, 9232, 10256, 11280, 12304, 14352, 16400)
STATE, SQO = PROB2, KB
OA_HI, OB_HI, MIXED2, MIXED2_HI, MGATE, TMP2 = STATE, STATE + 1024, VB, RB, KB, QB
XN, VN, TABLE, HOT, HOTC = 0, 4096, 4480, 4608, 5120
SH1, SC1, G1, SH2, SC2, G2 = (KD * j for j in range(6))
HALVES = [(0, CTX), (CTX, TOK)]
ADA_FIRST = 8
ADA = LAYERS * MODS // 2
PANELS_1, PANELS_2 = 176, 108


N_VEC = len(VEC) + 2
PER_BANK = {f"bank{b}": 31 for b in range(BANKS)}
PER_LAYER = {
    "pe": {**PER_BANK, "panel": PANELS_2, "squared": 3 * KD, "h_ready": 3 * KD, "act2_split": FT, "small_in": 48, "blocks_split": 2, "cmp_prob": 1,
           "nsa_prob": HEADS, "gla_in": 1, "gla_out": 1, "merge_in": 1, "merged": 4},
    "act": {**PER_BANK, "panel": PANELS_2, "act_step": 1, "h_plain": 3 * KD, "minus_abs_z": 1, "decay_ready": 2,
            "edecay_used": 1, "cmp_max": 1, "nsa_max": HEADS},
    "dve": {**PER_BANK, "dve_step": 63, "h_rounded": 3 * KD, "log1p_ready": 1, "edecay": 3, "cmp_exp": 1,
            "nsa_exp": HEADS},
}


def units(l):
    return [(kind, half, c, a) for kind in "mg" for half in ((0, 1) if l == 0 else (1,))
            for c in range(HEADS // 2) for a in range(2)]


def build(nc, W, out, scratch, copies):
    with ExitStack() as ctx:
        k = Chip(nc, ctx)
        S, ps, area = k.sem, k.ps, k.area
        ident, ones, pair = k.col("ident"), k.col("ones"), k.col("pair")
        block = ctx.enter_context(nc.Block())

        ckv, cq = area(CKV, 2, TOK), area(CQ, 2, TOK)
        kr, kg = area(KR, TOK), area(KG, TOK)
        vg, fin = area(VG, 4, P), area(FIN, 4, TOK)
        qg, qn, qr = area(QG, 4, TOK), area(QN, 4, TOK), area(QR, 2, TOK)
        kn, vm = area(KN, 4, TOK), area(VM, 4, TOK)
        om, og = area(OM, 4, TOK), area(OG, 4, TOK)
        prob, probT = area(PROB, 2, 2, TOK), area(PROBT, 2, 4, SEQ)
        dft1 = area(DFT1, 2, 2, 2 * P)
        sqk, sqk_r = area(SQK, 9, TOK), area(SQK, 9, TOK, rounded=True)
        ckv_hi, cq_hi = sqk_r[:, SQ_CQ + 1:SQ_CKV + 1:SQ_CKV - SQ_CQ - 1, :], sqk_r[:, SQ_KG:SQ_KG + 2, :]
        ckv_split = (ckv_hi, area(CKV, 2, TOK, rounded=True))
        cq_split = (cq_hi, area(CQ, 2, TOK, rounded=True))
        dft_d = k.col("dft_d")
        cos_s = k.col("cos_s").rearrange("p (t s) -> p t s", t=2)
        nsin_s = k.col("nsin_s").rearrange("p (t s) -> p t s", t=2)
        y = k.xT[:, :, CTX:TOK]
        branch = [fin, om, og]
        branch_split = [k.split(hi, lo, 4, TOK) for hi, lo in ((FIN_HI, FIN), (OM_HI, OM), (OG_HI, OG))]
        mixed, mixed_split = area(MIXED, KD, TOK), k.split(MIXED_HI, MIXED, KD, TOK)
        plain = area(PLAIN, KD, TOK)

        qa, kslc, kwin = area(QA, 4, SEQ), area(KSLC, SEQ), area(KWIN, SEQ)
        vslc, vwin = area(VSLC, 2, P), area(VWIN, 2, P)
        ga, dch = area(GA, 2, 3 * HEADS), area(DCH, GH, NCH)
        kcmp, vcmp, hidk = area(KCMP, NCMP), area(VCMP, 2, HD), area(HIDK, 2, 2 * NCMP)
        oa, pcT = area(OA, 4, SEQ), area(PCT, 4, P)
        prob2, probT2 = area(PROB2, 2, 768), area(PROBT2, 2, 6, P)
        qb, kb, kin = area(QB, GH, SEQ), area(KB, GH, SEQ), area(KIN, GH, SEQ)
        z, t1 = area(Z, GH, SEQ), area(T1, GH, SEQ)
        vb, rb, ob = area(VB, 2, GH * DV), area(RB, KD, SEQ), area(OB, KD, SEQ)
        state = area(STATE, NCH - 1, GH, DV)
        kst, att = area(T1, 2, GH, P), area(Z, 2, GH, P)
        at = CONST["cos32"][0]
        w_decay = k.const[:, at:at + 512]
        w_cmp = [k.const[:, at + 512 + x * P:at + 512 + x * P + P].rearrange("p (m n) -> p m n", m=2) for x in range(2)]
        gate_rows = k.const[0:3 * HEADS, at + 768:at + 768 + SEQ]
        at = CONST["pair"][0]
        hid_rows = k.const[0:2 * NCMP, at:at + 512].rearrange("p (x n) -> p x n", x=2)
        chain = k.const[:, CONST["cos_s"][0]:CONST["cos_s"][0] + GH * SEQ]
        act2, act2_split = area(A2, FT, SEQ), k.split(A2_HI, A2, FT, SEQ)
        plain2 = area(PLAIN2, KD, SEQ)
        oa_split, ob_split = k.split(OA_HI, OA, 4, SEQ), k.split(OB_HI, OB, KD, SEQ)
        mixed2, mixed2_split = area(MIXED2, KD, SEQ), k.split(MIXED2_HI, MIXED2, KD, SEQ)
        rotated = ([("rot32", kr), ("rot64", kg)] + [("rot32", qr[:, j, :]) for j in range(2)]
                   + [("rot64", qg[:, c, :]) for c in range(4)])

        def modulated(sc, sh, halves):
            return lambda kt: [(slice(*HALVES[s]), k.mods[:, sc + kt, s:s + 1], k.mods[:, sh + kt, s:s + 1])
                               for s in halves]

        def gate(m):
            return area(GATES + m * TOK, TOK)

        def relu(l, j):
            return area(HID_HI, HID_SLOTS, TOK if l == 0 else SEQ)[:, j % HID_SLOTS, :]

        def hidden(l):
            n = TOK if l == 0 else SEQ
            return (area(HID, 4 * KD, n), area(HID, 4 * KD, n, rounded=True), area(HID_HI, HID_SLOTS, n, rounded=True))

        @block.sync
        def _(sp):
            T = Tally()

            def slot():
                s, _, n = T.panel()
                if not (isinstance(n, int) and n <= SLOTS):
                    sp.wait_ge(k.panel_begun, n - SLOTS + 1)
                return s

            def load(s, parts):
                for j, (dst, src) in enumerate(parts):
                    last = j == len(parts) - 1
                    sp.dma_start(dst, src).then_inc(
                        k.panel_landed[s], LAND - 16 * (len(parts) - 1) if last else 16)

            def at(s, off, rows, cols):
                return k.ring[s][:, off:off + rows * cols].rearrange("p (k n) -> p k n", k=rows)

            def rows(w, r0=0, n=None):
                v = w.rearrange("o (k p) n -> p (o k) n", p=P)
                return v if n is None else v[:, r0:r0 + n, :]

            vn = area(VN, 3, P)
            n_vec = 0
            for name, (t, r, n) in VEC.items():
                src = W[name]
                flat = src if len(src.shape) == 1 else src.rearrange(
                    f"{' '.join('abc'[:len(src.shape)])} -> ({' '.join('abc'[:len(src.shape)])})")
                if name in ("gqa_q_g", "gqa_k_g"):
                    for half in range(2):
                        sp.dma_start(vn[r:r + n, t, half * HD:(half + 1) * HD], src).then_inc(S["vec_in"], 16)
                    n_vec += 2
                else:
                    sp.dma_start(vn[r:r + n, t, :], flat.rearrange("(r p) -> r p", p=P)).then_inc(S["vec_in"], 16)
                    n_vec += 1
            assert n_vec == N_VEC
            sp.dma_start(k.const[:, :], W["consts"]).then_inc(S["const_in"], 16)
            xn = area(XN, 4, D)
            sp.dma_start(xn[:, 0:2, :], W["ctx"][0].rearrange("(t p) d -> p t d", p=P)).then_inc(S["tok_in"], 16)
            sp.dma_start(xn[:, 2:4, :], W["x"][0].rearrange("(t p) d -> p t d", p=P)).then_inc(S["tok_in"], 16)
            sp.dma_start(area(TABLE, HEADS)[0:BUCKETS, :], W["rel_table_2"]).then_inc(S["table_in"], 16)
            sp.dma_start(area(HOT, 512)[0:BUCKETS + 1, :], W["bucket_of_distance"]).then_inc(S["table_in"], 16)
            sp.dma_start(area(HOTC, NCMP * SEQ)[0:BUCKETS + 1, :], W["bucket_of_block"]).then_inc(S["table_in"], 16)

            def ada(l, c0, i=0, step=0):
                s = slot()
                load(s, [(at(s, 0, KD, 256), rows(W["w_ada"][l:l + 1])[:, :, bass.ds(i * step + c0, 256)])])

            def project(l):
                w_in = rows(W["w_in"][l:l + 1])

                def cols(c0, n):
                    s = slot()
                    load(s, [(at(s, 0, KD, n), w_in[:, :, c0:c0 + n])])

                cols(0, 256)
                s = slot()
                v = at(s, 0, KD, 256)
                load(s, [(v[:, :, 32 * r:32 * r + 32], w_in[:, :, 256:288]) for r in range(4)]
                     + [(v[:, :, P:2 * P], w_in[:, :, 288:416])])
                for j in range(3):
                    cols(416 + 256 * j, 256)
                cols(1184, 256)
                for c in (0, 2):
                    s = slot()
                    v = at(s, 0, KD, 256)
                    load(s, [(v[:, :, j * P + a * HD:j * P + a * HD + HD],
                              w_in[:, :, 1312 + (4 * a + c + j) * HD:1312 + (4 * a + c + j + 1) * HD])
                             for j in range(2) for a in range(2)])
                s = slot()
                load(s, [(at(s, 0, 2, 512), rows(W["w_uk"][l:l + 1])), (at(s, 1024, 2, 512), rows(W["w_uv"][l:l + 1]))])
                s = slot()
                uq = W["w_uq"][l:l + 1].rearrange("o (k p) (h e) -> p (o k) h e", p=P, e=NOPE + ROPE)
                uqn = k.ring[s][:, 0:1024].rearrange("p (k h e) -> p k h e", k=2, h=HEADS)
                uqr = k.ring[s][:, 1024:1536].rearrange("p (k j a b e) -> p k j a b e", k=2, j=2, a=2, b=2)
                load(s, [(at(s, 1536, 2, 256), rows(W["w_uk"][l:l + 1])[:, :, 0:256])] + [(uqn[:, t], uq[:, t, :, 0:NOPE]) for t in range(2)]
                     + [(uqr[:, t, j, a], uq[:, t, 4 * j + a:4 * j + a + 3:2, NOPE:])
                        for t in range(2) for j in range(2) for a in range(2)])

            def mix_and_mlp(l):
                lay = slice(l, l + 1)
                w_in = rows(W["w_in"][lay])
                go = W["w_go"][lay].rearrange("o (a c d) n -> a d (o c) n", a=2, d=HD)
                for n in (0, 512):
                    for g, name in enumerate(("w_fo", "w_mo", "w_go")):
                        for j in range(2):
                            s = slot()
                            c0 = GATE0 + g * D + n + j * 256
                            load(s, [(at(s, 0, KD, 256), w_in[:, :, c0:c0 + 256])])
                        s = slot()
                        v = at(s, 0, 4, 512)
                        load(s, [(v[HD * a:HD * a + HD], go[a][:, :, n:n + 512]) for a in range(2)]
                             if name == "w_go" else [(v, rows(W[name][lay])[:, :, n:n + 512])])
                for j in range(4):
                    s = slot()
                    load(s, [(at(s, 0, KD, 256), rows(W["w_o"][lay])[:, :, 256 * j:256 * j + 256])])
                with sp.Fori(0, 4) as i, T.loop(i, 4, {"panel": 4}):
                    for j in range(4):
                        s = slot()
                        load(s, [(at(s, 0, KD, 256), rows(W["w1"][lay])[:, :, bass.ds(i * 1024 + j * 256, 256)])])
                with sp.Fori(0, 4) as i, T.loop(i, 4, {"panel": 4}):
                    for j in range(4):
                        s = slot()
                        load(s, [(at(s, 0, 2, D), rows(W["w2"][lay])[:, bass.ds(i * 8 + 2 * j, 2), :])])

            def ffn(l, f):
                lay = bass.ds(l, 1)
                gate, up, down = (rows(W[f"{f}_w_{x}_2"][lay]) for x in ("gate", "up", "down"))

                def pair(c0, i=0, step=0):
                    for w in (up, gate):
                        s = slot()
                        load(s, [(at(s, 0, KD, 256), w[:, :, bass.ds(i * step + c0, 256)])])

                pair(0)
                with sp.Fori(0, 5) as i, T.loop(i, 5, {"panel": 4}):
                    for j in range(2):
                        pair(256 + j * 256, i, 512)
                for j in range(FT // 2):
                    s = slot()
                    load(s, [(at(s, 0, 2, D), down[:, 2 * j:2 * j + 2, :])])

            def second_mixer(l):
                lay = bass.ds(l, 1)
                w_in = rows(W["w_in_2"][lay])

                def cols(c0, n):
                    for c in range(c0, c0 + n, 256):
                        s = slot()
                        load(s, [(at(s, 0, KD, 256), w_in[:, :, c:c + 256])])

                for c in (0, 2):
                    s = slot()
                    v = at(s, 0, KD, 256)
                    load(s, [(v[:, :, j * P + a * HD:j * P + a * HD + HD],
                              w_in[:, :, (4 * a + c + j) * HD:(4 * a + c + j + 1) * HD])
                             for j in range(2) for a in range(2)])
                for g in (0, 2):
                    s = slot()
                    v = at(s, 0, KD, 256)
                    load(s, [(v[:, :, j * P + r * HD:j * P + r * HD + HD],
                              w_in[:, :, 512 + (g + j) * HD:512 + (g + j + 1) * HD]) for j in range(2) for r in range(2)])
                cols(768, 512)
                cols(1280, 256)
                cols(3352, 256)
                sp.dma_start(w_decay[0:16, :], W["gla_a_w2_2"][lay].rearrange("o r n -> r (o n)")).then_inc(S["small_in"], 16)
                for x in range(2):
                    sp.dma_start(w_cmp[x], rows(W[f"cmp_{'kv'[x]}_w2_2"][lay])).then_inc(S["small_in"], 16)
                for x in "kv":
                    for j in range(2):
                        s = slot()
                        load(s, [(at(s, 0, 8, 256), rows(W[f"cmp_{x}_w1_2"][lay])[:, 8 * j:8 * j + 8, :])])
                cols(1304, 2048)
                cols(3368, 1024)
                nsa = W["w_branch_nsa_2"][lay].rearrange("o (a c d) n -> a d (o c) n", a=2, d=HD)
                for n in (0, 512):
                    cols(4392 + n, 512)
                    cols(4392 + D + n, 512)
                    s = slot()
                    v = at(s, 0, 4, 512)
                    load(s, [(v[HD * a:HD * a + HD], nsa[a][:, :, n:n + 512]) for a in range(2)])
                    for j in range(2):
                        s = slot()
                        c0 = n + j * 256
                        load(s, [(at(s, 0, KD, 256), rows(W["w_branch_gla_2"][lay])[:, :, c0:c0 + 256])])
                for j in range(4):
                    s = slot()
                    load(s, [(at(s, 0, KD, 256), rows(W["w_out_2"][lay])[:, :, 256 * j:256 * j + 256])])

            for j in range(SLOTS):
                ada(0, j * 256)
            sp.wait_ge(k.bank_read[0], 1)
            sp.dma_start(scratch, k.bias_row).then_inc(S["row_out"], 16)
            sp.wait_ge(S["row_out"], 16)
            sp.dma_start(copies, scratch.unsqueeze(0).broadcast_to([P, HEADS, 512])).then_inc(S["row_copied"], 16)
            for j in range(SLOTS, ADA_FIRST):
                ada(0, j * 256)
            project(0)
            for l, first in ((0, ADA_FIRST), (1, 0)):
                times = (MODS // 2 - first) // 4
                with sp.Fori(0, times) as i, T.loop(i, times, {"panel": 4}):
                    for j in range(4):
                        ada(l, (first + j) * 256, i, 1024)
            mix_and_mlp(0)
            project(1)
            mix_and_mlp(1)
            assert T.count["panel"] == PANELS_1, T.count["panel"]
            sp.wait_ge(S["row_copied"], 16)
            sp.wait_ge(S["y_ready"], KD)
            sp.dma_start(k.bias, bass.AP(copies.tensor, P - 1, [[512 * HEADS - 1, P], [512, HEADS], [1, 2 * P]])) \
                .then_inc(S["bias_in"], 16)
            with sp.Fori(0, LAYERS) as l, T.loop(l, LAYERS, {"panel": PANELS_2}):
                ffn(l, "ffn1")
                second_mixer(l)
                ffn(l, "ffn2")
            sp.wait_ge(S["out_ready"], 4)
            sp.dma_start(out[0].rearrange("(t p) d -> p t d", p=P), area(0, 2, D)).then_inc(S["out_done"], 16)
            sp.wait_ge(S["out_done"], 16)

        @block.tensor
        def _(pe):
            T = Tally()

            def bank():
                b, n = T.take()
                if not (isinstance(n, int) and n == 1):
                    pe.wait_ge(k.bank_read[b], n - 1)
                return b

            fresh = [False]

            def panel():
                s, rounds, _ = T.panel()
                pe.wait_ge(k.lo_ready[s], rounds)
                fresh[0] = True
                return k.ring_hi[s], k.ring_lo[s]

            def view(w, off, rows, cols):
                return tuple(v[:, off:off + rows * cols].rearrange("p (k n) -> p k n", k=rows) for v in w)

            def products(o, pairs, start=True, stop=True):
                passes = []
                for a, b in pairs:
                    passes += [(a[0], b[0]), (a[0], b[1]), (a[1], b[0])] if isinstance(a, tuple) else [(a, b)]
                for j, (lhsT, rhs) in enumerate(passes):
                    mm = pe.matmul(o, lhsT, rhs, start=start and j == 0, stop=stop and j == len(passes) - 1,
                                   skip_group_check=True)
                    if fresh[0]:
                        mm.then_inc(k.panel_begun, 1)
                        fresh[0] = False
                return mm

            def result(n, pairs):
                b = bank()
                products(ps[:, b, 0:n], pairs).then_inc(k.bank_done[b], 1)
                return T.last()

            def tile(w, m, x, cols):
                n = w[0].shape[1]
                return [(cut(w, ALL, kt, slice(m * P, m * P + P)), cut(x, ALL, kt, cols)) for kt in range(n)]

            def flip(o, src):
                return pe.transpose(o, src, ident)

            pe.wait_ge(S["table_in"], 48)
            pe.wait_ge(S["neg_row"], T.next("neg_row"))
            table = area(TABLE, HEADS)[0:BUCKETS + 1, :]
            b = bank()
            pe.matmul(ps[0:HEADS, b, :], table, area(HOT, 512)[0:BUCKETS + 1, :], start=True, stop=True) \
                .then_inc(k.bank_done[b], 1)
            hotc = area(HOTC, NCMP, SEQ)
            b = bank()
            for q in range(2):
                for n in range(NCMP):
                    at = (q * NCMP + n) * HEADS
                    mm = pe.matmul(ps[:, b, at:at + HEADS], hotc[0:BUCKETS + 1, n, q * P:q * P + P], table,
                                   start=True, stop=True)
            mm.then_inc(k.bank_done[b], 1)
            pe.wait_ge(S["const_in"], T.next("const_in", 16))
            pe.wait_ge(S["vec_in"], T.next("vec_in", 16 * N_VEC))
            b = bank()
            for t, r in enumerate(VEC_ROWS):
                mm = pe.transpose(ps[:, b, t * P:t * P + r], area(VN, 3, P)[0:r, t, :], ident[0:r, 0:r])
            mm.then_inc(k.bank_done[b], 1)
            pe.wait_ge(S["tok_in"], T.next("tok_in", 32))
            for kt in range(KD):
                b = bank()
                for t in range(4):
                    mm = flip(ps[:, b, t * P:t * P + P], area(XN, 4, D)[:, t, kt * P:kt * P + P])
                mm.then_inc(k.bank_done[b], 1)

            def modulation():
                b = bank()
                for j in range(2):
                    w = view(panel(), 0, KD, 256)
                    mm = products(ps[0:2, b, j * 256:j * 256 + 256], [(cut(k.silu_split, ALL, kt, ALL), cut(w, ALL, kt, ALL))
                                                                      for kt in range(KD)])
                mm.then_inc(k.bank_done[b], 1)
                return T.last()

            def mods_turned(row, group):
                pe.wait_ge(*k.moved(row))
                b = bank()
                for t in range(4):
                    mm = pe.transpose(ps[:, b, 2 * t:2 * t + 2], k.mod_rows[group % 2][:, t * P:t * P + P],
                                      ident[0:2, 0:2])
                mm.then_inc(k.bank_done[b], 1)

            def last_results():
                return [((T.bank + kt) % BANKS, T.value(f"bank{(T.bank + kt) % BANKS}")) for kt in range(KD)]

            def norm(cols, added):
                n = cols.stop - cols.start
                b = bank()
                for kt in range(KD):
                    if added:
                        pe.wait_ge(*k.moved(added[kt]))
                    else:
                        pe.wait_ge(S["x_ready"], T.next("x_ready"))
                    mm = products(ps[:, b, 0:n], [(ones, k.xT[:, kt, cols])], kt == 0, kt == KD - 1)
                mm.then_inc(k.bank_done[b], 1)
                sq = area(SQ, KD, TOK)
                b = bank()
                for kt in range(KD):
                    pe.wait_ge(S["squared"], T.next("squared"))
                    mm = products(ps[:, b, 0:n], [(ones, sq[:, kt, cols])], kt == 0, kt == KD - 1)
                mm.then_inc(k.bank_done[b], 1)

            def project(cols):
                n = cols.stop - cols.start
                h, every = k.h, slice(0, TOK)
                for c in range(2):
                    w = view(panel(), 0, KD, 256)
                    for m in range(2):
                        b = bank()
                        for kt in range(KD):
                            if c == 0 and m == 0:
                                pe.wait_ge(S["h_ready"], T.next("h_ready"))
                            mm = products(ps[:, b, 0:TOK], tile(w, m, h, every)[kt:kt + 1], kt == 0, kt == KD - 1)
                        mm.then_inc(k.bank_done[b], 1)
                w = view(panel(), 0, KD, 256)
                b = bank()
                for t in range(4):
                    mm = products(ps[:, b, t * P:t * P + P],
                                  [(cut(h, ALL, kt, slice(t * P, t * P + P)), cut(w, ALL, kt, slice(0, P)))
                                   for kt in range(KD)])
                mm.then_inc(k.bank_done[b], 1)
                result(n, tile(w, 1, h, cols))
                for _ in range(2):
                    w = view(panel(), 0, KD, 256)
                    for m in range(2):
                        result(n, tile(w, m, h, cols))
                result(n, tile(view(panel(), 0, KD, 256), 0, h, cols))
                for _ in range(2):
                    w = view(panel(), 0, KD, 256)
                    for m in range(2):
                        last = result(n, tile(w, m, h, cols))
                return last

            def fourier(l, qg_done):
                pe.wait_ge(*k.moved(qg_done))
                todo = [(half, g) for half in ((0, 1) if l == 0 else (1,)) for g in range(4)]
                first = []
                for u in range(len(todo) + 1):
                    if u < len(todo):
                        half, g = todo[u]
                        b = bank()
                        for t in range(2):
                            c0 = HALVES[half][0] + t * P
                            mm = products(ps[:, b, t * 2 * P:(t + 1) * 2 * P], [(fin[:, g, c0:c0 + P], dft_d)])
                        mm.then_inc(k.bank_done[b], 1)
                        first.append(T.last())
                    if u >= 1:
                        pe.wait_ge(*k.moved(first[u - 1]))
                        f = dft1[:, (u - 1) % 2]
                        result(SEQ, [(f[:, t, 0:P], cos_s[:, t, :]) for t in range(2)]
                               + [(f[:, t, P:2 * P], nsin_s[:, t, :]) for t in range(2)])

            def qk_norm(cols):
                n = cols.stop - cols.start
                pe.wait_ge(S["squared_qk"], T.next("squared_qk", 4))
                result(TOK, [(ones, sqk[:, SQ_CKV + j, :]) for j in range(2)])
                result(TOK, [(pair, sqk[:, SQ_KG, :])])
                result(n, [(ones, sqk[:, SQ_CQ + j, cols]) for j in range(2)])
                for c in range(4):
                    result(n, [(pair, sqk[:, SQ_QG + c, cols])])

            def heads(cols):
                n = cols.stop - cols.start
                every = slice(0, TOK)
                w = panel()
                uk, uv = view(w, 0, 2, 512), view(w, 1024, 2, 512)
                pe.wait_ge(S["latent_split"], T.next("latent_split"))
                for c in range(4):
                    result(TOK, tile(uk, c, ckv_split, every))
                for t4 in range(4):
                    result(512, [(cut(ckv_split, ALL, t, slice(t4 * P, t4 * P + P)), cut(uv, ALL, t, ALL))
                                 for t in range(2)])
                w = panel()
                uqn, uqr = view(w, 0, 2, 512), view(w, 1024, 2, 256)
                pe.wait_ge(S["latent_split"], T.next("latent_split"))
                for c in range(4):
                    result(n, tile(uqn, c, cq_split, cols))
                for j in range(2):
                    last = result(n, tile(uqr, j, cq_split, cols))
                return last

            def rope(qr_done):
                pe.wait_ge(S["normed"], T.next("normed", 4))
                pe.wait_ge(*k.moved(qr_done))
                for name, x in rotated:
                    result(SEQ, [(k.col(name), x[:, CTX:TOK])])

            def attention(l):
                todo = units(l)
                pe.wait_ge(S["roped"], T.next("roped"))
                pv = rows = None
                turned = {}
                for u in range(len(todo) + 2):
                    if l == 0 and u < (ADA - ADA_FIRST) // 2:
                        before, rows = rows, modulation()
                        if u >= 1:
                            mods_turned(before, u - 1)
                    elif l == 0 and u == (ADA - ADA_FIRST) // 2:
                        mods_turned(rows, u - 1)
                    if u < len(todo):
                        kind, half, c, a = todo[u]
                        keys = slice(0, HALVES[half][1])
                        for q in range(2):
                            c0 = HALVES[half][0] + q * P
                            qs = slice(c0, c0 + P)
                            at = slice(HD * a, HD * a + HD)
                            if kind == "m":
                                h = 2 * c + a
                                r0 = HD * a + ROPE * (c % 2)
                                rot = slice(r0, r0 + ROPE)
                                pairs = [(qn[at, c, qs], kn[at, c, keys]), (qr[rot, h // 4, qs], kr[rot, keys])]
                            else:
                                pairs = [(qg[at, c, qs], kg[at, keys])]
                            result(keys.stop, pairs)
                    if 1 <= u <= len(todo):
                        tt = HALVES[todo[u - 1][1]][1] // P
                        pe.wait_ge(S["prob_ready"], T.next("prob_ready"))
                        for q in range(2):
                            b = bank()
                            for t in range(tt):
                                mm = flip(ps[:, b, t * P:t * P + P], prob[:, (u - 1) % 2, q, t * P:t * P + P])
                            mm.then_inc(k.bank_done[b], 1)
                        turned[u - 1] = T.last()
                    if u >= 2:
                        kind, half, c, a = todo[u - 2]
                        tt = HALVES[half][1] // P
                        buf = u % 2
                        if a == 0:
                            pv = bank()
                        pe.wait_ge(*k.moved(turned[u - 2]))
                        at = slice(HD * a, HD * a + HD)
                        h = 2 * c + a
                        mm = products(ps[at, pv, 0:SEQ],
                                      [(vm[:, t, h * HD:h * HD + HD] if kind == "m" else vg[:, t, at],
                                        probT[:, buf, t, :]) for t in range(tt)])
                        if a == 1:
                            mm.then_inc(k.bank_done[pv], 1)

            def branches(cols):
                n = cols.stop - cols.start
                all_split = T.next("branch_split", 3)
                for c in range(2):
                    for g in range(3):
                        for j in range(2):
                            w = view(panel(), 0, KD, 256)
                            for m in range(2):
                                result(n, tile(w, m, k.h, cols))
                        w = view(panel(), 0, 4, 512)
                        pe.wait_ge(S["branch_split"], all_split)
                        for m in range(4):
                            result(n, tile(w, m, branch_split[g], cols))

            def mix_out(cols):
                n = cols.stop - cols.start
                for j in range(4):
                    w = view(panel(), 0, KD, 256)
                    for m in range(2):
                        b = bank()
                        for kt in range(KD):
                            if j == 0 and m == 0 and kt % 2 == 0:
                                pe.wait_ge(S["mixed_split"], T.next("mixed_split"))
                            mm = products(ps[:, b, 0:n], tile(w, m, mixed_split, cols)[kt:kt + 1], kt == 0, kt == KD - 1)
                        mm.then_inc(k.bank_done[b], 1)
                return T.last()

            def mlp(l, cols):
                n = cols.stop - cols.start

                def up(first=False):
                    for j in range(4):
                        w = view(panel(), 0, KD, 256)
                        for m in range(2):
                            b = bank()
                            for kt in range(KD):
                                if first and j == 0 and m == 0:
                                    pe.wait_ge(S["h_ready"], T.next("h_ready"))
                                mm = products(ps[:, b, 0:n], tile(w, m, k.h, cols)[kt:kt + 1], kt == 0, kt == KD - 1)
                            mm.then_inc(k.bank_done[b], 1)

                up(first=True)
                with pe.Fori(0, 3) as i, T.loop(i, 3, {"panel": 4, "tiles": 8}):
                    up()
                _, hid_lo, hid_hi = hidden(l)
                bs = []
                for kt in range(4 * KD):
                    if kt % 2 == 0:
                        w = view(panel(), 0, 2, D)
                    pe.wait_ge(S["hid_split"], T.next("hid_split"))
                    x = hid_hi[:, kt % HID_SLOTS, :], hid_lo[:, kt, :]
                    for m in range(KD):
                        if kt == 0:
                            bs.append(bank())
                        mm = products(ps[:, bs[m], 0:n], [(cut(w, ALL, kt % 2, slice(m * P, m * P + P)), x)],
                                      kt == 0, kt == 4 * KD - 1)
                        if kt == 4 * KD - 1:
                            mm.then_inc(k.bank_done[bs[m]], 1)
                    if kt < 4 * KD - HID_SLOTS:
                        mm.then_inc(S["hid_used"], 1)
                return T.last()

            x_moved = last_results()
            pe.wait_ge(S["silu_split"], T.next("silu_split"))
            rows = modulation()
            for group in range(1, ADA_FIRST // 2):
                before, rows = rows, modulation()
                mods_turned(before, group - 1)
            mods_turned(rows, group)
            for l in range(LAYERS):
                cols = slice(0 if l == 0 else CTX, TOK)
                norm(slice(0, TOK), x_moved if l == 0 else None)
                fourier(l, project(cols))
                qk_norm(cols)
                rope(heads(cols))
                attention(l)
                branches(cols)
                mix_out(cols)
                norm(cols, last_results())
                norm(cols, None)
                mlp(l, cols)
                norm(cols, last_results())

            h2 = k.h2

            def rms():
                sq = area(SQ2, KD, SEQ)
                b = bank()
                for kt in range(KD):
                    pe.wait_ge(S["squared"], T.next("squared"))
                    mm = products(ps[:, b, 0:SEQ], [(ones, sq[:, kt, :])], kt == 0, kt == KD - 1)
                mm.then_inc(k.bank_done[b], 1)

            def ffn():
                def pair(first=False):
                    for x in range(2):
                        w = view(panel(), 0, KD, 256)
                        for m in range(2):
                            b = bank()
                            for kt in range(KD):
                                if first and x == 0 and m == 0:
                                    pe.wait_ge(S["h_ready"], T.next("h_ready"))
                                mm = products(ps[:, b, 0:SEQ], tile(w, m, h2, ALL)[kt:kt + 1], kt == 0, kt == KD - 1)
                            mm.then_inc(k.bank_done[b], 1)

                pair(first=True)
                with pe.Fori(0, 5) as i, T.loop(i, 5, {"panel": 4, "tiles": 8}):
                    for j in range(2):
                        pair()
                bs = []
                for kt in range(FT):
                    if kt % 2 == 0:
                        w = view(panel(), 0, 2, D)
                        pe.wait_ge(S["act2_split"], T.next("act2_split"))
                    for m in range(KD):
                        if kt == 0:
                            bs.append(bank())
                        mm = products(ps[:, bs[m], 0:SEQ], [(cut(w, ALL, kt % 2, slice(m * P, m * P + P)),
                                                             cut(act2_split, ALL, kt, ALL))], kt == 0, kt == FT - 1)
                        if kt == FT - 1:
                            mm.then_inc(k.bank_done[bs[m]], 1)

            def wide(panels=2):
                for _ in range(panels):
                    w = view(panel(), 0, KD, 256)
                    for m in range(2):
                        result(SEQ, tile(w, m, h2, ALL))

            def by_token(w, c0, n):
                b = bank()
                for t in range(2):
                    mm = products(ps[:, b, t * n:t * n + n],
                                  [(cut(h2, ALL, kt, slice(t * P, t * P + P)), cut(w, ALL, kt, slice(c0, c0 + n)))
                                   for kt in range(KD)])
                mm.then_inc(k.bank_done[b], 1)
                return T.last()

            def in_projections():
                w = view(panel(), 0, KD, 256)
                for m in range(2):
                    b = bank()
                    for kt in range(KD):
                        if m == 0:
                            pe.wait_ge(S["h_ready"], T.next("h_ready"))
                        mm = products(ps[:, b, 0:SEQ], tile(w, m, h2, ALL)[kt:kt + 1], kt == 0, kt == KD - 1)
                    mm.then_inc(k.bank_done[b], 1)
                wide(1)
                wide()
                for _ in range(2):
                    w = view(panel(), 0, KD, 256)
                    result(SEQ, tile(w, 0, h2, ALL))
                    by_token(w, P, P)
                w = view(panel(), 0, KD, 256)
                b = bank()
                products(ps[0:3 * HEADS, b, 0:SEQ], [(cut(w, ALL, kt, slice(0, 3 * HEADS)), cut(h2, ALL, kt, ALL))
                                                     for kt in range(KD)]).then_inc(k.bank_done[b], 1)
                b = bank()
                w = view(panel(), 0, KD, 256)
                products(ps[0:16, b, 0:SEQ], [(cut(w, ALL, kt, slice(0, 16)), cut(h2, ALL, kt, ALL)) for kt in range(KD)]) \
                    .then_inc(k.bank_done[b], 1)
                pe.wait_ge(S["small_in"], T.next("small_in", 48))
                pe.wait_ge(*k.moved(T.last()))
                for h in range(GH):
                    result(SEQ, [(w_decay[0:16, h * P:h * P + P], area(ALR, SEQ)[0:16, :])])
                for x in range(2):
                    b = bank()
                    pe.wait_ge(S["blocks_split"], T.next("blocks_split"))
                    for half in range(2):
                        w1 = view(panel(), 0, 8, 256)
                        mm = products(ps[0:2 * NCMP, b, 0:256], [(cut(k.kbuf_split[x], ALL, 8 * half + j, ALL), cut(w1, ALL, j, ALL))
                                                                 for j in range(8)], half == 0, half == 1)
                    mm.then_inc(k.bank_done[b], 1)
                rows = T.last()
                w = view(panel(), 0, KD, 256)
                result(SEQ, tile(w, 0, h2, ALL))
                b = bank()
                pe.wait_ge(*k.moved(rows))
                result(SEQ, tile(w, 1, h2, ALL))
                for x in range(2):
                    for m in range(2):
                        o = (2 * x + m) * 2 * NCMP
                        pe.transpose(ps[:, b, o:o + 2 * NCMP], hid_rows[:, x, m * P:m * P + P],
                                     ident[0:2 * NCMP, 0:2 * NCMP])
                for t in range(2):
                    o = 8 * NCMP + t * 3 * HEADS
                    mm = pe.transpose(ps[:, b, o:o + 3 * HEADS], gate_rows[:, t * P:t * P + P],
                                      ident[0:3 * HEADS, 0:3 * HEADS])
                mm.then_inc(k.bank_done[b], 1)
                turned = (b, T.value(f"bank{b}"))
                wide(1)
                pe.wait_ge(*k.moved(turned))
                b = bank()
                for g in range(2):
                    products(ps[HD * g:HD * g + HD, b, 0:NCMP],
                             [(w_cmp[0][:, m, :], hidk[:, m, g * NCMP:(g + 1) * NCMP]) for m in range(2)])
                for g in range(2):
                    mm = products(ps[:, b, (g + 1) * HD:(g + 2) * HD],
                                  [(k.hid_v[:, m, g].rearrange("p r n -> p (r n)"), w_cmp[1][:, m, :]) for m in range(2)])
                mm.then_inc(k.bank_done[b], 1)
                wide(2)
                for _ in range(4):
                    by_token(view(panel(), 0, KD, 256), 0, 256)
                wide(4)

            def sparse_attention():
                pe.wait_ge(*k.moved(T.last()))
                for a in range(2):
                    b = bank()
                    at = slice(HD * a, HD * a + HD)
                    for q in range(2):
                        for c in range(4):
                            o = (q * 4 + c) * NCMP
                            mm = products(ps[:, b, o:o + NCMP], [(qa[at, c, q * P:q * P + P], kcmp[at, :])])
                    mm.then_inc(k.bank_done[b], 1)
                pv, turned = None, {}
                for u in range(HEADS + 2):
                    if u < HEADS:
                        c, a = u // 2, u % 2
                        at = slice(HD * a, HD * a + HD)
                        for q in range(2):
                            n = (q + 1) * P
                            b = bank()
                            for j, key in enumerate((kslc, kwin)):
                                mm = products(ps[:, b, j * n:j * n + n],
                                              [(qa[at, c, q * P:q * P + P], key[at, 0:n])])
                            mm.then_inc(k.bank_done[b], 1)
                    if 1 <= u <= HEADS:
                        pe.wait_ge(S["nsa_prob"], T.next("nsa_prob"))
                        for blocks in (range(4), range(4, 6)):
                            b = bank()
                            for j, blk in enumerate(blocks):
                                mm = flip(ps[:, b, j * P:j * P + P], prob2[:, (u - 1) % 2, blk * P:blk * P + P])
                            mm.then_inc(k.bank_done[b], 1)
                        turned[u - 1] = T.last()
                    if u == 2:
                        pe.wait_ge(S["cmp_prob"], T.next("cmp_prob"))
                        b = bank()
                        for q in range(2):
                            for g in range(2):
                                o = (q * 2 + g) * P
                                mm = flip(ps[:, b, o:o + P],
                                          k.p_cmp[:, q, 4 * g:4 * g + 4, :].rearrange("p h n -> p (h n)"))
                        mm.then_inc(k.bank_done[b], 1)
                        pe.wait_ge(*k.moved(T.last()))
                    if u >= 2:
                        c, a = (u - 2) // 2, u % 2
                        at = slice(HD * a, HD * a + HD)
                        if a == 0:
                            pv = bank()
                        pe.wait_ge(*k.moved(turned[u - 2]))
                        row = slice(32 * c, 32 * c + NCMP)
                        pt = probT2[:, u % 2]
                        products(ps[at, pv, 0:P], [(vslc[:, 0, at], pt[:, 0, :]), (vwin[:, 0, at], pt[:, 1, :]),
                                                   (vcmp[row, a, :], pcT[row, a, :])])
                        mm = products(ps[at, pv, P:2 * P],
                                      [(vslc[:, t, at], pt[:, 2 + t, :]) for t in range(2)]
                                      + [(vwin[:, t, at], pt[:, 4 + t, :]) for t in range(2)]
                                      + [(vcmp[row, a, :], pcT[row, 2 + a, :])])
                        if a == 1:
                            mm.then_inc(k.bank_done[pv], 1)

            def linear_attention():
                pe.wait_ge(S["gla_in"], T.next("gla_in"))
                for t in range(2):
                    b = bank()
                    for h in range(GH):
                        mm = flip(ps[:, b, h * P:h * P + P], kb[:, h, t * P:t * P + P])
                    mm.then_inc(k.bank_done[b], 1)
                k_turned = T.last()
                for t in range(2):
                    b = bank()
                    for h in range(GH):
                        mm = products(ps[:, b, h * P:h * P + P], [(kin[:, h, t * P:t * P + P], qb[:, h, t * P:t * P + P])])
                    mm.then_inc(k.bank_done[b], 1)
                pe.wait_ge(*k.moved(k_turned))
                for n in range(NCH - 1):
                    rows = slice(CHUNK * (n % 2), CHUNK * (n % 2) + CHUNK)
                    for hp in range(2):
                        b = bank()
                        for j in range(2):
                            h = 2 * hp + j
                            mm = products(ps[:, b, j * DV:j * DV + DV],
                                          [(kst[rows, n // 2, h, :], vb[rows, n // 2, h * DV:h * DV + DV])])
                        mm.then_inc(k.bank_done[b], 1)
                pe.wait_ge(*k.moved(T.last()))
                for h in range(GH):
                    for v in range(2):
                        b = bank()
                        c0 = h * DV + v * P
                        for t in range(2):
                            products(ps[:, b, t * P:t * P + P], [(vb[:, t, c0:c0 + P], att[:, t, h, :])],
                                     start=t == 0, stop=False)
                        for n in range(1, NCH):
                            mm = products(ps[:, b, n * CHUNK:(n + 1) * CHUNK],
                                          [(state[:, n - 1, h, v * P:v * P + P], qb[:, h, n * CHUNK:(n + 1) * CHUNK])],
                                          start=False, stop=n == NCH - 1)
                        mm.then_inc(k.bank_done[b], 1)
                pe.wait_ge(S["gla_out"], T.next("gla_out"))
                sq = area(SQO, KD, SEQ)
                for hp in range(2):
                    b = bank()
                    for j in range(2):
                        h = 2 * hp + j
                        mm = products(ps[:, b, j * SEQ:j * SEQ + SEQ], [(ones, sq[:, 2 * h + v, :]) for v in range(2)])
                    mm.then_inc(k.bank_done[b], 1)

            def merge():
                ready = T.next("merge_in")
                for c in range(2):
                    wide(4)
                    w = view(panel(), 0, 4, 512)
                    pe.wait_ge(S["merge_in"], ready)
                    for m in range(4):
                        result(SEQ, tile(w, m, oa_split, ALL))
                    for j in range(2):
                        w = view(panel(), 0, KD, 256)
                        for m in range(2):
                            result(SEQ, tile(w, m, ob_split, ALL))
                for j in range(4):
                    w = view(panel(), 0, KD, 256)
                    for m in range(2):
                        b = bank()
                        for kt in range(KD):
                            if j == 0 and m == 0 and kt % 2 == 0:
                                pe.wait_ge(S["merged"], T.next("merged"))
                            mm = products(ps[:, b, 0:SEQ], tile(w, m, mixed2_split, ALL)[kt:kt + 1], kt == 0, kt == KD - 1)
                        mm.then_inc(k.bank_done[b], 1)

            with pe.Fori(0, LAYERS) as l, T.loop(l, LAYERS, PER_LAYER["pe"]):
                rms()
                ffn()
                rms()
                in_projections()
                sparse_attention()
                linear_attention()
                merge()
                rms()
                ffn()
            rms()
            pe.wait_ge(S["final_ready"], T.next("final_ready"))
            for t in range(2):
                for g in range(2):
                    b = bank()
                    for j in range(4):
                        mm = flip(ps[:, b, j * P:j * P + P], plain2[:, 4 * g + j, t * P:t * P + P])
                    mm.then_inc(k.bank_done[b], 1)

        @block.gpsimd
        def _(pool):
            with pool.Fori(0, (PANELS_1 + LAYERS * PANELS_2) // SLOTS) as i:
                for s in range(SLOTS):
                    pool.wait_ge(k.hi_ready[s], i + 1)
                    pool.tensor_tensor(k.ring_lo[s][:, :], k.ring[s][:, :], k.ring_hi[s][:, :], ALU.subtract) \
                        .then_inc(k.lo_ready[s], 1)

        @block.scalar
        def _(act):
            T = Tally()

            def skip(n):
                for _ in range(n):
                    T.take()
                return T.last()

            eps, one = k.col("eps"), k.col("one")

            def split():
                s, rounds, _ = T.panel()
                act.wait_ge(k.panel_landed[s], rounds * LAND)
                act.activation(k.ring_hi[s][:, :], k.ring[s][:, :], ACT.Copy).then_inc(k.hi_ready[s], 1)

            skip(2)
            act.wait_ge(*k.moved(skip(1)))
            for s, name in enumerate(("c_ctx", "c")):
                t, r, n = VEC[name]
                ins = act.activation(k.silu_c[:, :, s], k.vecT[:, t * P + r:t * P + r + n], ACT.Silu)
            ins.then_inc(S["silu_plain"], 1)
            act.wait_ge(S["silu_plain"], T.next("silu_plain"))
            act.activation(k.silu_split[0], k.silu_c, ACT.Copy).then_inc(S["silu_rounded"], 1)
            skip(KD)
            split()
            split()

            def modulation(group):
                for _ in range(2):
                    split()
                b, v = T.take()
                act.wait_ge(k.bank_done[b], v)
                act.activation(k.mod_rows[group % 2], ps[0:2, b, :], ACT.Copy).then_inc(k.bank_read[b], 1)

            def norm(centred, cols, affine=None):
                n = cols.stop - cols.start
                skip(1)
                for kt in range(KD):
                    act.wait_ge(S["centred"], T.next("centred"))
                    act.activation(area(SQ, KD, TOK)[:, kt, cols], centred[:, kt, cols], ACT.Square) \
                        .then_inc(S["squared"], 1)
                b, v = T.take()
                act.wait_ge(k.bank_done[b], v)
                act.activation(area(STD, TOK)[:, cols], ps[:, b, 0:n],
                               ACT.Sqrt, scale=1.0 / D, bias=eps).then_inc(k.bank_read[b], 1)
                if affine:
                    for kt in range(KD + 1):
                        if kt < KD:
                            act.wait_ge(S["scaled"], T.next("scaled"))
                            for part, scale, shift in affine(kt):
                                ins = act.activation(centred[:, kt, part], centred[:, kt, part], ACT.Identity,
                                                     scale=scale, bias=shift)
                            ins.then_inc(S["h_plain"], 1)
                        if kt >= 1:
                            act.wait_ge(S["h_plain"], T.next("h_plain"))
                            act.activation(k.h[0][:, kt - 1, cols], centred[:, kt - 1, cols], ACT.Copy) \
                                .then_inc(S["h_rounded"], 1)

            def project(cols):
                n = cols.stop - cols.start

                split()
                for m in range(2):
                    b, v = T.take()
                    act.wait_ge(k.bank_done[b], v)
                    act.activation(ckv[:, m, :], ps[:, b, 0:TOK], ACT.Copy).then_inc(k.bank_read[b], 1)
                act.wait_ge(*k.moved(T.last()))
                act.activation(sqk[:, SQ_CKV:SQ_CKV + 2, :], ckv, ACT.Square).then_inc(S["squared_qk"], 1)
                split()
                for x in (kr, kg):
                    b, v = T.take()
                    act.wait_ge(k.bank_done[b], v)
                    act.activation(x, ps[:, b, 0:TOK], ACT.Copy).then_inc(k.bank_read[b], 1)
                act.wait_ge(*k.moved(T.last()))
                act.activation(sqk[:, SQ_KG, :], kg, ACT.Square).then_inc(S["squared_qk"], 1)
                split()
                b, v = T.take()
                act.wait_ge(k.bank_done[b], v)
                act.activation(vg, ps[:, b, :].rearrange("p (t c) -> p t c", t=4),
                               ACT.Copy).then_inc(k.bank_read[b], 1)
                into = [fin[:, m, cols] for m in range(4)] + [cq[:, m, cols] for m in range(2)]
                for j, o in enumerate(into):
                    if j in (1, 3, 5):
                        split()
                    b, v = T.take()
                    act.wait_ge(k.bank_done[b], v)
                    act.activation(o, ps[:, b, 0:n], ACT.Copy).then_inc(k.bank_read[b], 1)
                act.wait_ge(*k.moved(T.last()))
                act.activation(sqk[:, SQ_CQ:SQ_CQ + 2, cols], cq[:, :, cols], ACT.Square).then_inc(S["squared_qk"], 1)
                for m in range(4):
                    if m % 2 == 0:
                        split()
                    b, v = T.take()
                    act.wait_ge(k.bank_done[b], v)
                    act.activation(qg[:, m, cols], ps[:, b, 0:n], ACT.Copy).then_inc(k.bank_read[b], 1)
                act.wait_ge(*k.moved(T.last()))
                act.activation(sqk[:, SQ_QG:SQ_QG + 4, cols], qg[:, :, cols], ACT.Square).then_inc(S["squared_qk"], 1)

            def fourier(l):
                todo = [(half, g) for half in ((0, 1) if l == 0 else (1,)) for g in range(4)]
                for u in range(len(todo) + 1):
                    if u < len(todo):
                        skip(1)
                    if u >= 1:
                        half, g = todo[u - 1]
                        b, v = T.take()
                        act.wait_ge(k.bank_done[b], v)
                        act.activation(fin[:, g, slice(*HALVES[half])], ps[:, b, 0:SEQ],
                                       ACT.Copy).then_inc(k.bank_read[b], 1)

            def qk_norm(cols):
                n = cols.stop - cols.start
                for tile, m, w, cs in ((STD_CKV, TOK, RANK, slice(0, TOK)), (SQ_KG, TOK, HD, slice(0, TOK)),
                                       (SQ_CQ, n, RANK, cols)):
                    b, v = T.take()
                    act.wait_ge(k.bank_done[b], v)
                    act.activation(sqk[:, tile, cs], ps[:, b, 0:m], ACT.Sqrt, scale=1.0 / w, bias=eps) \
                        .then_inc(k.bank_read[b], 1)
                act.wait_ge(S["normed"], T.next("normed"))
                act.activation(ckv_split[0], ckv, ACT.Copy).then_inc(S["latent_rounded"], 1)
                act.wait_ge(S["normed"], T.next("normed", 2))
                act.activation(cq_split[0][:, :, cols], cq[:, :, cols], ACT.Copy).then_inc(S["latent_rounded"], 1)
                T.next("normed")
                for c in range(4):
                    b, v = T.take()
                    act.wait_ge(k.bank_done[b], v)
                    act.activation(sqk[:, SQ_QG + c, cols], ps[:, b, 0:n],
                                   ACT.Sqrt, scale=1.0 / HD, bias=eps).then_inc(k.bank_read[b], 1)

            def heads(cols):
                n = cols.stop - cols.start
                split()
                for c in range(4):
                    b, v = T.take()
                    act.wait_ge(k.bank_done[b], v)
                    act.activation(kn[:, c, :], ps[:, b, 0:TOK], ACT.Copy).then_inc(k.bank_read[b], 1)
                for t in range(4):
                    b, v = T.take()
                    act.wait_ge(k.bank_done[b], v)
                    act.activation(vm[:, t, :], ps[:, b, 0:512], ACT.Copy).then_inc(k.bank_read[b], 1)
                split()
                for c in range(4):
                    b, v = T.take()
                    act.wait_ge(k.bank_done[b], v)
                    act.activation(qn[:, c, cols], ps[:, b, 0:n], ACT.Copy).then_inc(k.bank_read[b], 1)
                for j in range(2):
                    b, v = T.take()
                    act.wait_ge(k.bank_done[b], v)
                    act.activation(qr[:, j, cols], ps[:, b, 0:n], ACT.Copy).then_inc(k.bank_read[b], 1)
                skip(len(rotated))

            def attention(l):
                todo = units(l)
                pv = None
                for u in range(len(todo) + 2):
                    if l == 0 and u < (ADA - ADA_FIRST) // 2:
                        modulation(u)
                    if l == 0 and 1 <= u <= (ADA - ADA_FIRST) // 2:
                        skip(1)
                    if u < len(todo):
                        kind, half, c, a = todo[u]
                        buf = u % 2
                        n = HALVES[half][1]
                        tiles = [T.take() for _ in range(2)]
                        act.wait_ge(S["row_max"], T.next("row_max"))
                        for q, (b, v) in enumerate(tiles):
                            act.wait_ge(k.bank_done[b], v)
                            act.activation(prob[:, buf, q, 0:n], ps[:, b, 0:n], ACT.Exp,
                                           bias=k.stat[:, 8 * buf + q:8 * buf + q + 1],
                                           scale=MLA_SCALE if kind == "m" else GQA_SCALE,
                                           accum_out=k.stat[:, 8 * buf + 2 + q:8 * buf + 3 + q]) \
                                .then_inc(k.bank_read[b], 1)
                    if 1 <= u <= len(todo):
                        tt = HALVES[todo[u - 1][1]][1] // P
                        for q in range(2):
                            b, v = T.take()
                            act.wait_ge(k.bank_done[b], v)
                            act.activation(probT[:, (u - 1) % 2, 0:tt, q * P:q * P + P], ps[:, b, 0:tt * P].rearrange("p (t c) -> p t c", t=tt),
                                           ACT.Copy).then_inc(k.bank_read[b], 1)
                    if u >= 2 and todo[u - 2][3] == 0:
                        pv = skip(1)
                return pv

            def branches(l, cols, attended):
                n = cols.stop - cols.start
                act.wait_ge(*k.moved(attended))
                for x, x_split in zip(branch, branch_split):
                    act.activation(x_split[0][:, :, cols], x[:, :, cols], ACT.Copy).then_inc(S["branch_rounded"], 1)
                for c in range(2):
                    for g in range(3):
                        for m in range(4):
                            if m % 2 == 0:
                                split()
                            used = (T.bank + 4) % BANKS
                            act.wait_ge(k.bank_read[used], T.value(f"bank{used}"))
                            b, v = T.take()
                            act.wait_ge(k.bank_done[b], v)
                            act.activation(gate(m)[:, cols], ps[:, b, 0:n], ACT.Sigmoid,
                                           bias=k.vec("b_gate", (l * 3 + g) * KD + 4 * c + m)).then_inc(k.bank_read[b], 1)
                        split()
                        skip(4)

            def mix_out(cols):
                act.wait_ge(S["gated"], T.next("gated", KD))
                for j in range(4):
                    two = slice(2 * j, 2 * j + 2)
                    act.activation(mixed_split[0][:, two, cols], mixed[:, two, cols], ACT.Copy) \
                        .then_inc(S["mixed_rounded"], 1)
                for j in range(4):
                    split()
                    skip(2)

            def mlp(l, cols):
                hid, _, hid_hi = hidden(l)

                def up():
                    for j in range(4):
                        split()
                        for m in range(2):
                            used = (T.bank + BANKS - HID_SLOTS) % BANKS
                            act.wait_ge(k.bank_read[used], T.value(f"bank{used}"))
                            b, v = T.take()
                            act.wait_ge(k.bank_done[b], v)
                            act.activation(relu(l, 2 * j + m), ps[:, b, 0:TOK if l == 0 else SEQ], ACT.Relu) \
                                .then_inc(S["relu_ready"], 1)

                up()
                with act.Fori(0, 3) as i, T.loop(i, 3, {"panel": 4, "tiles": 8}):
                    up()
                act.wait_ge(*k.moved(T.last()))
                for kt in range(4 * KD):
                    if kt >= HID_SLOTS:
                        act.wait_ge(S["hid_used"], T.next("hid_used"))
                    act.activation(hid_hi[:, kt % HID_SLOTS, :], hid[:, kt, :], ACT.Copy).then_inc(S["hid_rounded"], 1)
                    if kt % 2 == 1 and (l == 0 or kt < 4 * KD - 4):
                        split()
                skip(KD)

            for group in range(ADA_FIRST // 2):
                modulation(group)
                if group >= 1:
                    skip(1)
            skip(1)
            for l in range(LAYERS):
                cols = slice(0 if l == 0 else CTX, TOK)
                halves, mod = (0, 1) if l == 0 else (1,), l * MODS
                norm(plain, slice(0, TOK), modulated(mod + SC1, mod + SH1, (0, 1)))
                project(cols)
                fourier(l)
                qk_norm(cols)
                heads(cols)
                branches(l, cols, attention(l))
                mix_out(cols)
                norm(k.xT, cols)
                norm(plain, cols, modulated(mod + SC2, mod + SH2, halves))
                mlp(l, cols)
                norm(k.xT, cols)

            def rms(halved=True, split_first=False):
                for kt in range(KD):
                    b = (T.bank + kt) % BANKS
                    act.wait_ge(k.bank_read[b], T.value(f"bank{b}"))
                    act.activation(area(SQ2, KD, SEQ)[:, kt, :], y[:, kt, :], ACT.Square).then_inc(S["squared"], 1)
                if split_first:
                    split()
                    split()
                b, v = T.take()
                act.wait_ge(k.bank_done[b], v)
                act.activation(area(STD2, SEQ), ps[:, b, 0:SEQ],
                               ACT.Sqrt, scale=1.0 / D, bias=eps).then_inc(k.bank_read[b], 1)
                if halved:
                    for kt in range(KD):
                        act.wait_ge(S["h_plain"], T.next("h_plain"))
                        act.activation(k.h2[0][:, kt, :], plain2[:, kt, :], ACT.Copy).then_inc(S["h_rounded"], 1)

            def ffn(ahead):
                def pair(j):
                    split()
                    skip(2)
                    split()
                    for m in range(2):
                        b, v = T.take()
                        act.wait_ge(k.bank_done[b], v)
                        act.activation(area(SILU2, 2, 2, SEQ)[:, j % 2, m, :], ps[:, b, 0:SEQ],
                                       ACT.Silu).then_inc(k.bank_read[b], 1)

                pair(0)
                with act.Fori(0, 5) as i, T.loop(i, 5, {"panel": 4, "tiles": 8}):
                    for j in range(2):
                        pair(j + 1)
                for j in range(FT // 2):
                    if ahead or j < FT // 2 - 2:
                        split()
                skip(KD)

            def in_projections():
                for m in range(4):
                    if m % 2 == 0:
                        split()
                    b, v = T.take()
                    act.wait_ge(k.bank_done[b], v)
                    act.activation(qa[:, m, :], ps[:, b, 0:SEQ],
                                   ACT.Copy, scale=HD ** -0.5).then_inc(k.bank_read[b], 1)
                for _ in range(2):
                    split()
                    skip(2)
                two = lambda b: ps[:, b, 0:2 * P].rearrange("p (t c) -> p t c", t=2)
                split()
                b, v = T.take()
                act.wait_ge(k.bank_done[b], v)
                act.activation(kslc, ps[:, b, 0:SEQ], ACT.Copy).then_inc(k.bank_read[b], 1)
                b, v = T.take()
                act.wait_ge(k.bank_done[b], v)
                act.activation(vslc, two(b), ACT.Copy).then_inc(k.bank_read[b], 1)
                split()
                b, v = T.take()
                act.wait_ge(k.bank_done[b], v)
                act.activation(kwin, ps[:, b, 0:SEQ], ACT.Copy).then_inc(k.bank_read[b], 1)
                b, v = T.take()
                act.wait_ge(k.bank_done[b], v)
                act.activation(vwin, two(b), ACT.Copy).then_inc(k.bank_read[b], 1)
                split()
                b, v = T.take()
                act.wait_ge(k.bank_done[b], v)
                act.activation(gate_rows, ps[0:3 * HEADS, b, 0:SEQ], ACT.Sigmoid).then_inc(k.bank_read[b], 1)
                split()
                b, v = T.take()
                act.wait_ge(k.bank_done[b], v)
                act.activation(area(ALR, SEQ)[0:16, :], ps[0:16, b, 0:SEQ], ACT.Copy).then_inc(k.bank_read[b], 1)
                skip(GH)
                for x in range(2):
                    for _ in range(2):
                        split()
                    b, v = T.take()
                    act.wait_ge(k.bank_done[b], v)
                    act.activation(hid_rows[:, x, :], ps[0:2 * NCMP, b, 0:256], ACT.Silu).then_inc(k.bank_read[b], 1)
                act.wait_ge(S["minus_abs_z"], T.next("minus_abs_z"))
                act.activation(t1, t1, ACT.Exp).then_inc(S["act_step"], 1)
                act.wait_ge(S["act_step"], T.next("act_step"))
                act.activation(t1, t1, ACT.Ln, bias=one).then_inc(S["log1p_ready"], 1)
                def q_moved(m):
                    b, v = T.take()
                    act.wait_ge(k.bank_done[b], v)
                    act.activation(qb[:, m, :], ps[:, b, 0:SEQ], ACT.Copy, scale=P ** -0.5).then_inc(k.bank_read[b], 1)

                split()
                q_moved(0)
                b, v = T.take()
                q_moved(1)
                act.wait_ge(k.bank_done[b], v)
                act.activation(hidk, ps[:, b, 0:4 * NCMP].rearrange("p (m n) -> p m n", m=2), ACT.Copy)
                for m in range(2):
                    src = ps[:, b, (2 + m) * 2 * NCMP:(3 + m) * 2 * NCMP].rearrange("p (g n) -> p g n", g=2)
                    act.activation(k.hid_v[:, m, :, :, 0:NCMP], src.unsqueeze(2).broadcast_to([P, 2, 4, NCMP]), ACT.Copy)
                act.activation(ga, ps[:, b, 8 * NCMP:8 * NCMP + 6 * HEADS].rearrange("p (t c) -> p t c", t=2), ACT.Copy) \
                    .then_inc(k.bank_read[b], 1)
                split()
                q_moved(2)
                q_moved(3)
                b, v = T.take()
                act.wait_ge(k.bank_done[b], v)
                act.activation(kcmp, ps[:, b, 0:NCMP], ACT.Copy)
                act.activation(vcmp, ps[:, b, HD:3 * HD].rearrange("p (g c) -> p g c", g=2),
                               ACT.Copy).then_inc(k.bank_read[b], 1)
                for m in range(4):
                    if m % 2 == 0:
                        split()
                    b, v = T.take()
                    act.wait_ge(k.bank_done[b], v)
                    act.activation(kb[:, m, :], ps[:, b, 0:SEQ], ACT.Copy).then_inc(k.bank_read[b], 1)
                act.wait_ge(S["decay_ready"], T.next("decay_ready"))
                act.activation(z, t1, ACT.Exp, scale=1.0 / TAU).then_inc(S["edecay"], 1)
                for c in range(4):
                    split()
                    b, v = T.take()
                    act.wait_ge(k.bank_done[b], v)
                    act.activation(vb[:, :, c * 256:c * 256 + 256], ps[:, b, :].rearrange("p (t c) -> p t c", t=2),
                                   ACT.Copy).then_inc(k.bank_read[b], 1)
                act.wait_ge(S["edecay_used"], T.next("edecay_used"))
                act.activation(z, t1, ACT.Exp, scale=-1.0 / TAU).then_inc(S["edecay"], 1)
                for m in range(4):
                    if m % 2 == 0:
                        split()
                    b, v = T.take()
                    act.wait_ge(k.bank_done[b], v)
                    act.activation(rb[:, m, :], ps[:, b, 0:SEQ], ACT.Silu).then_inc(k.bank_read[b], 1)
                act.wait_ge(S["decay_ready"], T.next("decay_ready"))
                act.activation(z, z, ACT.Exp, scale=1.0 / TAU).then_inc(S["edecay"], 1)
                for m in range(4, KD):
                    if m % 2 == 0:
                        split()
                    b, v = T.take()
                    act.wait_ge(k.bank_done[b], v)
                    act.activation(rb[:, m, :], ps[:, b, 0:SEQ], ACT.Silu).then_inc(k.bank_read[b], 1)

            def sparse_attention():
                skip(2)
                act.wait_ge(S["cmp_max"], T.next("cmp_max"))
                pc = k.p_cmp[:, :, :, 0:NCMP]
                act.activation(pc, pc, ACT.Exp).then_inc(S["cmp_exp"], 1)
                for u in range(HEADS + 2):
                    if u < HEADS:
                        skip(2)
                        buf = u % 2
                        act.wait_ge(S["nsa_max"], T.next("nsa_max"))
                        for j in range(4):
                            n = P if j < 2 else 2 * P
                            o = j * P if j < 2 else 2 * P + (j - 2) * 2 * P
                            p = prob2[:, buf, o:o + n]
                            ins = act.activation(p, p, ACT.Exp, bias=k.stat[:, 16 * buf + j:16 * buf + j + 1],
                                                 accum_out=k.stat[:, 16 * buf + 4 + j:16 * buf + 5 + j])
                        ins.then_inc(S["nsa_exp"], 1)
                    if 1 <= u <= HEADS:
                        for b0, n in ((0, 4), (4, 2)):
                            b, v = T.take()
                            act.wait_ge(k.bank_done[b], v)
                            act.activation(probT2[:, (u - 1) % 2, b0:b0 + n, :], ps[:, b, 0:n * P].rearrange("p (t c) -> p t c", t=n),
                                           ACT.Copy).then_inc(k.bank_read[b], 1)
                    if u == 2:
                        b, v = T.take()
                        act.wait_ge(k.bank_done[b], v)
                        act.activation(pcT, ps[:, b, :].rearrange("p (t c) -> p t c", t=4),
                                       ACT.Copy).then_inc(k.bank_read[b], 1)
                    if u >= 2 and u % 2 == 0:
                        skip(1)

            def linear_attention():
                for t in range(2):
                    b, v = T.take()
                    act.wait_ge(k.bank_done[b], v)
                    act.activation(kst[:, t], ps[:, b, :].rearrange("p (t c) -> p t c", t=4),
                                   ACT.Copy).then_inc(k.bank_read[b], 1)
                skip(2 + 2 * (NCH - 1))
                for j in range(KD):
                    b, v = T.take()
                    act.wait_ge(k.bank_done[b], v)
                    act.activation(ob[:, j, :], ps[:, b, 0:SEQ], ACT.Copy).then_inc(k.bank_read[b], 1)
                    last = T.last()
                act.wait_ge(*k.moved(last))
                act.activation(area(SQO, KD, SEQ), ob, ACT.Square).then_inc(S["gla_out"], 1)
                for hp in range(2):
                    b, v = T.take()
                    act.wait_ge(k.bank_done[b], v)
                    act.activation(t1[:, 2 * hp:2 * hp + 2, :], ps[:, b, :].rearrange("p (h c) -> p h c", h=2),
                                   ACT.Sqrt, scale=1.0 / DV, bias=eps).then_inc(k.bank_read[b], 1)

            def merge():
                for c in range(2):
                    for g in range(2):
                        for m in range(4):
                            if m % 2 == 0:
                                split()
                            b, v = T.take()
                            act.wait_ge(k.bank_done[b], v)
                            act.activation(area(MGATE, 2, 4, SEQ)[:, g, m, :], ps[:, b, 0:SEQ],
                                           ACT.Sigmoid).then_inc(k.bank_read[b], 1)
                    split()
                    skip(4)
                    for j in range(2):
                        split()
                        skip(2)
                for _ in range(4):
                    split()
                    skip(2)

            act.wait_ge(S["y_ready"], T.next("y_ready", KD))
            with act.Fori(0, LAYERS) as l, T.loop(l, LAYERS, PER_LAYER["act"]):
                rms(split_first=True)
                ffn(ahead=True)
                rms()
                in_projections()
                sparse_attention()
                linear_attention()
                merge()
                rms()
                ffn(ahead=False)
            rms(halved=False)
            outT = area(0, 2, D)
            for t in range(2):
                for g in range(2):
                    b, v = T.take()
                    act.wait_ge(k.bank_done[b], v)
                    act.activation(outT[:, t, g * 512:g * 512 + 512], ps[:, b, :], ACT.Copy) \
                        .then_inc(S["out_ready"], 1)

        @block.vector
        def _(dve):
            T = Tally()

            def skip(n):
                for _ in range(n):
                    T.take()
                return T.last()

            def over(v, dims):
                return v.broadcast_to(dims)

            dve.memset(area(TABLE, HEADS)[BUCKETS:BUCKETS + 1, :], NEG).then_inc(S["neg_row"], 1)
            b, v = T.take()
            dve.wait_ge(k.bank_done[b], v)
            dve.tensor_copy(k.bias_row, ps[0:HEADS, b, :]).then_inc(k.bank_read[b], 1)
            b, v = T.take()
            dve.wait_ge(k.bank_done[b], v)
            dve.tensor_copy(k.cmp_bias, ps[:, b, 0:2 * NCMP * HEADS].rearrange(
           "p (q n h) -> p q h n", q=2, n=NCMP)) \
                .then_inc(k.bank_read[b], 1)
            b, v = T.take()
            dve.wait_ge(k.bank_done[b], v)
            for t, r in enumerate(VEC_ROWS):
                ins = dve.tensor_copy(k.vecT[:, t * P:t * P + r], ps[:, b, t * P:t * P + r])
            ins.then_inc(k.bank_read[b], 1)
            for kt in range(KD):
                b, v = T.take()
                dve.wait_ge(k.bank_done[b], v)
                dve.tensor_copy(k.xT[:, kt, :], ps[:, b, :]).then_inc(k.bank_read[b], 1)
            dve.wait_ge(*k.moved(T.last()))

            dve.wait_ge(S["silu_rounded"], T.next("silu_rounded"))
            dve.tensor_tensor(k.silu_split[1], k.silu_c, k.silu_split[0], ALU.subtract).then_inc(S["silu_split"], 1)

            def modulation(group):
                t, r, _ = VEC["b_ada"]
                four = slice(4 * group, 4 * group + 4)
                b, v = T.take()
                dve.wait_ge(k.bank_done[b], v)
                bias = k.vecT[:, t * P + r + four.start:t * P + r + four.stop]
                dve.tensor_tensor(k.mods[:, four, :], ps[:, b, 0:8].rearrange("p (m s) -> p m s", s=2),
                                  over(bias.unsqueeze(2), [P, 4, 2]), ALU.add).then_inc(k.bank_read[b], 1)

            def scales(rows):
                dve.wait_ge(*k.moved(T.last()))
                for sc in rows:
                    ins = dve.tensor_scalar(k.mods[:, sc:sc + KD, :], k.mods[:, sc:sc + KD, :], 1.0, None, ALU.add)
                ins.then_inc(S["dve_step"], 1)
                dve.wait_ge(S["dve_step"], T.next("dve_step"))

            def norm(dst, cols, affine, ready):
                n = cols.stop - cols.start
                mean, std = area(MEAN, TOK)[:, cols], area(STD, TOK)[:, cols]
                b, v = T.take()
                dve.wait_ge(k.bank_done[b], v)
                dve.tensor_scalar(mean, ps[:, b, 0:n], 1.0 / D, None, ALU.mult).then_inc(k.bank_read[b], 1)
                dve.wait_ge(*k.moved(T.last()))
                for kt in range(KD):
                    dve.tensor_tensor(dst[:, kt, cols], k.xT[:, kt, cols], mean, ALU.subtract).then_inc(S["centred"], 1)
                dve.wait_ge(*k.moved(skip(1)))
                dve.reciprocal(std, std).then_inc(S["dve_step"], 1)
                dve.wait_ge(S["dve_step"], T.next("dve_step"))
                for kt in range(KD + 2):
                    d = dst[:, kt % KD, cols]
                    if kt < KD:
                        dve.tensor_tensor(d, d, std, ALU.mult).then_inc(S["scaled" if affine is None else "dve_step"], 1)
                    if affine is None and kt >= 2:
                        dve.wait_ge(S["h_rounded"], T.next("h_rounded"))
                        dve.tensor_tensor(k.h[1][:, kt - 2, cols], dst[:, kt - 2, cols], k.h[0][:, kt - 2, cols],
                                          ALU.subtract).then_inc(S["h_ready"], 1)
                    if affine is not None and 1 <= kt <= KD:
                        dve.wait_ge(S["dve_step"], T.next("dve_step"))
                        gain, bias = affine(kt - 1)
                        o = dst[:, kt - 1, cols]
                        dve.tensor_scalar(o, o, gain, bias, ALU.mult, ALU.add).then_inc(S[ready], 1)
                if affine is not None:
                    dve.wait_ge(S[ready], T.next(ready, KD))

            def gained(name, l):
                return lambda kt: (k.vec(f"{name}_g", l * KD + kt), k.vec(f"{name}_b", l * KD + kt))

            def fourier(l):
                todo = 8 if l == 0 else 4
                for u in range(todo + 1):
                    if u < todo:
                        b, v = T.take()
                        dve.wait_ge(k.bank_done[b], v)
                        dve.tensor_copy(dft1[:, u % 2], ps[:, b, :].rearrange("p (t c) -> p t c", t=2)) \
                            .then_inc(k.bank_read[b], 1)
                    if u >= 1:
                        skip(1)

            def qk_norm(l, cols):
                every = slice(0, TOK)
                for x, std, name, col, tiles, cs in (
                        (ckv, STD_CKV, "mla_kv_g", 2 * l, 2, every), (kg.unsqueeze(1), SQ_KG, "gqa_k_g", l, 1, every),
                        (cq, SQ_CQ, "mla_q_g", 2 * l, 2, cols)):
                    dve.wait_ge(*k.moved(skip(1)))
                    r = sqk[:, std, cs]
                    dve.reciprocal(r, r).then_inc(S["dve_step"], 1)
                    dve.wait_ge(S["dve_step"], T.next("dve_step"))
                    for j in range(tiles):
                        ins = dve.scalar_tensor_tensor(x[:, j, cs], x[:, j, cs], k.vec(name, col + j), r,
                                                       ALU.mult, ALU.mult)
                    ins.then_inc(S["normed"], 1)
                for x, x_split, cs in ((ckv, ckv_split, every), (cq, cq_split, cols)):
                    dve.wait_ge(S["latent_rounded"], T.next("latent_rounded"))
                    dve.tensor_tensor(x_split[1][:, :, cs], x[:, :, cs], x_split[0][:, :, cs], ALU.subtract) \
                        .then_inc(S["latent_split"], 1)
                dve.wait_ge(*k.moved(skip(4)))
                r = sqk[:, SQ_QG:SQ_QG + 4, cols]
                dve.reciprocal(r, r).then_inc(S["dve_step"], 1)
                dve.wait_ge(S["dve_step"], T.next("dve_step"))
                x = qg[:, :, cols]
                ins = dve.scalar_tensor_tensor(x, x, k.vec("gqa_q_g", l), r, ALU.mult, ALU.mult)
                ins.then_inc(S["normed"], 1)
                dve.wait_ge(S["normed"], T.next("normed", 4))

            def rope():
                skip(4 + 4 + 4 + 2)
                todo = rotated
                for j, (name, x) in enumerate(todo):
                    b, v = T.take()
                    dve.wait_ge(k.bank_done[b], v)
                    sin, cos = k.col(name.replace("rot", "sin")), k.col(name.replace("rot", "cos"))
                    dve.tensor_tensor(area(ROT + j * SEQ, SEQ), ps[:, b, 0:SEQ], sin, ALU.mult) \
                        .then_inc(k.bank_read[b], 1)
                    ins = dve.tensor_tensor(x[:, CTX:TOK], x[:, CTX:TOK], cos, ALU.mult)
                ins.then_inc(S["dve_step"], 1)
                dve.wait_ge(S["dve_step"], T.next("dve_step"))
                for j, (name, x) in enumerate(todo):
                    ins = dve.tensor_tensor(x[:, CTX:TOK], x[:, CTX:TOK], area(ROT + j * SEQ, SEQ), ALU.add)
                ins.then_inc(S["roped"], 1)

            def attention(l):
                todo = units(l)
                score, out_of = {}, {}

                def moved(u):
                    kind, half, c, a = todo[u]
                    b, n = out_of[u // 2]
                    dve.wait_ge(k.bank_done[b], n)
                    o = om if kind == "m" else og
                    dve.tensor_copy(o[:, c, slice(*HALVES[half])], ps[:, b, 0:SEQ]).then_inc(k.bank_read[b], 1)

                for u in range(len(todo) + 2):
                    if u >= 4 and u % 2 == 0:
                        moved(u - 3)
                    if l == 0 and u < (ADA - ADA_FIRST) // 2:
                        skip(1)
                    if l == 0 and 1 <= u <= (ADA - ADA_FIRST) // 2:
                        modulation(ADA_FIRST // 2 + u - 1)
                        if u == (ADA - ADA_FIRST) // 2:
                            scales((SC2, MODS + SC1, MODS + SC2))
                    if u < len(todo):
                        score[u] = [T.take() for _ in range(2)]
                    if 1 <= u <= len(todo):
                        buf, n = (u - 1) % 2, HALVES[todo[u - 1][1]][1]
                        dve.wait_ge(*k.moved(score[u - 1][1]))
                        rsum = k.stat[:, 8 * buf + 2:8 * buf + 4]
                        dve.reciprocal(rsum, rsum).then_inc(S["dve_step"], 1)
                        dve.wait_ge(S["dve_step"], T.next("dve_step"))
                        for q in range(2):
                            p = prob[:, buf, q, 0:n]
                            ins = dve.tensor_scalar(p, p, rsum[:, q:q + 1], None, ALU.mult)
                        ins.then_inc(S["prob_ready"], 1)
                        skip(2)
                    if u < len(todo):
                        buf, n = u % 2, HALVES[todo[u][1]][1]
                        nmax = k.stat[:, 8 * buf:8 * buf + 2]
                        for q, (b, v) in enumerate(score[u]):
                            dve.wait_ge(k.bank_done[b], v)
                            ins = dve.tensor_reduce(nmax[:, q:q + 1], ps[:, b, 0:n], AX, ALU.max, negate=True)
                        ins.then_inc(S["dve_step"], 1)
                        dve.wait_ge(S["dve_step"], T.next("dve_step"))
                        scale = MLA_SCALE if todo[u][0] == "m" else GQA_SCALE
                        dve.tensor_scalar(nmax, nmax, scale, None, ALU.mult).then_inc(S["row_max"], 1)
                    if u >= 2 and todo[u - 2][3] == 0:
                        out_of[(u - 2) // 2] = T.take()
                moved(len(todo) - 1)

            def branches(cols):
                n = cols.stop - cols.start
                x = k.xT[:, :, cols]
                dve.tensor_scalar(x, x, ALPHA, None, ALU.mult)
                for part, x_split in zip(branch, branch_split):
                    dve.wait_ge(S["branch_rounded"], T.next("branch_rounded"))
                    dve.tensor_tensor(x_split[1][:, :, cols], part[:, :, cols], x_split[0][:, :, cols], ALU.subtract) \
                        .then_inc(S["branch_split"], 1)
                tm = area(TMP_M, TOK)[:, cols]
                for c in range(2):
                    for g in range(3):
                        skip(4)
                        for t in range(4):
                            m = mixed[:, 4 * c + t, cols]
                            b, v = T.take()
                            dve.wait_ge(k.bank_done[b], v)
                            dve.wait_ge(*k.moved(((b + 4) % BANKS, T.value(f"bank{(b + 4) % BANKS}"))))
                            dve.tensor_tensor(m if g == 0 else tm, gate(t)[:, cols], ps[:, b, 0:n], ALU.mult) \
                                .then_inc(k.bank_read[b], 1)
                            if g > 0:
                                dve.wait_ge(*k.moved(T.last()))
                                step = "dve_step" if g == 1 else "gated"
                                dve.tensor_tensor(m, m, tm, ALU.add).then_inc(S[step], 1)
                                dve.wait_ge(S[step], T.next(step))
                for j in range(4):
                    two = slice(2 * j, 2 * j + 2)
                    dve.wait_ge(S["mixed_rounded"], T.next("mixed_rounded"))
                    dve.tensor_tensor(mixed_split[1][:, two, cols], mixed[:, two, cols], mixed_split[0][:, two, cols],
                                      ALU.subtract).then_inc(S["mixed_split"], 1)

            def residual(tile, b, cols, halves, g):
                for s in halves:
                    c0, c1 = HALVES[s]
                    x = k.xT[:, tile, c0:c1]
                    ins = dve.scalar_tensor_tensor(x, ps[:, b, c0 - cols.start:c1 - cols.start],
                                                   k.mods[:, g + tile, s:s + 1], x, ALU.mult, ALU.add)
                return ins

            for group in range(ADA_FIRST // 2):
                skip(1)
                if group >= 1:
                    modulation(group - 1)
            modulation(group)
            scales((SC1,))
            for l in range(LAYERS):
                cols = slice(0 if l == 0 else CTX, TOK)
                n = cols.stop - cols.start
                halves = (0, 1) if l == 0 else (1,)
                mod = l * MODS
                norm(plain, slice(0, TOK), None, "h_ready")
                skip(4 + 1 + 2 + 4 + 4)
                fourier(l)
                qk_norm(l, cols)
                rope()
                attention(l)
                branches(cols)
                for m in range(KD):
                    b, v = T.take()
                    dve.wait_ge(k.bank_done[b], v)
                    residual(m, b, cols, halves, mod + G1).then_inc(k.bank_read[b], 1)
                dve.wait_ge(*k.moved(T.last()))
                norm(k.xT, cols, gained("ln1", l), "x_ready")
                norm(plain, cols, None, "h_ready")
                x = k.xT[:, :, cols]
                dve.tensor_scalar(x, x, ALPHA, None, ALU.mult).then_inc(S["dve_step"], 1)
                dve.wait_ge(S["dve_step"], T.next("dve_step"))
                hid, hid_lo, hid_hi = hidden(l)

                def squared(j, o):
                    b, v = T.take()
                    dve.wait_ge(S["relu_ready"], T.next("relu_ready"))
                    dve.tensor_tensor(o, relu(l, j), ps[:, b, 0:n], ALU.mult).then_inc(k.bank_read[b], 1)

                for j in range(8):
                    squared(j, hid[:, j, :])
                with dve.Fori(0, 3) as i, T.loop(i, 3, {"tiles": 8, "relu_ready": 8}):
                    for j in range(8):
                        squared(j, hid[:, bass.ds(i * 8 + (8 + j), 1), :].rearrange("p o n -> p (o n)"))
                for kt in range(4 * KD):
                    dve.wait_ge(S["hid_rounded"], T.next("hid_rounded"))
                    dve.tensor_tensor(hid_lo[:, kt, :], hid[:, kt, :], hid_hi[:, kt % HID_SLOTS, :], ALU.subtract) \
                        .then_inc(S["hid_split"], 1)
                for m in range(KD):
                    b, v = T.take()
                    dve.wait_ge(k.bank_done[b], v)
                    residual(m, b, cols, halves, mod + G2).then_inc(k.bank_read[b], 1)
                dve.wait_ge(*k.moved(T.last()))
                norm(k.xT, cols, gained("ln2", l), "x_ready" if l == 0 else "y_ready")

            dve.memset(chain, 1.0)
            dve.memset(k.p_cmp, 0.0)
            dve.memset(k.hid_v, 0.0).then_inc(S["dve_step"], 1)
            dve.wait_ge(S["dve_step"], T.next("dve_step"))
            dve.memset(chain.rearrange("p (n i) -> p n i", i=CHUNK)[:, :, 0:1], 0.0).then_inc(S["dve_step"], 1)
            dve.wait_ge(S["dve_step"], T.next("dve_step"))
            dve.wait_ge(S["bias_in"], 16)

            def rms(name, l):
                std = area(STD2, SEQ)
                dve.wait_ge(*k.moved(skip(1)))
                dve.reciprocal(std, std).then_inc(S["dve_step"], 1)
                dve.wait_ge(S["dve_step"], T.next("dve_step"))
                if l is None:
                    for kt in range(KD):
                        ins = dve.scalar_tensor_tensor(plain2[:, kt, :], y[:, kt, :], k.vec(name, kt), std, ALU.mult, ALU.mult)
                    ins.then_inc(S["final_ready"], 1)
                    return
                for kt in range(KD + 2):
                    if kt < KD:
                        dve.scalar_tensor_tensor(plain2[:, kt, :], y[:, kt, :], k.vec(name, l * KD + kt), std,
                                                 ALU.mult, ALU.mult).then_inc(S["h_plain"], 1)
                    if kt >= 2:
                        dve.wait_ge(S["h_rounded"], T.next("h_rounded"))
                        dve.tensor_tensor(k.h2[1][:, kt - 2, :], plain2[:, kt - 2, :], k.h2[0][:, kt - 2, :], ALU.subtract) \
                            .then_inc(S["h_ready"], 1)

            def parts(x, hi, lo):
                dve.tensor_scalar(hi, x, 1.0, None, ALU.mult).then_inc(S["dve_step"], 1)
                dve.wait_ge(S["dve_step"], T.next("dve_step"))
                return dve.tensor_tensor(lo, x, hi, ALU.subtract)

            def ffn():
                def pair(j, two):
                    up = [T.take() for _ in range(2)]
                    x = act2[:, two, :]
                    for m, (b, v) in enumerate(up):
                        dve.wait_ge(k.bank_done[b], v)
                        dve.wait_ge(*k.moved(skip(1)))
                        dve.tensor_tensor(x[:, m, :], area(SILU2, 2, 2, SEQ)[:, j % 2, m, :], ps[:, b, 0:SEQ], ALU.mult) \
                            .then_inc(k.bank_read[b], 1)
                    dve.wait_ge(*k.moved(up[1]))
                    parts(x, act2_split[0][:, two, :], act2_split[1][:, two, :]).then_inc(S["act2_split"], 1)

                pair(0, slice(0, 2))
                with dve.Fori(0, 5) as i, T.loop(i, 5, {"tiles": 8, "dve_step": 2}):
                    for j in range(2):
                        pair(j + 1, bass.ds(i * 4 + (2 + 2 * j), 2))
                for m in range(KD):
                    b, v = T.take()
                    dve.wait_ge(k.bank_done[b], v)
                    dve.scalar_tensor_tensor(y[:, m, :], ps[:, b, 0:SEQ], 0.5, y[:, m, :], ALU.mult, ALU.add) \
                        .then_inc(k.bank_read[b], 1)
                dve.wait_ge(*k.moved(T.last()))

            def in_projections(l):
                skip(4)
                for x, name in enumerate(("cmp_pos_k_2", "cmp_pos_v_2")):
                    t, r, _ = VEC[name]
                    for g in range(2):
                        b, v = T.take()
                        dve.wait_ge(k.bank_done[b], v)
                        for half in range(2):
                            at = slice(HD * half, HD * half + HD)
                            src = ps[at, b, 0:SEQ].rearrange("p (n j e) -> p e j n", j=JP // 2, e=2)
                            for s in range(2):
                                pos = k.vecT[at, bass.ds(l * JP + (t * P + r + s * JP // 2), JP // 2)]
                                ins = dve.tensor_tensor(
                                    k.kbuf[x][at, s * JP // 2:(s + 1) * JP // 2, g * NCMP:(g + 1) * NCMP], src[:, half, :, s:s + NCMP],
                                    over(pos.unsqueeze(2), [HD, JP // 2, NCMP]), ALU.add)
                        ins.then_inc(k.bank_read[b], 1)
                    dve.wait_ge(*k.moved(T.last()))
                    parts(k.kbuf[x], *k.kbuf_split[x]).then_inc(S["blocks_split"], 1)
                skip(6)
                for h in range(GH):
                    b, v = T.take()
                    dve.wait_ge(k.bank_done[b], v)
                    dve.tensor_scalar(z[:, h, :], ps[:, b, 0:SEQ], k.vec("gla_a_b_2", l * GH + h), None,
                                      ALU.add) \
                        .then_inc(k.bank_read[b], 1)
                dve.wait_ge(*k.moved(T.last()))
                dve.scalar_tensor_tensor(t1, z, -1.0, z, ALU.mult, ALU.min).then_inc(S["minus_abs_z"], 1)
                dve.wait_ge(S["log1p_ready"], T.next("log1p_ready"))
                dve.scalar_tensor_tensor(z, z, 0.0, t1, ALU.min, ALU.subtract).then_inc(S["dve_step"], 1)
                dve.wait_ge(S["dve_step"], T.next("dve_step"))
                flat = lambda v: v.rearrange("p h t -> p (h t)")
                dve.tensor_tensor_scan(flat(t1), chain, flat(z), 0.0, ALU.mult, ALU.add) \
                    .then_inc(S["decay_ready"], 1)
                dve.wait_ge(S["edecay"], T.next("edecay"))
                ends = z.rearrange("p h (n i) -> p h n i", n=NCH)[:, :, :, CHUNK - 1]
                dve.tensor_copy(dch, ends)
                dve.tensor_tensor(qb, qb, z, ALU.mult).then_inc(S["edecay_used"], 1)
                dve.wait_ge(S["edecay"], T.next("edecay"))
                dve.tensor_tensor(kin, kb, z, ALU.mult).then_inc(S["dve_step"], 1)
                dve.wait_ge(S["dve_step"], T.next("dve_step"))
                chunks = lambda v: flat(v).rearrange("p (n i) -> p n i", i=CHUNK)
                dve.tensor_tensor(chunks(z), over(chunks(t1)[:, :, CHUNK - 1:CHUNK], [P, GH * NCH, CHUNK]),
                                  chunks(t1), ALU.subtract).then_inc(S["decay_ready"], 1)
                dve.wait_ge(S["edecay"], T.next("edecay"))
                dve.tensor_tensor(kb, kb, z, ALU.mult).then_inc(S["gla_in"], 1)
                skip(4 + 4 + 4 + 4 + 8)

            def sparse_attention():
                pc = k.p_cmp[:, :, :, 0:NCMP]
                for a in range(2):
                    b, v = T.take()
                    dve.wait_ge(k.bank_done[b], v)
                    dve.tensor_tensor(pc[:, :, 4 * a:4 * a + 4, :],
                                      ps[:, b, 0:8 * NCMP].rearrange("p (q c n) -> p q c n", q=2, c=4),
                                      k.cmp_bias[:, :, 4 * a:4 * a + 4, :], ALU.add) \
                        .then_inc(k.bank_read[b], 1)
                dve.wait_ge(*k.moved(T.last()))
                st = k.stat[:, 32:48].rearrange("p (q h) -> p q h", q=2)
                wide = [P, 2, HEADS, NCMP]
                dve.tensor_reduce(st, pc, AX, ALU.max).then_inc(S["dve_step"], 1)
                dve.wait_ge(S["dve_step"], T.next("dve_step"))
                dve.tensor_tensor(pc, pc, over(st.unsqueeze(3), wide), ALU.subtract).then_inc(S["cmp_max"], 1)
                heads3 = ga.rearrange("p q (h b) -> p q h b", b=3)
                dve.wait_ge(S["cmp_exp"], T.next("cmp_exp"))
                dve.tensor_reduce(st, pc, AX, ALU.add).then_inc(S["dve_step"], 1)
                dve.wait_ge(S["dve_step"], T.next("dve_step"))
                dve.reciprocal(st, st).then_inc(S["dve_step"], 1)
                dve.wait_ge(S["dve_step"], T.next("dve_step"))
                dve.tensor_tensor(st, st, heads3[:, :, :, 0], ALU.mult).then_inc(S["dve_step"], 1)
                dve.wait_ge(S["dve_step"], T.next("dve_step"))
                dve.tensor_tensor(st, st, over(k.col("has_cmp").unsqueeze(2), [P, 2, HEADS]), ALU.mult) \
                    .then_inc(S["dve_step"], 1)
                dve.wait_ge(S["dve_step"], T.next("dve_step"))
                dve.tensor_tensor(pc, pc, over(st.unsqueeze(3), wide), ALU.mult).then_inc(S["cmp_prob"], 1)

                out_of = {}

                def moved(u):
                    b, n = out_of[u // 2]
                    dve.wait_ge(k.bank_done[b], n)
                    dve.tensor_copy(oa[:, u // 2, :], ps[:, b, 0:SEQ]).then_inc(k.bank_read[b], 1)

                for u in range(HEADS + 2):
                    if u >= 4 and u % 2 == 0:
                        moved(u - 3)
                    if u < HEADS:
                        scores = [T.take() for _ in range(2)]
                    if 1 <= u <= HEADS:
                        c, a = (u - 1) // 2, (u - 1) % 2
                        h, buf = c + 4 * a, (u - 1) % 2
                        dve.wait_ge(S["nsa_exp"], T.next("nsa_exp"))
                        sums = k.stat[:, 16 * buf + 4:16 * buf + 8]
                        dve.reciprocal(sums, sums).then_inc(S["dve_step"], 1)
                        dve.wait_ge(S["dve_step"], T.next("dve_step"))
                        two = sums.rearrange("p (q j) -> p q j", q=2)
                        dve.tensor_tensor(two, two, heads3[:, :, h, 1:3], ALU.mult).then_inc(S["dve_step"], 1)
                        dve.wait_ge(S["dve_step"], T.next("dve_step"))
                        for j in range(4):
                            n = P if j < 2 else 2 * P
                            o = j * P if j < 2 else 2 * P + (j - 2) * 2 * P
                            p = prob2[:, buf, o:o + n]
                            ins = dve.tensor_scalar(p, p, sums[:, j:j + 1], None, ALU.mult)
                        ins.then_inc(S["nsa_prob"], 1)
                        skip(2)
                    if u < HEADS:
                        c, a = u // 2, u % 2
                        h, buf = c + 4 * a, u % 2
                        nmax = k.stat[:, 16 * buf:16 * buf + 4]
                        parts = []
                        for q in range(2):
                            n = (q + 1) * P
                            b, v = scores[q]
                            dve.wait_ge(k.bank_done[b], v)
                            p = prob2[:, buf, q * 2 * P:q * 2 * P + 2 * n].rearrange("p (j t) -> p j t", j=2)
                            dve.tensor_tensor(p, ps[:, b, 0:2 * n].rearrange("p (j t) -> p j t", j=2),
                                              over(k.bias[:, h, 2 * P - n:2 * P].unsqueeze(1), [P, 2, n]),
                                              ALU.add) \
                                .then_inc(k.bank_read[b], 1)
                            parts.append(p)
                        dve.wait_ge(*k.moved(scores[1]))
                        for q in range(2):
                            ins = dve.tensor_reduce(nmax[:, 2 * q:2 * q + 2], parts[q], AX, ALU.max, negate=True)
                        ins.then_inc(S["nsa_max"], 1)
                    if u == 2:
                        skip(1)
                    if u >= 2 and u % 2 == 0:
                        out_of[(u - 2) // 2] = T.take()
                moved(HEADS - 1)

            def linear_attention(l):
                skip(2)
                for t in range(2):
                    b, v = T.take()
                    dve.wait_ge(k.bank_done[b], v)
                    dve.tensor_tensor(att[:, t], ps[:, b, :].rearrange("p (h c) -> p h c", h=GH),
                                      over(k.col("causal").unsqueeze(1), [P, GH, P]), ALU.mult) \
                        .then_inc(k.bank_read[b], 1)
                for n in range(NCH - 1):
                    for hp in range(2):
                        b, v = T.take()
                        dve.wait_ge(k.bank_done[b], v)
                        two = state[:, n, 2 * hp:2 * hp + 2, :]
                        kv = ps[:, b, :].rearrange("p (h c) -> p h c", h=2)
                        if n == 0:
                            ins = dve.tensor_copy(two, kv)
                        else:
                            for j in range(2):
                                h = 2 * hp + j
                                ins = dve.scalar_tensor_tensor(two[:, j, :], state[:, n - 1, h, :], dch[:, h, n:n + 1],
                                                               kv[:, j, :], ALU.mult, ALU.add)
                        ins.then_inc(k.bank_read[b], 1)
                    dve.wait_ge(*k.moved(T.last()))
                skip(KD)
                dve.wait_ge(*k.moved(skip(2)))
                dve.reciprocal(t1, t1).then_inc(S["dve_step"], 1)
                dve.wait_ge(S["dve_step"], T.next("dve_step"))
                heads = ob.rearrange("p (h v) t -> p h v t", v=2)
                dve.tensor_tensor(heads, heads, over(t1.unsqueeze(2), [P, GH, 2, SEQ]), ALU.mult) \
                    .then_inc(S["dve_step"], 1)
                dve.wait_ge(S["dve_step"], T.next("dve_step"))
                for j in range(KD):
                    ins = dve.scalar_tensor_tensor(ob[:, j, :], ob[:, j, :], k.vec("gla_out_norm_2", l * KD + j),
                                                   rb[:, j, :], ALU.mult, ALU.mult)
                ins.then_inc(S["dve_step"], 1)
                dve.wait_ge(S["dve_step"], T.next("dve_step"))

            def merge():
                for x, x_split in ((oa, oa_split), (ob, ob_split)):
                    ins = parts(x, *x_split)
                ins.then_inc(S["merge_in"], 1)
                for c in range(2):
                    gates = area(MGATE, 2, 4, SEQ)
                    dve.wait_ge(*k.moved(skip(8)))
                    for t in range(4):
                        b, v = T.take()
                        dve.wait_ge(k.bank_done[b], v)
                        dve.tensor_tensor(mixed2[:, 4 * c + t, :], gates[:, 0, t, :], ps[:, b, 0:SEQ], ALU.mult) \
                            .then_inc(k.bank_read[b], 1)
                    for j in range(2):
                        two = slice(4 * c + 2 * j, 4 * c + 2 * j + 2)
                        m, tmp = mixed2[:, two, :], area(TMP2, 2, SEQ)
                        for t in range(2):
                            b, v = T.take()
                            dve.wait_ge(k.bank_done[b], v)
                            dve.tensor_tensor(tmp[:, t, :], gates[:, 1, 2 * j + t, :], ps[:, b, 0:SEQ], ALU.mult) \
                                .then_inc(k.bank_read[b], 1)
                        dve.wait_ge(*k.moved(T.last()))
                        dve.tensor_tensor(m, m, tmp, ALU.add).then_inc(S["dve_step"], 1)
                        dve.wait_ge(S["dve_step"], T.next("dve_step"))
                        parts(m, mixed2_split[0][:, two, :], mixed2_split[1][:, two, :]).then_inc(S["merged"], 1)
                for j in range(KD):
                    b, v = T.take()
                    dve.wait_ge(k.bank_done[b], v)
                    dve.tensor_tensor(y[:, j, :], y[:, j, :], ps[:, b, 0:SEQ], ALU.add).then_inc(k.bank_read[b], 1)
                dve.wait_ge(*k.moved(T.last()))

            with dve.Fori(0, LAYERS) as l, T.loop(l, LAYERS, PER_LAYER["dve"]):
                rms("ffn1_norm_2", l)
                ffn()
                rms("mix_norm_2", l)
                in_projections(l)
                sparse_attention()
                linear_attention(l)
                merge()
                rms("ffn2_norm_2", l)
                ffn()
            rms("final_norm_2", None)


_INS = ["x", "c", "ctx", "c_ctx", "w_ada", "b_ada", "w_in", "b_gate", "mla_q_g", "mla_kv_g", "w_uq", "w_uk", "w_uv",
        "gqa_q_g", "gqa_k_g", "w_fo", "w_mo", "w_go", "w_o", "ln1_g", "ln1_b", "w1", "w2", "ln2_g", "ln2_b",
        "rel_table_2", "ffn1_norm_2", "ffn1_w_gate_2", "ffn1_w_up_2", "ffn1_w_down_2", "mix_norm_2", "w_in_2",
        "cmp_pos_k_2", "cmp_pos_v_2", "cmp_k_w1_2", "cmp_k_w2_2", "cmp_v_w1_2", "cmp_v_w2_2", "gla_a_w2_2",
        "gla_a_b_2", "gla_out_norm_2", "w_branch_nsa_2", "w_branch_gla_2", "w_out_2", "ffn2_norm_2",
        "ffn2_w_gate_2", "ffn2_w_up_2", "ffn2_w_down_2", "final_norm_2"]


def kernel(**inputs):
    import numpy as np
    import concourse.bacc as bacc
    from concourse.bass_utils import run_bass_kernel_spmd

    nc = bacc.Bacc("TRN2", target_bir_lowering=False, num_devices=1)
    arrays = {name: np.ascontiguousarray(inputs[name]) for name in _INS}
    arrays.update(shape_constants())
    feed, W = {}, {}
    for name, a in arrays.items():
        feed[f"in_{name}"] = a
        W[name] = nc.dram_tensor(f"in_{name}", a.shape, mybir.dt.from_np(a.dtype), kind="ExternalInput").ap()
    out = nc.dram_tensor("out", (1, SEQ, D), F32, kind="ExternalOutput").ap()
    scratch = nc.dram_tensor("bias_by_distance", (HEADS, 512), F32, kind="Internal").ap()
    copies = nc.dram_tensor("bias_copies", (P, HEADS, 512), F32, kind="Internal").ap()
    build(nc, W, out, scratch, copies)
    r = run_bass_kernel_spmd(nc, [feed], core_ids=[0])
    return r.results[0]["out"]
```
